# Optimizing a Trainium2 kernel written in Bass

```python
import jax, jax.numpy as jnp
from jax import lax
import numpy as np

D_MODEL = 1024
BATCH = 1
SEQ = 1024
DEPTH = 2

GRID_W = 64
CTX_LEN = 256
N_HEADS = 8
N_KV_HEADS = 2
HEAD_DIM = 64
GROUP = N_HEADS // N_KV_HEADS
ATTN_W = N_HEADS * HEAD_DIM
KV_W = N_KV_HEADS * HEAD_DIM
SHORT_W = 512
SHORT_K = 3
CONF_W = 512
CONF_K = 31
N_BRANCH = 3
Q_BLOCK = 128
ROPE_THETA = 10000.0
RMS_EPS = 1e-6
LN_EPS = 1e-5
SPLIT_SIZES = (ATTN_W, KV_W, KV_W, ATTN_W,
               SHORT_W, SHORT_W, SHORT_W, SHORT_W,
               CONF_W, CONF_W, CONF_W,
               N_BRANCH * D_MODEL)
D_IN = sum(SPLIT_SIZES)
K_LO = ATTN_W
V_HI = ATTN_W + 2 * KV_W

kernel_name = "hybrid_gqa_shortconv_conformer_dit_block"

def _split_proj(p):
    idx = [int(i) for i in np.cumsum(SPLIT_SIZES)[:-1]]
    return jnp.split(p, idx, axis=-1)

def _layer_norm(x, g, b):
    xf = x.astype(jnp.float32)
    mu = jnp.mean(xf, axis=-1, keepdims=True)
    var = jnp.mean(jnp.square(xf - mu), axis=-1, keepdims=True)
    return ((xf - mu) * lax.rsqrt(var + LN_EPS)).astype(x.dtype) * g + b

def _rms_norm(x, g):
    xf = x.astype(jnp.float32)
    return (xf * lax.rsqrt(jnp.mean(jnp.square(xf), axis=-1, keepdims=True) + RMS_EPS)).astype(x.dtype) * g

def _depthwise_conv(x, w):
    k, ch = w.shape
    return lax.conv_general_dilated(x, w[:, None, :], window_strides=(1,), padding=[(k // 2, k // 2)],
                                    dimension_numbers=('NWC', 'WIO', 'NWC'), feature_group_count=ch)

def _axial_rope_tables(n_tokens):
    n_rows = n_tokens // GRID_W
    rows = jnp.repeat(jnp.arange(n_rows, dtype=jnp.float32), GRID_W)
    cols = jnp.tile(jnp.arange(GRID_W, dtype=jnp.float32), n_rows)
    quarter = HEAD_DIM // 4
    freqs = ROPE_THETA ** (-jnp.arange(quarter, dtype=jnp.float32) / quarter)
    ang_r = rows[:, None] * freqs
    ang_c = cols[:, None] * freqs
    return (jnp.cos(ang_r)[:, None, :], jnp.sin(ang_r)[:, None, :],
            jnp.cos(ang_c)[:, None, :], jnp.sin(ang_c)[:, None, :])

def _rot_half(xh, cos, sin):
    q = xh.shape[-1] // 2
    x1, x2 = xh[..., :q], xh[..., q:]
    return jnp.concatenate([x1 * cos - x2 * sin, x2 * cos + x1 * sin], axis=-1)

def _apply_axial_rope(x, tabs):
    cr, sr, cc, sc = tabs
    xf = x.astype(jnp.float32)
    half = HEAD_DIM // 2
    out = jnp.concatenate([_rot_half(xf[..., :half], cr, sr), _rot_half(xf[..., half:], cc, sc)], axis=-1)
    return out.astype(x.dtype)

def _attend(q, k, v):
    s = jnp.einsum('bqkgd,bskd->bkgqs', q, k).astype(jnp.float32) * (HEAD_DIM ** -0.5)
    p = jax.nn.softmax(s, axis=-1).astype(v.dtype)
    return jnp.einsum('bkgqs,bskd->bqkgd', p, v)

def _blocked_attention(q, k, v):
    b, s = q.shape[0], q.shape[1]
    nb = s // Q_BLOCK
    qb = jnp.moveaxis(q.reshape(b, nb, Q_BLOCK, N_KV_HEADS, GROUP, HEAD_DIM), 1, 0)
    o = lax.map(lambda blk: _attend(blk, k, v), qb)
    return jnp.moveaxis(o, 0, 1).reshape(b, s, ATTN_W)

def _heads(t, n):
    return t.reshape(t.shape[0], t.shape[1], n, HEAD_DIM)

def _merge_branches(o_attn, parts, w_pa, w_sc, w_ps, w_cdw, b_cdw, cln_g, cln_b, w_pc, b_pc, w_o):
    _, _, _, z_a, s_b, s_c, s_h, z_s, c_a, c_g, z_c, g_m = parts
    br_a = (o_attn * jax.nn.silu(z_a)) @ w_pa
    br_b = (s_b * _depthwise_conv(s_c * s_h, w_sc) * jax.nn.silu(z_s)) @ w_ps
    hc = c_a * jax.nn.sigmoid(c_g)
    hc = _depthwise_conv(hc, w_cdw) + b_cdw
    hc = jax.nn.silu(_layer_norm(hc, cln_g, cln_b))
    br_c = (hc * jax.nn.silu(z_c)) @ w_pc + b_pc
    g_a, g_b, g_c = jnp.split(g_m, N_BRANCH, axis=-1)
    merged = jax.nn.sigmoid(g_a) * br_a + jax.nn.sigmoid(g_b) * br_b + jax.nn.sigmoid(g_c) * br_c
    return merged @ w_o

def setup_inputs(seed: int = 0) -> dict:
    key = jax.random.key(seed)
    ks = jax.random.split(key, 24)
    f32 = jnp.float32
    beta = (8.0 * DEPTH) ** -0.25

    def nrm(k, shape, scale):
        return jax.random.normal(k, shape, f32) * scale

    return {
        "x": nrm(ks[0], (BATCH, SEQ, D_MODEL), 1.0),
        "c": nrm(ks[1], (BATCH, D_MODEL), 1.0),
        "ctx": nrm(ks[2], (BATCH, CTX_LEN, D_MODEL), 1.0),
        "c_ctx": nrm(ks[3], (D_MODEL,), 1.0),
        "w_mod": nrm(ks[4], (DEPTH, D_MODEL, 3 * D_MODEL), D_MODEL ** -0.5),
        "b_mod": nrm(ks[5], (DEPTH, 3 * D_MODEL), 0.02),
        "w_in": nrm(ks[6], (DEPTH, D_MODEL, D_IN), D_MODEL ** -0.5),
        "q_gain": 1.0 + nrm(ks[7], (DEPTH, HEAD_DIM), 0.02),
        "k_gain": 1.0 + nrm(ks[8], (DEPTH, HEAD_DIM), 0.02),
        "w_proj_attn": nrm(ks[9], (DEPTH, ATTN_W, D_MODEL), beta * ATTN_W ** -0.5),
        "w_short_conv": nrm(ks[10], (DEPTH, SHORT_K, SHORT_W), SHORT_K ** -0.5),
        "w_proj_short": nrm(ks[11], (DEPTH, SHORT_W, D_MODEL), beta * SHORT_W ** -0.5),
        "w_conf_dw": nrm(ks[12], (DEPTH, CONF_K, CONF_W), CONF_K ** -0.5),
        "b_conf_dw": nrm(ks[13], (DEPTH, CONF_W), 0.02),
        "conf_ln_g": 1.0 + nrm(ks[14], (DEPTH, CONF_W), 0.02),
        "conf_ln_b": nrm(ks[15], (DEPTH, CONF_W), 0.02),
        "w_proj_conf": nrm(ks[16], (DEPTH, CONF_W, D_MODEL), beta * CONF_W ** -0.5),
        "b_proj_conf": nrm(ks[17], (DEPTH, D_MODEL), 0.02),
        "w_out": nrm(ks[18], (DEPTH, D_MODEL, D_MODEL), beta * D_MODEL ** -0.5),
        "post_ln_g": 1.0 + nrm(ks[19], (DEPTH, D_MODEL), 0.02),
        "post_ln_b": nrm(ks[20], (DEPTH, D_MODEL), 0.02),
    }

def reference(x, c, ctx, c_ctx, w_mod, b_mod, w_in, q_gain, k_gain, w_proj_attn, w_short_conv,
              w_proj_short, w_conf_dw, b_conf_dw, conf_ln_g, conf_ln_b, w_proj_conf, b_proj_conf,
              w_out, post_ln_g, post_ln_b):
    alpha = (2.0 * DEPTH) ** 0.25
    b, s = x.shape[0], x.shape[1]
    lc = ctx.shape[1]
    tabs = _axial_rope_tables(s)
    h_lat, h_ctx = x, ctx
    for l in range(DEPTH):
        last = l == DEPTH - 1
        branch_w = (w_proj_attn[l], w_short_conv[l], w_proj_short[l], w_conf_dw[l], b_conf_dw[l],
                    conf_ln_g[l], conf_ln_b[l], w_proj_conf[l], b_proj_conf[l], w_out[l])
        shift, scale, gate = jnp.split(jax.nn.silu(c) @ w_mod[l] + b_mod[l], 3, axis=-1)
        shift_c, scale_c, gate_c = jnp.split(jax.nn.silu(c_ctx) @ w_mod[l] + b_mod[l], 3, axis=-1)
        u_lat = h_lat * (1.0 + scale[:, None, :]) + shift[:, None, :]
        u_ctx = h_ctx * (1.0 + scale_c) + shift_c

        if last:
            k_c, v_c = jnp.split(u_ctx @ w_in[l][:, K_LO:V_HI], 2, axis=-1)
        else:
            p_ctx = _split_proj(u_ctx @ w_in[l])
            k_c, v_c = p_ctx[1], p_ctx[2]
        k_c = _rms_norm(_heads(k_c, N_KV_HEADS), k_gain[l])
        v_c = _heads(v_c, N_KV_HEADS)

        p_lat = _split_proj(u_lat @ w_in[l])
        q_l = _apply_axial_rope(_rms_norm(_heads(p_lat[0], N_HEADS), q_gain[l]), tabs)
        q_l = q_l.reshape(b, s, N_KV_HEADS, GROUP, HEAD_DIM)
        k_l = _apply_axial_rope(_rms_norm(_heads(p_lat[1], N_KV_HEADS), k_gain[l]), tabs)
        v_l = _heads(p_lat[2], N_KV_HEADS)
        k_all = jnp.concatenate([k_c, k_l], axis=1)
        v_all = jnp.concatenate([v_c, v_l], axis=1)
        o_lat = _blocked_attention(q_l, k_all, v_all)
        out_lat = _merge_branches(o_lat, p_lat, *branch_w)

        if not last:
            q_c = _rms_norm(_heads(p_ctx[0], N_HEADS), q_gain[l]).reshape(b, lc, N_KV_HEADS, GROUP, HEAD_DIM)
            o_ctx = _attend(q_c, k_c, v_c).reshape(b, lc, ATTN_W)
            out_ctx = _merge_branches(o_ctx, p_ctx, *branch_w)
            h_ctx = _layer_norm(alpha * h_ctx + gate_c * out_ctx, post_ln_g[l], post_ln_b[l])

        h_lat = _layer_norm(alpha * h_lat + gate[:, None, :] * out_lat, post_ln_g[l], post_ln_b[l])
    return h_lat


_drawn_inputs = setup_inputs


def setup_inputs(seed=0):
    import zlib

    import numpy as np

    out = dict(_drawn_inputs(seed))
    spreads = {}
    factors = {'ctx': 8.0,
     'c_ctx': 6.027,
     'b_mod': 6.147,
     'q_gain': 8.0,
     'k_gain': 8.0,
     'b_conf_dw': 8.0,
     'conf_ln_g': 58.661,
     'conf_ln_b': 53.441,
     'b_proj_conf': 35.364}
    for name, (base, spread) in spreads.items():
        noise = np.random.default_rng([zlib.crc32(name.encode()), seed]).standard_normal(out[name].shape)
        drawn = base * np.exp(spread * noise) if base else spread * noise
        out[name] = __import__('jax').numpy.asarray(drawn.astype(out[name].dtype))
    for name, factor in factors.items():
        out[name] = (out[name] * factor).astype(out[name].dtype)
    return out
```

```python
from contextlib import ExitStack, contextmanager

import numpy as np
import concourse.bass as bass
from concourse import mybir

F32 = mybir.dt.float32
F32R = mybir.dt.float32r
ACT = mybir.ActivationFunctionType
ALU = mybir.AluOpType
AX_X = mybir.AxisListType.X

P = 128
D = 1024
KD = D // P
LAT, CTX = 1024, 256
TALL = LAT + CTX
NTOK = TALL // P
DEPTH = 2
GRID_W = 64
HD = 64
NKV = 2
W3 = 512
KW = W3 // P
SHORT_K, CONF_K = 3, 31
SPAD, CPAD = SHORT_K // 2, CONF_K // 2
ALPHA = (2.0 * DEPTH) ** 0.25
LN_EPS, RMS_EPS = 1e-5, 1e-6
HCW = CPAD + LAT + CPAD + CTX + CPAD + 1
EW = 1296

_Q, _K, _V, _ZA = range(0, 4), [4], [5], range(6, 10)
_SB, _SC, _SH, _ZS = range(10, 14), range(14, 18), range(18, 22), range(22, 26)
_CA, _CG, _ZC = range(26, 30), range(30, 34), range(34, 38)
_GA, _GB, _GC = range(38, 46), range(46, 54), range(54, 62)
W_ORDER = [*_K, *_V, *_Q, *_ZA]
for _i in range(KW):
    W_ORDER += [_CG[_i], _CA[_i]]
W_ORDER += [*_GA]
for _i in range(KW):
    W_ORDER += [_SC[_i], _SH[_i], _ZS[_i], _SB[_i]]
W_ORDER += [*_GB, *_ZC, *_GC]
N_WIN = len(W_ORDER)
N_W8 = N_WIN + KD
W8_QKV, W8_ZA, W8_CONF, W8_GA, W8_SHORT, W8_GB, W8_ZC, W8_GC, W8_OUT = 0, 6, 10, 18, 26, 42, 50, 54, 62
J_QKV, J_ZA, J_CONF, J_MA, J_SHORT, J_MB, J_ZC, J_MC, J_OUT, NJ = 0, 6, 10, 18, 34, 50, 66, 70, 86, 94

V_PG, V_PB, V_BPC, V_CG, V_CB, V_BDW = 0, 8, 16, 24, 28, 32
V_WS = 36
V_WC = V_WS + KW * SHORT_K
NV = V_WC + KW * CONF_K

O_K, O_V, O_Q0, O_KT0, O_Q1, O_KT1, O_Q2, O_Q3 = range(8)
O_OT, O_CMEAN, O_CVAR, O_OMEAN, O_OVAR, N_OPS = 8, 12, 13, 14, 15, 16
SLOT = (0, 1536)
TB = (3072, 3584)
PT0 = (2560, 3072)
O0 = 3584


def chunks(n):
    return [(c, min(512, n - c)) for c in range(0, n, 512)]


def op_width(l, op):
    return TALL if l == 0 or op in (O_K, O_V, O_KT0, O_KT1) else LAT


def pieces(l, op):
    n = sum(len(chunks(op_width(a, b))) for a in range(DEPTH) for b in range(N_OPS) if (a, b) < (l, op))
    return [(n + i, c, m) for i, (c, m) in enumerate(chunks(op_width(l, op)))]


def segs(T):
    return [(0, LAT, 0)] + ([(LAT, CTX, 1)] if T > LAT else [])


def heads_at(nk, kt):
    if nk == 2:
        return [2 * kt, 2 * kt + 1]
    return [(kt - 1) // 2] if kt % 2 == 1 and kt < 8 else []


def score_parts(h, nk):
    if nk * P <= 256:
        return [], [(0, nk * P)]
    if h % 2 == 0:
        return [(0, 512), (512, 512)], [(1024, 256)]
    return [(256, 512), (768, 512)], [(0, 256)]


class Steps:

    def __init__(self, eng, sem):
        self.eng, self.sem, self.base, self.i, self.per, self.lo = eng, sem, 0, None, 0, 0

    def done(self, ins):
        ins.then_inc(self.sem, 1)
        self.base += 1
        n = self.base if self.i is None else (self.i - self.lo) * self.per + self.base
        self.eng.wait_ge(self.sem, n)

    @contextmanager
    def loop(self, lo, hi, per):
        start = self.base
        with self.eng.Fori(lo, hi) as i:
            self.i, self.per, self.lo = i, per, lo
            yield i
        assert self.base - start == per, (self.base - start, per)
        self.i = None
        self.base = start + per * (hi - lo)


def build(nc, hT_in, cvec, wmod, bmod, w8, w4, vecs, gains, rope, ident_in, stack_in, outT):
    with ExitStack() as ctx:
        def sem(name):
            return ctx.enter_context(nc.semaphore(name))

        base = [(nc.sbuf_base + 31) // 32 * 32]

        def region(nbytes):
            at = base[0]
            base[0] = at + (nbytes + 31) // 32 * 32
            return at

        def at(name, shape, dt, offset):
            return nc.alloc_sbuf_tensor_at(name, shape, dt, offset=offset)

        rU = region(2 * KD * TALL * 4)
        rY = region(2 * KW * TALL * 4)
        rX = region(41984)
        rE = region(6 * EW * 4)
        rW = region(6 * D * 4)
        rC = region(0)
        Uh = at("Uh", [P, KD, TALL], F32R, rU)
        Ul = at("Ul", [P, KD, TALL], F32R, rU + KD * TALL * 4)
        Yh = at("Yh", [P, KW, TALL], F32R, rY)
        Yl = at("Yl", [P, KW, TALL], F32R, rY + KW * TALL * 4)
        Pr = at("Pr", [P, 2, 4, TALL], F32, rY)
        Z = at("Z", [P, KD, TALL], F32, rY)
        B5 = TALL * 4
        raw = [at(f"raw{i}", [P, TALL], F32, rY + (6 + i) * B5) for i in range(2)]
        fc = [at(f"fc{i}", [P, TALL], F32, rY + i * B5) for i in range(2)]
        sq = at("sq", [P, TALL], F32, rY + 2 * B5)
        qn = at("qn", [P, TALL], F32, rY + 3 * B5)
        qa = at("qa", [P, TALL], F32, rY + 4 * B5)
        qb = at("qb", [P, TALL], F32, rY + 5 * B5)
        modrow = at("modrow", [2, 3 * D], F32, rY)
        bmod_sb = at("bmod_sb", [2, DEPTH, 3 * D], F32, rY + 12288)
        qo = at("qo", [P, NTOK, W3], F32, rX)
        cosT = at("cosT", [P, TALL], F32, rX)
        sinT = at("sinT", [P, TALL], F32, rX + B5)
        kT = at("kT", [P, NKV, TALL], F32R, rX + 20480)
        Vt = at("Vt", [P, NTOK, NKV, P], F32R, rX + 30720)
        hc = at("hc", [P, KW, HCW], F32, rX)
        cv = at("cv", [P, KW, TALL], F32, rX + 21248)
        X = at("X", [P, KD, TALL], F32, rX)
        wm = [at(f"wm{i}", [P, 3 * D], F32, rX + i * 12288) for i in range(3)]
        e = [at(f"e{i}", [P, EW], F32, rE + i * EW * 4) for i in range(6)]
        kd = at("kd", [P, NTOK, NKV, 2, HD], F32, rE + 2 * EW * 4)
        qTh = [at(f"qTh{i}", [P, 512], F32R, rE + i * 2048) for i in range(2)]
        qTl = [at(f"qTl{i}", [P, 512], F32R, rE + 4096 + i * 2048) for i in range(2)]
        qd = [at(f"qd{i}", [P, 4, 2, HD], F32, rE + 8192 + i * 2048) for i in range(2)]
        ob = at("ob", [P, 512], F32, rE + 12288)
        PTh = [at(f"PTh{i}", [P, 512], F32R, rE + 14336 + i * 2048) for i in range(2)]
        PTl = [at(f"PTl{i}", [P, 512], F32R, rE + 18432 + i * 2048) for i in range(2)]
        wraw = [at(f"wraw{i}", [P, D], F32, rW + i * 4096) for i in range(2)]
        wh = [at(f"wh{i}", [P, D], F32R, rW + 8192 + i * 4096) for i in range(2)]
        wl = [at(f"wl{i}", [P, D], F32R, rW + 16384 + i * 4096) for i in range(2)]
        cpos = [rC]

        def small(name, shape):
            n = 4
            for s in shape[1:]:
                n *= s
            o = cpos[0]
            cpos[0] = o + (n + 31) // 32 * 32
            return at(name, shape, F32, o)

        ident = small("ident", [P, P])
        stackI = small("stackI", [P, HD])
        ones = small("ones", [P, P])
        vec = small("vec", [P, DEPTH, NV])
        gain = small("gain", [P, 4, P])
        craw = small("craw", [P, KD, 2])
        csilu = small("csilu", [P, KD, 2])
        mod = small("mod", [P, DEPTH, 3 * KD, 2])
        ss = small("ss", [P, 2 * NTOK])
        ms = small("ms", [P, 2 * NTOK])
        rstd = small("rstd", [P, 2 * NTOK])
        mhalf = small("mhalf", [P, 2 * NTOK])
        mx = small("mx", [P, 8])
        nm = small("nm", [P, 8])
        eps = small("eps", [P, 1])
        rs = small("rs", [P, 2, 2, 4])
        rsum = small("rsum", [P, 4])
        ri = small("ri", [P, 4])
        assert cpos[0] <= nc.sbuf_usable_end, (cpos[0], nc.sbuf_usable_end)

        PS = ctx.enter_context(nc.psum_tensor("PS", [P, 4096], F32))
        hT1 = nc.dram_tensor("hT1", [KD, P, TALL], F32, kind="Internal").ap()
        accd = nc.dram_tensor("accd", [2, KD, P, TALL], F32, kind="Internal").ap()

        def tbank(f, n):
            return PS[:, TB[f % 2]:TB[f % 2] + n]

        def slot(par, T):
            return PS[:, SLOT[par]:SLOT[par] + T]

        s_c = sem("s_consts")
        s_bm = sem("s_bmod")
        s_wm = [sem(f"s_wmod{i}") for i in range(3)]
        s_wmu = sem("s_wmod_used")
        s_csilu = sem("s_csilu")
        s_modrow = sem("s_mod_row")
        s_modtr = sem("s_mod_transposed")
        s_mod = sem("s_mod_ready")
        s_ones = sem("s_ones")
        wland = [sem(f"w_landed{i}") for i in range(2)]
        whi = [sem(f"w_hi{i}") for i in range(2)]
        wsplit = [sem(f"w_split{i}") for i in range(2)]
        mm = [sem(f"mm_done{i}") for i in range(2)]
        sfree = [sem(f"slot_free{i}") for i in range(2)]
        t_done = sem("piece_done")
        t_free = sem("piece_read")
        s_rawfree = sem("raw_free")
        s_oraw = sem("o_transposed")
        s_mean = sem("ln_mean")
        s_tail = sem("exp_tail_done")
        s_hin = [sem(f"h_landed{i}") for i in range(2)]
        s_hused = sem("h_used")
        s_ufp = sem("u_written")
        s_u = sem("u_ready")
        s_rope = sem("s_rope")
        s_gain = sem("s_gain")
        s_tab = sem("rope_tables")
        s_fc = sem("feature_copy")
        s_sq = sem("squares")
        s_ms = sem("mean_square")
        s_rstd = sem("rstd")
        s_kd = sem("k_duplicated")
        s_vhi = sem("v_hi")
        s_khi = sem("k_hi")
        s_kv = sem("kv_ready")
        s_q = sem("q_ready")
        s_qd = sem("q_duplicated")
        pt_done = [sem(f"pt_done{i}") for i in range(2)]
        pt_hi = [sem(f"pt_hi{i}") for i in range(2)]
        pt_free = [sem(f"pt_free{i}") for i in range(2)]
        s_s = sem("scores")
        s_nm = sem("neg_max")
        s_exp = sem("exp_done")
        s_pv = sem("pv_done")
        s_o = sem("o_copied")
        s_oatt = sem("o_written")
        s_gate = sem("gate_written")
        s_yf = sem("y_float")
        s_yh = sem("y_hi")
        s_y = sem("y_ready")
        s_pad = sem("pads_zeroed")
        s_acc = sem("acc_ready")
        s_accin = sem("acc_landed")
        s_accst = sem("acc_stored")
        s_mgh = sem("merged_hi")
        s_mg = sem("merged_split")
        s_mgf = sem("merged_float")
        s_carry = sem("wait_carrier")
        s_mgd = sem("merge_done")
        s_lacc = sem("ln_square_added")
        s_csum = sem("ln_sum")
        s_dev = sem("ln_deviation")
        s_lsq = sem("ln_square")
        s_std = sem("ln_std")
        s_norm = sem("ln_normalised")
        s_hact = sem("conf_activated")
        s_scaled = sem("out_scaled")
        s_z = sem("z_ready")
        s_hn = sem("h_normalised")
        s_hst = sem("h_stored")
        s_outst = [sem(f"out_stored{i}") for i in range(2)]
        c_pe, c_act, c_dve, c_pool = sem("c_pe"), sem("c_act"), sem("c_dve"), sem("c_pool")

        TL = [TALL] + [LAT] * (DEPTH - 1)

        def jobs_qkv(l):
            return [TALL, TALL] + [TL[l]] * 4

        def att_calls(l):
            out = [(0, LAT // P, 0, NTOK)]
            if TL[l] > LAT:
                out.append((LAT // P, CTX // P, LAT // P, CTX // P))
            return out

        def att_base(l, call):
            units, pt, ks = 0, [0, 0], 0
            for ll in range(DEPTH):
                for n, (t0, nt, k0, nk) in enumerate(att_calls(ll)):
                    if (ll, n) == (l, call):
                        return units, pt, ks
                    U = 2 * nt
                    pt = [pt[0] + 1 + (nk // 2 + 1) * U - 2, pt[1] + 1 + (nk // 2 + 1) * U]
                    units += U
                    ks += nk * U
            return units, pt, ks

        block = ctx.enter_context(nc.Block())

        @block.sync
        def _(sp):
            sp.dma_start(craw[:], cvec).then_inc(s_c, 16)
            sp.dma_start(ident[:], ident_in).then_inc(s_c, 16)
            sp.dma_start(stackI[:], stack_in).then_inc(s_c, 16)
            sp.dma_start(vec[:], vecs).then_inc(s_c, 16)
            sp.dma_start(bmod_sb[:], bmod).then_inc(s_bm, 16)
            for s in range(DEPTH * KD):
                if s >= 3:
                    sp.wait_ge(s_wmu, s - 2)
                sp.dma_start(wm[s % 3][:], wmod[s // KD, s % KD]).then_inc(s_wm[s % 3], 16)

            def load(nh, par, src, width):
                if not isinstance(nh, int) or nh > 0:
                    sp.wait_ge(wsplit[par], nh)
                sp.dma_start(wraw[par][:, :width], src).then_inc(wland[par], 16)

            def load_merge(l, jb, w8b, w4b):
                with sp.Fori(0, 2) as i:
                    for j in range(4):
                        load(i * 4 + (jb // 2 + j), 0, w8[l, i * 4 + (w8b + j)], D)
                        load(i * 4 + (jb // 2 + j), 1, w4[l, i * 4 + (w4b + j)], W3)

            for l in range(DEPTH):
                jl = l * NJ
                if l == 0:
                    for j in range(KD):
                        if j >= 2:
                            sp.wait_ge(s_hused, j - 1)
                        sp.dma_start(e[2 + j % 2][:, :TALL], hT_in[j]).then_inc(s_hin[j % 2], 16)
                    for n in range(2):
                        load(n // 2, n % 2, w8[l, W8_QKV + n], D)
                sp.wait_ge(s_u, KD * (l + 1))
                if l > 0:
                    sp.wait_ge(s_hst, 16 * KD)
                sp.dma_start(cosT[:], rope[0]).then_inc(s_rope, 16)
                sp.dma_start(sinT[:], rope[1]).then_inc(s_rope, 16)
                sp.dma_start(gain[:], gains[l]).then_inc(s_gain, 16)
                for n in range(2, 6):
                    load((jl + n) // 2, n % 2, w8[l, W8_QKV + n], D)
                for n in range(4):
                    load((jl + J_ZA + n) // 2, n % 2, w8[l, W8_ZA + n], D)
                with sp.Fori(0, 4) as i:
                    for c in range(2):
                        load(i + (jl + J_CONF) // 2, c, w8[l, i * 2 + (W8_CONF + c)], D)
                load_merge(l, jl + J_MA, W8_GA, 0)
                with sp.Fori(0, 4) as i:
                    for c in range(4):
                        load(i * 2 + ((jl + J_SHORT) // 2 + c // 2), c % 2, w8[l, i * 4 + (W8_SHORT + c)], D)
                load_merge(l, jl + J_MB, W8_GB, KD)
                for n in range(4):
                    load((jl + J_ZC + n) // 2, n % 2, w8[l, W8_ZC + n], D)
                load_merge(l, jl + J_MC, W8_GC, 2 * KD)
                T = TL[l]
                src = hT_in if l == 0 else hT1
                sp.wait_ge(s_mgf, KD * (l + 1))
                for j in range(KD):
                    load((jl + J_OUT + j) // 2, j % 2, w8[l, W8_OUT + j], D)
                    if j >= 2:
                        sp.wait_ge(s_z, KD * l + j - 1)
                    sp.dma_start(e[2 + j % 2][:, :T], src[j][:, :T]).then_inc(s_hin[j % 2], 16)
                if l + 1 < DEPTH:
                    for n in range(2):
                        load((jl + NJ + n) // 2, n % 2, w8[l + 1, W8_QKV + n], D)
                    for j in range(KD):
                        sp.wait_ge(s_hn, j + 1)
                        sp.dma_start(hT1[j], X[:, j, :]).then_inc(s_hst, 16)
                else:
                    for j in range(KD):
                        sp.wait_ge(s_hn, KD * (DEPTH - 1) + j + 1)
                        sp.dma_start(outT[j], e[j % 2][:, :LAT]).then_inc(s_outst[j % 2], 16)
                    for p in range(2):
                        sp.wait_ge(s_outst[p], 16 * (KD // 2))
            sp.wait_ge(s_accst, 16 * 2 * KD * DEPTH)

        @block.gpsimd
        def _(pool):
            st = Steps(pool, c_pool)

            def split(nh, par, width):
                pool.wait_ge(wland[par], nh * 16 + 16)
                if not isinstance(nh, int) or nh > 0:
                    pool.wait_ge(mm[par], nh)
                if not isinstance(nh, int):
                    pool.sem_inc(s_carry, 1)
                nc.gpsimd.tensor_copy(wh[par][:, :width], wraw[par][:, :width]).then_inc(whi[par], 1)
                pool.wait_ge(whi[par], nh + 1)
                nc.gpsimd.tensor_tensor(wl[par][:, :width], wraw[par][:, :width],
                                        wh[par][:, :width].bitcast(F32), ALU.subtract).then_inc(wsplit[par], 1)

            def split_merge(jb):
                with pool.Fori(0, 2) as i:
                    for j in range(4):
                        split(i * 4 + (jb // 2 + j), 0, D)
                        split(i * 4 + (jb // 2 + j), 1, W3)

            nc.gpsimd.memset(ones[:], 1.0 / D).then_inc(s_ones, 1)
            nc.gpsimd.memset(mhalf[:], -0.5).then_inc(s_ones, 1)
            nc.gpsimd.memset(eps[:], LN_EPS).then_inc(s_ones, 1)
            pool.wait_ge(s_ones, 3)
            for l in range(DEPTH):
                jl = l * NJ
                T = TL[l]
                for n in range(2):
                    split((jl + n) // 2, n % 2, D)
                pool.wait_ge(s_rope, 32 * (l + 1))
                pool.wait_ge(s_gain, 16 * (l + 1))
                pool.wait_ge(s_u, KD * (l + 1))
                for g, (dst, tab) in enumerate([(e[0], cosT), (e[1], sinT), (e[4], cosT), (e[5], sinT)]):
                    nc.gpsimd.tensor_tensor(
                        dst[:, :TALL].rearrange("p (t c) -> p t c", c=P),
                        tab[:].rearrange("p (t c) -> p t c", c=P),
                        gain[:, g:g + 1, :].broadcast_to([P, NTOK, P]), ALU.mult).then_inc(s_tab, 1)

                def rms(n):
                    pool.wait_ge(s_ms, l * 5 + n + 1)
                    nc.gpsimd.tensor_tensor(rstd[:], ms[:], mhalf[:], ALU.pow).then_inc(s_rstd, 1)

                rms(0)
                for n in range(4):
                    split((jl + 2 + n) // 2, n % 2, D)
                    if n >= 1:
                        rms(n)
                rms(4)
                for n in range(2):
                    split((jl + J_ZA + n) // 2, n % 2, D)
                pool.wait_ge(s_q, 4 * (l + 1))
                pool.wait_ge(s_kv, 3 * (l + 1))
                for n, (t0, nt, k0, nk) in enumerate(att_calls(l)):
                    ub, _, _ = att_base(l, n)

                    def dup(t, g):
                        pool.sem_inc(s_carry, 1)
                        nc.gpsimd.tensor_copy(
                            qd[g][:],
                            qo[:, t, g * 4 * HD:(g + 1) * 4 * HD].rearrange("p (h u d) -> p h u d", h=4, u=1)
                            .broadcast_to([P, 4, 2, HD])).then_inc(s_qd, 1)

                    if n > 0:
                        pool.wait_ge(s_s, 4 * ub)
                    for g in range(NKV):
                        dup(t0, g)
                    with pool.Fori(0, nt - 1) as i:
                        for g in range(NKV):
                            pool.wait_ge(s_s, i * 8 + (4 * (ub + g) + 4))
                            dup(i + (t0 + 1), g)
                for n in range(2, 4):
                    split((jl + J_ZA + n) // 2, n % 2, D)
                pool.wait_ge(t_done, pieces(l, O_OT + 3)[-1][0] + 1)
                nc.gpsimd.memset(hc[:], 0.0).then_inc(s_pad, 1)
                with pool.Fori(0, 4) as i:
                    for c in range(2):
                        split(i + (jl + J_CONF) // 2, c, D)
                split_merge(jl + J_MA)
                with pool.Fori(0, 4) as i:
                    for c in range(4):
                        split(i * 2 + ((jl + J_SHORT) // 2 + c // 2), c % 2, D)
                split_merge(jl + J_MB)
                for n in range(4):
                    split((jl + J_ZC + n) // 2, n % 2, D)
                split_merge(jl + J_MC)
                for n in range(KD):
                    split((jl + J_OUT + n) // 2, n % 2, D)

        @block.tensor
        def _(pe):
            mmul = nc.tensor.matmul

            def job(nh, par, K, T, hi, lo, before_k=None):
                pe.wait_ge(wsplit[par], nh + 1)
                if not isinstance(nh, int) or nh > 0:
                    pe.wait_ge(sfree[par], nh)
                for k in range(K):
                    if before_k is not None:
                        before_k(k)
                    for a, w, x in ((0, wh, hi), (1, wh, lo), (2, wl, hi)):
                        for c, n in chunks(T):
                            last = mmul(PS[:, SLOT[par] + c:SLOT[par] + c + n], w[par][:, k * P:(k + 1) * P],
                                        x[:, k, c:c + n], start=(k == 0 and a == 0), stop=(k == K - 1 and a == 2))
                last.then_inc(mm[par], 1)

            def piece_wait(f):
                if f >= 2:
                    pe.wait_ge(t_free, f - 1)

            def transposes(l, op, srcs):
                for f, c, n in pieces(l, op):
                    piece_wait(f)
                    for t in range(n // P):
                        last = nc.tensor.transpose(tbank(f, n)[:, t * P:(t + 1) * P], srcs[c // P + t], ident[:])
                    last.then_inc(t_done, 1)

            def stat(l, op, src):
                for f, c, n in pieces(l, op):
                    piece_wait(f)
                    mmul(tbank(f, n), ones[:], src[:, c:c + n], start=True, stop=True).then_inc(t_done, 1)

            pe.wait_ge(s_csilu, 1)
            for l in range(DEPTH):
                if l > 0:
                    pe.wait_ge(s_modrow, l)
                for k in range(KD):
                    s = l * KD + k
                    pe.wait_ge(s_wm[s % 3], 16 * (s // 3 + 1))
                    for n in range(6):
                        last = mmul(PS[0:2, n * 512:(n + 1) * 512], csilu[:, k, :], wm[s % 3][:, n * 512:(n + 1) * 512],
                                    start=(k == 0), stop=(k == KD - 1))
                    last.then_inc(s_wmu, 1)
                pe.wait_ge(s_modrow, l + 1)
                if l > 0:
                    pe.wait_ge(s_mod, l)
                for n in range(3 * KD):
                    last = nc.tensor.transpose(PS[:, 3072 + 2 * n:3074 + 2 * n], modrow[0:2, n * P:(n + 1) * P],
                                               ident[0:2, 0:2])
                last.then_inc(s_modtr, 1)
            pe.wait_ge(s_mod, DEPTH)

            for l in range(DEPTH):
                jl = l * NJ
                T = TL[l]
                tok = T // P

                def qkv_job(n):
                    job((jl + n) // 2, n % 2, KD, jobs_qkv(l)[n], Uh, Ul,
                        (lambda k: pe.wait_ge(s_u, KD * l + k + 1)) if n == 0 else None)

                def to_tokens(f, n):
                    pe.wait_ge(s_fc, 6 * l + n + 1)
                    transposes(l, f, [fc[n % 2][:, t * P:(t + 1) * P] for t in range(jobs_qkv(l)[n] // P)])

                def to_keys(f, g):
                    pe.wait_ge(s_kd, l + 1)
                    transposes(l, f, [kd[:, t, g].rearrange("p a d -> p (a d)") for t in range(NTOK)])

                qkv_job(0)
                qkv_job(1)
                to_tokens(0, 0)
                qkv_job(2)
                to_tokens(1, 1)
                qkv_job(3)
                to_tokens(2, 2)
                to_keys(3, 0)
                qkv_job(4)
                to_tokens(4, 3)
                to_keys(5, 1)
                qkv_job(5)
                to_tokens(6, 4)
                to_tokens(7, 5)

                for p in range(2):
                    pe.wait_ge(sfree[p], (jl + J_ZA) // 2)
                pe.wait_ge(t_free, pieces(l, O_Q3)[-1][0] + 1)
                pe.wait_ge(s_kv, 3 * (l + 1))
                for call, (t0, nt, k0, nk) in enumerate(att_calls(l)):
                    ub, ptb, ksb = att_base(l, call)
                    per = nk // 2 + 1

                    def q_fill(un, g, par, idx):
                        pe.wait_ge(s_qd, un + (ub + 1))
                        if not isinstance(idx, int) or idx > 0:
                            pe.wait_ge(pt_free[par], idx)
                        for h in range(4):
                            last = nc.tensor.transpose(PS[:, PT0[par] + h * P:PT0[par] + (h + 1) * P],
                                                       qd[g][:, h].rearrange("p a d -> p (a d)"), ident[:])
                        last.then_inc(pt_done[par], 1)

                    def scores(un, g, h):
                        first = isinstance(un, int) and ub + un == 0
                        if not (first and h < 2):
                            pe.wait_ge(s_exp, un * 4 + (4 * ub + h - 1))
                        s0 = (h % 2) * TALL
                        main, tail = score_parts(h, nk)
                        for c, n in main + tail:
                            if (c, n) in tail and not (first and h == 0):
                                pe.wait_ge(s_tail, un * 4 + (4 * ub + h))
                            for a, x in enumerate((qTh, qTl)):
                                last = mmul(PS[:, s0 + c:s0 + c + n], x[g][:, h * P:(h + 1) * P],
                                            kT[:, g, k0 * P + c:k0 * P + c + n], start=(a == 0), stop=(a == 1))
                        last.then_inc(s_s, 1)

                    def pv(un, g, kt, i0, i1):
                        par = kt % 2
                        pe.wait_ge(pt_free[par], (i0, i1)[par] + (kt // 2 + 1))
                        for a, x in enumerate((PTh, PTl)):
                            last = mmul(PS[:, O0:O0 + 512], Vt[:, k0 + kt, g, :], x[par][:],
                                        start=(kt == 0 and a == 0), stop=(kt == nk - 1 and a == 1))
                        if kt == nk - 1:
                            last.then_inc(s_pv, 1)

                    def unit(un, g, i0, i1, nxt, nxt2):
                        pe.wait_ge(s_exp, un * 4 + (4 * ub + 4))
                        for kt in range(nk):
                            par = kt % 2
                            pe.wait_ge(pt_free[par], (i0, i1)[par] + kt // 2)
                            for h in range(4):
                                last = nc.tensor.transpose(PS[:, PT0[par] + h * P:PT0[par] + (h + 1) * P],
                                                           Pr[:, g, h, kt * P:(kt + 1) * P], ident[:])
                            last.then_inc(pt_done[par], 1)
                            if nxt:
                                for h in heads_at(nk, kt):
                                    scores(un + 1, 1 - g, h)
                            if kt >= 1:
                                pv(un, g, kt - 1, i0, i1)
                        pv(un, g, nk - 1, i0, i1)
                        if nxt2:
                            q_fill(un + 2, g, 0, i0 + nk // 2)
                        pe.wait_ge(s_o, un + (ub + 1))
                        pe.wait_ge(pt_free[1], i1 + nk // 2)
                        for h in range(4):
                            last = mmul(PS[:, PT0[1] + h * HD:PT0[1] + (h + 1) * HD], ob[:, h * P:(h + 1) * P],
                                        stackI[:], start=True, stop=True)
                        last.then_inc(pt_done[1], 1)

                    q_fill(0, 0, 0, ptb[0])
                    q_fill(1, 1, 1, ptb[1])
                    pe.wait_ge(pt_free[0], ptb[0] + 1)
                    for h in range(4):
                        scores(0, 0, h)
                    pe.wait_ge(pt_free[1], ptb[1] + 1)
                    with pe.Fori(0, nt - 1) as i:
                        for g in range(NKV):
                            if g == 1:
                                pe.wait_ge(pt_free[0], i * (2 * per) + (ptb[0] + 1 + per))
                            unit(i * 2 + g, g, i * (2 * per) + (ptb[0] + 1 + g * per),
                                 i * (2 * per) + (ptb[1] + 1 + g * per), True, True)
                    un = 2 * (nt - 1)
                    unit(un, 0, ptb[0] + 1 + un * per, ptb[1] + 1 + un * per, True, False)
                    unit(un + 1, 1, ptb[0] + (un + 1) * per, ptb[1] + 1 + (un + 1) * per, False, False)

                pe.wait_ge(s_oatt, sum(2 * c[1] for ll in range(l + 1) for c in att_calls(ll)))
                for i in range(KW):
                    job((jl + J_ZA + i) // 2, i % 2, KD, T, Uh, Ul)
                    transposes(l, O_OT + i, [qo[:, t, i * P:(i + 1) * P] for t in range(tok)])
                with pe.Fori(0, 4) as i:
                    for c in range(2):
                        job(i + (jl + J_CONF) // 2, c, KD, T, Uh, Ul)

                def merge_jobs(jb):
                    with pe.Fori(0, 2) as i:
                        for j in range(4):
                            job(i * 4 + (jb // 2 + j), 0, KD, T, Uh, Ul)
                            job(i * 4 + (jb // 2 + j), 1, KW, T, Yh, Yl)

                pe.wait_ge(s_y, 12 * l + 4)
                merge_jobs(jl + J_MA)
                with pe.Fori(0, 4) as i:
                    for c in range(4):
                        job(i * 2 + ((jl + J_SHORT) // 2 + c // 2), c % 2, KD, T, Uh, Ul)
                pe.wait_ge(s_y, 12 * l + 8)
                merge_jobs(jl + J_MB)
                def zc_job(n):
                    job((jl + J_ZC + n) // 2, n % 2, KD, T, Uh, Ul)

                zc_job(0)
                pe.wait_ge(s_csum, 4 * l + 1)
                stat(l, O_CMEAN, e[4])
                zc_job(1)
                pe.wait_ge(s_csum, 4 * l + 2)
                stat(l, O_CVAR, e[5])
                zc_job(2)
                zc_job(3)
                pe.wait_ge(s_y, 12 * l + 12)
                merge_jobs(jl + J_MC)
                for j in range(KD):
                    job((jl + J_OUT + j) // 2, j % 2, KD, T, Uh, Ul,
                        (lambda k: pe.wait_ge(s_mg, KD * l + k + 1)) if j == 0 else None)
                pe.wait_ge(s_csum, 4 * l + 3)
                stat(l, O_OMEAN, e[4])
                pe.wait_ge(s_csum, 4 * l + 4)
                stat(l, O_OVAR, e[5])

        @block.scalar
        def _(act):
            st = Steps(act, c_act)
            fn = nc.scalar.activation

            act.wait_ge(s_c, 64)
            fn(csilu[:], craw[:], ACT.Silu).then_inc(s_csilu, 1)

            def modulate(l, j, src, first_use):
                b = KD * l + j
                if first_use is not None:
                    act.wait_ge(s_u, first_use)
                for c0, n, who in segs(TALL):
                    last = fn(e[j % 2][:, c0:c0 + n], src[:, c0:c0 + n], ACT.Identity,
                              scale=mod[:, l, KD + j, who:who + 1], bias=mod[:, l, j, who:who + 1])
                st.done(last)
                fn(Uh[:, j, :], e[j % 2][:, :TALL], ACT.Copy).then_inc(s_ufp, 1)

            act.wait_ge(s_mod, DEPTH)
            for j in range(KD):
                act.wait_ge(s_hin[j % 2], 16 * (j // 2 + 1))
                if j >= 2:
                    act.wait_ge(s_u, j - 1)
                for c0, n, who in segs(TALL):
                    last = fn(e[j % 2][:, c0:c0 + n], e[2 + j % 2][:, c0:c0 + n], ACT.Identity,
                              scale=mod[:, 0, KD + j, who:who + 1], bias=mod[:, 0, j, who:who + 1])
                last.then_inc(s_hused, 1)
                act.wait_ge(s_hused, j + 1)
                fn(Uh[:, j, :], e[j % 2][:, :TALL], ACT.Copy).then_inc(s_ufp, 1)

            for l in range(DEPTH):
                jl = l * NJ
                T = TL[l]
                gb = 40 * l

                def evac(n):
                    act.wait_ge(mm[n % 2], (jl + n) // 2 + 1)
                    if n >= 2:
                        act.wait_ge(t_done, pieces(l, (O_K, O_V, O_Q0, O_Q1)[n - 2])[-1][0] + 1)
                    Tn = jobs_qkv(l)[n]
                    fn(fc[n % 2][:, :Tn], slot(n % 2, Tn), ACT.Copy).then_inc(sfree[n % 2], 1)
                    act.wait_ge(sfree[n % 2], (jl + n) // 2 + 1)
                    act.sem_inc(s_fc, 1)

                def copy_pieces(op, dst, scale=1.0):
                    for f, c, n in pieces(l, op):
                        act.wait_ge(t_done, f + 1)
                        fn(dst[:, c:c + n], tbank(f, n), ACT.Copy, scale=scale).then_inc(t_free, 1)
                    act.wait_ge(t_free, f + 1)

                def copy_raw(op):
                    if 8 * l + op >= 2:
                        act.wait_ge(s_rawfree, 8 * l + op - 1)
                    copy_pieces(op, raw[op % 2])
                    return raw[op % 2]

                def square(op):
                    Tn = op_width(l, op)
                    x = copy_raw(op)
                    if op != O_K:
                        act.wait_ge(s_ms, 5 * l + [O_K, O_Q0, O_Q1, O_Q2, O_Q3].index(op))
                    fn(sq[:, :Tn], x[:, :Tn], ACT.Square).then_inc(s_sq, 1)

                def k_hi(op, g):
                    x = copy_raw(op)
                    fn(kT[:, g, :], x[:], ACT.Copy).then_inc(s_khi, 1)

                evac(0)
                evac(1)
                square(O_K)
                evac(2)
                x = copy_raw(O_V)
                if l > 0:
                    act.wait_ge(s_hst, 16 * KD)
                fn(Vt[:, :, :, 0:HD], x[:].rearrange("p (t g d) -> p t g d", g=NKV, d=HD),
                   ACT.Copy).then_inc(s_vhi, 1)
                evac(3)
                square(O_Q0)
                k_hi(O_KT0, 0)
                evac(4)
                square(O_Q1)
                k_hi(O_KT1, 1)
                evac(5)
                square(O_Q2)
                square(O_Q3)

                act.wait_ge(s_q, 4 * (l + 1))
                act.wait_ge(s_kv, 3 * (l + 1))
                for call, (t0, nt, k0, nk) in enumerate(att_calls(l)):
                    ub, ptb, ksb = att_base(l, call)
                    per = nk // 2 + 1

                    def q_hi(g, par, idx):
                        act.wait_ge(pt_done[par], idx + 1)
                        fn(qTh[g][:], PS[:, PT0[par]:PT0[par] + 512], ACT.Copy).then_inc(pt_hi[par], 1)

                    def exps(un, g, h):
                        act.wait_ge(s_nm, un * 4 + (4 * ub + h + 1))
                        s0 = (h % 2) * TALL
                        main, tail = score_parts(h, nk)
                        m = 4 * g + h
                        (c, n), = tail
                        fn(Pr[:, g, h, c:c + n], PS[:, s0 + c:s0 + c + n], ACT.Exp, bias=nm[:, m:m + 1],
                           scale=HD ** -0.5, accum_out=rs[:, g, 0, h:h + 1]).then_inc(s_tail, 1)
                        if main:
                            c = main[0][0]
                            fn(Pr[:, g, h, c:c + 1024], PS[:, s0 + c:s0 + c + 1024], ACT.Exp, bias=nm[:, m:m + 1],
                               scale=HD ** -0.5, accum_out=rs[:, g, 1, h:h + 1]).then_inc(s_exp, 1)
                        else:
                            act.wait_ge(s_tail, un * 4 + (4 * ub + h + 1))
                            act.sem_inc(s_exp, 1)

                    def unit(un, g, i0, i1, nxt, nxt2):
                        for kt in range(nk):
                            par = kt % 2
                            act.wait_ge(pt_done[par], (i0, i1)[par] + (kt // 2 + 1))
                            fn(PTh[par][:], PS[:, PT0[par]:PT0[par] + 512], ACT.Copy).then_inc(pt_hi[par], 1)
                            if nxt:
                                for h in heads_at(nk, kt):
                                    exps(un + 1, 1 - g, h)
                        act.wait_ge(s_pv, un + (ub + 1))
                        fn(ob[:], PS[:, O0:O0 + 512], ACT.Copy).then_inc(s_o, 1)
                        if nxt2:
                            q_hi(g, 0, i0 + nk // 2)

                    q_hi(0, 0, ptb[0])
                    q_hi(1, 1, ptb[1])
                    for h in range(4):
                        exps(0, 0, h)
                    with act.Fori(0, nt - 1) as i:
                        for g in range(NKV):
                            unit(i * 2 + g, g, i * (2 * per) + (ptb[0] + 1 + g * per),
                                 i * (2 * per) + (ptb[1] + 1 + g * per), True, True)
                    un = 2 * (nt - 1)
                    unit(un, 0, ptb[0] + 1 + un * per, ptb[1] + 1 + un * per, True, False)
                    unit(un + 1, 1, ptb[0] + (un + 1) * per, ptb[1] + 1 + (un + 1) * per, False, False)

                act.wait_ge(s_oatt, sum(2 * c[1] for ll in range(l + 1) for c in att_calls(ll)))
                for i in range(KW):
                    act.wait_ge(mm[i % 2], (jl + J_ZA + i) // 2 + 1)
                    if i >= 2:
                        act.wait_ge(s_yf, 12 * l + i - 1)
                    fn(e[i % 2][:, :T], slot(i % 2, T), ACT.Silu).then_inc(sfree[i % 2], 1)
                    if i >= 2:
                        act.wait_ge(s_yf, 12 * l + i - 1)
                    copy_pieces(O_OT + i, e[4 + i % 2])
                    act.sem_inc(s_oraw, 1)
                    act.wait_ge(s_yf, 12 * l + i + 1)
                    fn(Yh[:, i, :T], e[2 + i % 2][:, :T], ACT.Copy).then_inc(s_yh, 1)

                with act.Fori(0, 4) as i:
                    act.wait_ge(mm[0], i + ((jl + J_CONF) // 2 + 1))
                    act.wait_ge(sfree[1], i + (jl + J_CONF) // 2)
                    fn(e[0][:, :T], slot(0, T), ACT.Sigmoid).then_inc(sfree[0], 1)

                def merge(branch):
                    jb = jl + (J_MA, J_MB, J_MC)[branch]
                    yb = (3 * l + branch) * KD
                    ab = 2 * l * KD
                    with act.Fori(0, 2) as i:
                        for j in range(4):
                            act.wait_ge(sfree[1], i * 4 + (jb // 2 + j))
                            if branch > 0:
                                act.wait_ge(s_mgd, i * 4 + (yb + j))
                                act.dma_start(e[1][:, :T], accd[branch - 1, i * 4 + j][:, :T]).then_inc(s_accin, 16)
                            act.wait_ge(mm[0], i * 4 + (jb // 2 + j + 1))
                            fn(e[0][:, :T], slot(0, T), ACT.Sigmoid).then_inc(sfree[0], 1)
                            if branch < 2:
                                act.wait_ge(s_mgd, i * 4 + (yb + j + 1))
                                act.dma_start(accd[branch, i * 4 + j][:, :T], e[4 + j % 2][:, :T]).then_inc(s_accst, 16)
                                act.wait_ge(s_accst, i * 64 + 16 * (ab + branch * KD + j + 1))

                merge(0)

                with act.Fori(0, 4) as i:
                    hb = (jl + J_SHORT) // 2
                    act.wait_ge(mm[0], i * 2 + (hb + 1))
                    act.wait_ge(sfree[1], i * 2 + hb)
                    fn(e[0][:, :T], slot(0, T), ACT.Copy).then_inc(sfree[0], 1)
                    act.wait_ge(mm[0], i * 2 + (hb + 2))
                    act.wait_ge(sfree[1], i * 2 + (hb + 1))
                    act.wait_ge(s_yf, i + (12 * l + 4))
                    fn(e[4][:, :T], slot(0, T), ACT.Silu).then_inc(sfree[0], 1)
                    act.wait_ge(s_yf, i + (12 * l + 5))
                    act.sem_inc(s_carry, 1)
                    fn(Yh[:, i, :T], e[3][:, :T], ACT.Copy).then_inc(s_yh, 1)

                merge(1)

                def silu_z(n):
                    act.wait_ge(mm[n % 2], (jl + J_ZC + n) // 2 + 1)
                    fn(hc[:, n, :T], slot(n % 2, T), ACT.Silu).then_inc(sfree[n % 2], 1)

                def squares(first, srcs):
                    for n, s in enumerate(srcs):
                        act.wait_ge(s_dev, first + n + 1)
                        if n >= 2:
                            act.wait_ge(s_lacc, first + n - 1)
                        fn(e[n % 2][:, :T], s, ACT.Square).then_inc(s_lsq, 1)

                def mean(op, nt):
                    copy_pieces(op, e[4], float(KD) / nt)
                    act.sem_inc(s_mean, 1)

                def root(op, nt):
                    for f, c, n in pieces(l, op):
                        act.wait_ge(t_done, f + 1)
                        fn(e[4][:, c:c + n], tbank(f, n), ACT.Sqrt, scale=float(KD) / nt,
                           bias=eps[:]).then_inc(t_free, 1)
                    act.wait_ge(t_free, f + 1)
                    act.sem_inc(s_std, 1)

                act.wait_ge(s_csum, 4 * l + 1)
                silu_z(0)
                mean(O_CMEAN, KW)
                squares(12 * l, [cv[:, n, :T] for n in range(KW)])
                silu_z(1)
                root(O_CVAR, KW)
                silu_z(2)
                silu_z(3)
                for n in range(KW):
                    act.wait_ge(s_norm, 12 * l + n + 1)
                    if n >= 2:
                        act.wait_ge(s_yf, 12 * l + 8 + n - 1)
                    fn(e[n % 2][:, :T], cv[:, n, :T], ACT.Silu, scale=vec[:, l, V_CG + n:V_CG + n + 1],
                       bias=vec[:, l, V_CB + n:V_CB + n + 1]).then_inc(s_hact, 1)
                    act.wait_ge(s_yf, 12 * l + 8 + n + 1)
                    fn(Yh[:, n, :T], e[2 + n % 2][:, :T], ACT.Copy).then_inc(s_yh, 1)

                merge(2)

                act.wait_ge(mm[0], (jl + J_OUT) // 2)
                for j in range(KD):
                    act.wait_ge(s_mgf, KD * l + j + 1)
                    fn(Uh[:, j, :T], X[:, j, :T], ACT.Copy).then_inc(s_mgh, 1)

                for j in range(KD):
                    act.wait_ge(mm[j % 2], (jl + J_OUT + j) // 2 + 1)
                    if j >= 2:
                        act.wait_ge(s_z, KD * l + j - 1)
                    for c0, n, who in segs(T):
                        last = fn(e[j % 2][:, c0:c0 + n], PS[:, SLOT[j % 2] + c0:SLOT[j % 2] + c0 + n], ACT.Copy,
                                  scale=mod[:, l, 2 * KD + j, who:who + 1])
                    last.then_inc(sfree[j % 2], 1)
                mean(O_OMEAN, KD)
                squares(12 * l + 4, [Z[:, n, :T] for n in range(KD)])
                root(O_OVAR, KD)
                for j in range(KD):
                    act.wait_ge(s_norm, 12 * l + 4 + j + 1)
                    if l + 1 < DEPTH:
                        fn(X[:, j, :T], Z[:, j, :T], ACT.Identity, scale=vec[:, l, V_PG + j:V_PG + j + 1],
                           bias=vec[:, l, V_PB + j:V_PB + j + 1]).then_inc(s_hn, 1)
                        act.wait_ge(s_hn, KD * l + j + 1)
                        modulate(l + 1, j, X[:, j, :], KD * (l + 1) + j - 1 if j >= 2 else None)
                    else:
                        if j >= 2:
                            act.wait_ge(s_outst[j % 2], 16 * (j // 2))
                        fn(e[j % 2][:, :T], Z[:, j, :T], ACT.Identity, scale=vec[:, l, V_PG + j:V_PG + j + 1],
                           bias=vec[:, l, V_PB + j:V_PB + j + 1]).then_inc(s_hn, 1)

        @block.vector
        def _(dve):
            st = Steps(dve, c_dve)
            tt, stt, ts = nc.vector.tensor_tensor, nc.vector.scalar_tensor_tensor, nc.vector.tensor_scalar

            dve.wait_ge(s_bm, 16)
            for l in range(DEPTH):
                dve.wait_ge(s_wmu, KD * (l + 1))
                if l > 0:
                    dve.wait_ge(s_modtr, l)
                tt(modrow[:], PS[0:2, 0:3 * D], bmod_sb[:, l, :], ALU.add).then_inc(s_modrow, 1)
                dve.wait_ge(s_modtr, l + 1)
                cols = PS[:, 3072:3072 + 6 * KD].rearrange("p (n w) -> p n w", w=2)
                st.done(nc.vector.tensor_copy(mod[:, l], cols))
                ts(mod[:, l, KD:2 * KD], cols[:, KD:2 * KD], 1.0, None, ALU.add).then_inc(s_mod, 1)

            def u_lo(l, j):
                dve.wait_ge(s_ufp, KD * l + j + 1)
                tt(Ul[:, j, :], e[j % 2][:, :TALL], Uh[:, j, :].bitcast(F32), ALU.subtract).then_inc(s_u, 1)

            for j in range(KD):
                u_lo(0, j)

            for l in range(DEPTH):
                jl = l * NJ
                T = TL[l]

                def normed(op, n, Tn, A, B, dst):
                    H2 = 2 * Tn // P
                    dve.wait_ge(s_sq, 5 * l + n + 1)
                    st.done(nc.vector.reduce_sum(ss[:, :H2], sq[:, :Tn].rearrange("p (h d) -> p h d", d=HD), AX_X))
                    ts(ms[:, :H2], ss[:, :H2], 1.0 / HD, RMS_EPS, ALU.mult, ALU.add).then_inc(s_ms, 1)
                    dve.wait_ge(s_rstd, 5 * l + n + 1)
                    tt(qn[:, :Tn].rearrange("p (h d) -> p h d", d=HD),
                       raw[op % 2][:, :Tn].rearrange("p (h d) -> p h d", d=HD),
                       rstd[:, :H2].rearrange("p (h o) -> p h o", o=1).broadcast_to([P, H2, HD]),
                       ALU.mult).then_inc(s_rawfree, 1)
                    dve.wait_ge(s_rawfree, 8 * l + op + 1)
                    if n < 2:
                        dve.wait_ge(s_tab, 4 * l + 2 + 2 * n)
                    tt(qa[:, :Tn], qn[:, :Tn], A[:, :Tn], ALU.mult)

                    def pair(x, a):
                        return x[:, :Tn].rearrange("p (b a c) -> p b a c", a=2, c=HD // 4)[:, :, a, :]

                    tt(pair(qb, 0), pair(qn, 1), pair(B, 0), ALU.mult)
                    st.done(tt(pair(qb, 1), pair(qn, 0), pair(B, 1), ALU.mult))
                    return dst(Tn)

                def k_out(Tn):
                    for a in range(2):
                        last = tt(kd[:, :, :, a, :].rearrange("p t g d -> p (t g) d"),
                                  qa[:].rearrange("p (h d) -> p h d", d=HD),
                                  qb[:].rearrange("p (h d) -> p h d", d=HD), ALU.add)
                    last.then_inc(s_kd, 1)

                def q_out(i):
                    def f(Tn):
                        tt(qo[:, :Tn // P, i * P:(i + 1) * P], qa[:, :Tn].rearrange("p (t c) -> p t c", c=P),
                           qb[:, :Tn].rearrange("p (t c) -> p t c", c=P), ALU.add).then_inc(s_q, 1)
                    return f

                def k_lo(g):
                    dve.wait_ge(s_khi, 2 * l + g + 1)
                    st.done(tt(kT[HD:P, g, :], raw[1][HD:P, :], kT[HD:P, g, :].bitcast(F32), ALU.subtract))
                    dve.sem_inc(s_rawfree, 1)
                    dve.sem_inc(s_kv, 1)

                normed(O_K, 0, TALL, e[0], e[1], k_out)
                dve.wait_ge(s_vhi, l + 1)
                st.done(tt(Vt[:, :, :, HD:P].rearrange("p t g d -> p (t g) d"),
                           raw[O_V % 2][:].rearrange("p (h d) -> p h d", d=HD),
                           Vt[:, :, :, 0:HD].rearrange("p t g d -> p (t g) d").bitcast(F32), ALU.subtract))
                dve.sem_inc(s_rawfree, 1)
                dve.sem_inc(s_kv, 1)
                normed(O_Q0, 1, T, e[4], e[5], q_out(0))
                k_lo(0)
                normed(O_Q1, 2, T, e[4], e[5], q_out(1))
                k_lo(1)
                normed(O_Q2, 3, T, e[4], e[5], q_out(2))
                normed(O_Q3, 4, T, e[4], e[5], q_out(3))

                for call, (t0, nt, k0, nk) in enumerate(att_calls(l)):
                    ub, ptb, ksb = att_base(l, call)
                    per = nk // 2 + 1
                    hb = [ptb[0], ptb[1] - ub]

                    def q_lo(g, par, idx_hi):
                        dve.wait_ge(pt_hi[par], idx_hi + 1)
                        tt(qTl[g][:], PS[:, PT0[par]:PT0[par] + 512], qTh[g][:].bitcast(F32),
                           ALU.subtract).then_inc(pt_free[par], 1)

                    def maxes(un, g, h):
                        dve.wait_ge(s_s, un * 4 + (4 * ub + h + 1))
                        s0 = (h % 2) * TALL
                        m = 4 * g + h
                        st.done(nc.vector.reduce_max(mx[:, m:m + 1], PS[:, s0:s0 + nk * P], AX_X))
                        ts(nm[:, m:m + 1], mx[:, m:m + 1], -(HD ** -0.5), None, ALU.mult).then_inc(s_nm, 1)

                    def unit(un, t, g, h0, h1, nxt, nxt2):
                        for kt in range(nk):
                            par = kt % 2
                            dve.wait_ge(pt_hi[par], (h0, h1)[par] + (kt // 2 + 1))
                            tt(PTl[par][:], PS[:, PT0[par]:PT0[par] + 512], PTh[par][:].bitcast(F32),
                               ALU.subtract).then_inc(pt_free[par], 1)
                            if nxt:
                                for h in heads_at(nk, kt):
                                    maxes(un + 1, 1 - g, h)
                        if nk * P > 256:
                            st.done(tt(rsum[:], rs[:, g, 0, :], rs[:, g, 1, :], ALU.add))
                            st.done(nc.vector.reciprocal(ri[:], rsum[:]))
                        else:
                            st.done(nc.vector.reciprocal(ri[:], rs[:, g, 0, :]))
                        if nxt2:
                            q_lo(g, 0, h0 + nk // 2)
                        dve.wait_ge(pt_done[1], h1 + (nk // 2 + 1) + un + ub)
                        st.done(tt(qo[:, t, g * 4 * HD:(g + 1) * 4 * HD].rearrange("p (h d) -> p h d", d=HD),
                                   PS[:, PT0[1]:PT0[1] + 4 * HD].rearrange("p (h d) -> p h d", d=HD),
                                   ri[:].rearrange("p (h o) -> p h o", o=1).broadcast_to([P, 4, HD]), ALU.mult))
                        dve.sem_inc(pt_free[1], 1)
                        dve.sem_inc(s_oatt, 1)

                    q_lo(0, 0, hb[0])
                    q_lo(1, 1, hb[1])
                    for h in range(4):
                        maxes(0, 0, h)
                    p1 = nk // 2
                    with st.loop(0, nt - 1, 14 if nk * P > 256 else 12) as i:
                        for g in range(NKV):
                            unit(i * 2 + g, i + t0, g, i * (2 * per) + (hb[0] + 1 + g * per),
                                 i * (2 * p1) + (hb[1] + 1 + g * p1), True, True)
                    un = 2 * (nt - 1)
                    unit(un, t0 + nt - 1, 0, hb[0] + 1 + un * per, hb[1] + 1 + un * p1, True, False)
                    unit(un + 1, t0 + nt - 1, 1, hb[0] + (un + 1) * per, hb[1] + 1 + (un + 1) * p1, False, False)

                for i in range(KW):
                    dve.wait_ge(sfree[i % 2], (jl + J_ZA + i) // 2 + 1)
                    dve.wait_ge(s_oraw, KW * l + i + 1)
                    tt(e[2 + i % 2][:, :T], e[4 + i % 2][:, :T], e[i % 2][:, :T], ALU.mult).then_inc(s_yf, 1)
                    dve.wait_ge(s_yh, 12 * l + i + 1)
                    tt(Yl[:, i, :T], e[2 + i % 2][:, :T], Yh[:, i, :T].bitcast(F32), ALU.subtract).then_inc(s_y, 1)

                dve.wait_ge(s_pad, l + 1)
                hb = (jl + J_CONF) // 2
                wmid = V_WC + CPAD
                with st.loop(0, 4, 2) as i:
                    dve.wait_ge(mm[1], i + (hb + 1))
                    dve.wait_ge(sfree[0], i + (hb + 1))
                    for c0, n, who in segs(T):
                        last = tt(hc[:, i, CPAD * (1 + who) + c0:CPAD * (1 + who) + c0 + n],
                                  PS[:, SLOT[1] + c0:SLOT[1] + c0 + n], e[0][:, c0:c0 + n], ALU.mult)
                    st.done(last)
                    dve.sem_inc(sfree[1], 1)
                    for c0, n, who in segs(T):
                        last = ts(cv[:, i, c0:c0 + n], hc[:, i, CPAD * (1 + who) + c0:CPAD * (1 + who) + c0 + n],
                           vec[:, l, bass.ds(i * CONF_K + wmid, 1)], vec[:, l, bass.ds(i + V_BDW, 1)],
                           ALU.mult, ALU.add)
                    st.done(last)

                def conv_taps(i, c_base, taps):
                    for tap in taps:
                        for c0, n, who in segs(T):
                            last = stt(cv[:, i + c_base, c0:c0 + n],
                                       hc[:, i + c_base, CPAD * who + c0 + tap:CPAD * who + c0 + tap + n],
                                       vec[:, l, bass.ds(i * CONF_K + (V_WC + c_base * CONF_K + tap), 1)],
                                       cv[:, i + c_base, c0:c0 + n], ALU.mult, ALU.add)
                        st.done(last)

                TAPS = [t for t in range(CONF_K) if t != CPAD]
                PART = [TAPS[0:8], TAPS[8:15], TAPS[15:23], TAPS[23:30]]

                def merge(branch):
                    jb = (jl + (J_MA, J_MB, J_MC)[branch]) // 2
                    conv = branch < 2
                    with st.loop(0, 2, (30 if conv else 0) + (4 if branch > 0 else 0)) as i:
                        for j in range(4):
                            if conv:
                                conv_taps(i, 2 * branch, PART[j])
                            dve.wait_ge(mm[1], i * 4 + (jb + j + 1))
                            dve.wait_ge(sfree[0], i * 4 + (jb + j + 1))
                            a = e[4 + j % 2][:, :T]
                            if branch == 0:
                                tt(a, slot(1, T), e[0][:, :T], ALU.mult).then_inc(sfree[1], 1)
                                dve.wait_ge(sfree[1], i * 4 + (jb + j + 1))
                                dve.sem_inc(s_mgd, 1)
                                continue
                            if branch == 1:
                                tt(a, slot(1, T), e[0][:, :T], ALU.mult).then_inc(sfree[1], 1)
                            else:
                                stt(a, slot(1, T), vec[:, l, bass.ds(i * 4 + (V_BPC + j), 1)], e[0][:, :T],
                                    ALU.add, ALU.mult).then_inc(sfree[1], 1)
                            dve.wait_ge(sfree[1], i * 4 + (jb + j + 1))
                            nin = (2 * l + branch - 1) * KD + j
                            dve.wait_ge(s_accin, i * 64 + 16 * (nin + 1))
                            dst = a if branch == 1 else X[:, i * 4 + j, :T]
                            st.done(tt(dst, a, e[1][:, :T], ALU.add))
                            dve.sem_inc(s_mgd, 1)
                            if branch == 2:
                                dve.sem_inc(s_mgf, 1)

                merge(0)
                dve.wait_ge(s_accst, 16 * (2 * l + 1) * KD)

                dve.wait_ge(mm[1], (jl + J_SHORT) // 2)
                st.done(nc.vector.memset(e[1][:], 0.0))
                hb = (jl + J_SHORT) // 2
                with st.loop(0, 4, 5) as i:
                    dve.wait_ge(mm[1], i * 2 + (hb + 1))
                    dve.wait_ge(sfree[0], i * 2 + (hb + 1))
                    for c0, n, who in segs(T):
                        last = tt(e[1][:, SPAD * (1 + who) + c0:SPAD * (1 + who) + c0 + n],
                                  PS[:, SLOT[1] + c0:SLOT[1] + c0 + n], e[0][:, c0:c0 + n], ALU.mult)
                    st.done(last)
                    dve.sem_inc(sfree[1], 1)
                    for tap in range(SHORT_K):
                        wt = vec[:, l, bass.ds(i * SHORT_K + (V_WS + tap), 1)]
                        for c0, n, who in segs(T):
                            x = e[1][:, SPAD * who + c0 + tap:SPAD * who + c0 + tap + n]
                            if tap == 0:
                                last = ts(e[2][:, c0:c0 + n], x, wt, None, ALU.mult)
                            else:
                                last = stt(e[2][:, c0:c0 + n], x, wt, e[2][:, c0:c0 + n], ALU.mult, ALU.add)
                        st.done(last)
                    dve.wait_ge(mm[1], i * 2 + (hb + 2))
                    st.done(tt(e[2][:, :T], slot(1, T), e[2][:, :T], ALU.mult))
                    dve.wait_ge(sfree[0], i * 2 + (hb + 2))
                    tt(e[3][:, :T], e[2][:, :T], e[4][:, :T], ALU.mult).then_inc(s_yf, 1)
                    dve.sem_inc(sfree[1], 1)
                    dve.wait_ge(s_yh, i + (12 * l + 5))
                    tt(Yl[:, i, :T], e[3][:, :T], Yh[:, i, :T].bitcast(F32), ALU.subtract).then_inc(s_y, 1)

                merge(1)
                dve.wait_ge(s_accst, 16 * (2 * l + 2) * KD)

                def norm(k, z, nt, first):
                    dve.wait_ge(s_mean, k + 1)
                    for j in range(nt):
                        tt(z(j), z(j), e[4][:, :T], ALU.subtract).then_inc(s_dev, 1)
                        if j >= 1:
                            add_square(j - 1, first)
                    add_square(nt - 1, first)
                    dve.wait_ge(s_lacc, first + nt)
                    dve.sem_inc(s_csum, 1)
                    dve.wait_ge(s_std, k + 1)
                    st.done(nc.vector.reciprocal(e[4][:, :T], e[4][:, :T]))

                def add_square(j, first):
                    dve.wait_ge(s_lsq, first + j + 1)
                    if j == 0:
                        nc.vector.tensor_copy(e[5][:, :T], e[0][:, :T]).then_inc(s_lacc, 1)
                    else:
                        dve.wait_ge(s_lacc, first + j)
                        tt(e[5][:, :T], e[5][:, :T], e[j % 2][:, :T], ALU.add).then_inc(s_lacc, 1)

                st.done(tt(e[4][:, :T], cv[:, 0, :T], cv[:, 1, :T], ALU.add))
                st.done(tt(e[4][:, :T], e[4][:, :T], cv[:, 2, :T], ALU.add))
                st.done(tt(e[4][:, :T], e[4][:, :T], cv[:, 3, :T], ALU.add))
                dve.sem_inc(s_csum, 1)
                norm(2 * l, lambda j: cv[:, j, :T], KW, 12 * l)
                for n in range(KW):
                    tt(cv[:, n, :T], cv[:, n, :T], e[4][:, :T], ALU.mult).then_inc(s_norm, 1)
                dve.wait_ge(mm[1], (jl + J_ZC) // 2)
                for n in range(KW):
                    dve.wait_ge(s_hact, 4 * l + n + 1)
                    dve.wait_ge(sfree[n % 2], (jl + J_ZC + n) // 2 + 1)
                    tt(e[2 + n % 2][:, :T], e[n % 2][:, :T], hc[:, n, :T], ALU.mult).then_inc(s_yf, 1)
                    dve.wait_ge(s_yh, 12 * l + 8 + n + 1)
                    tt(Yl[:, n, :T], e[2 + n % 2][:, :T], Yh[:, n, :T].bitcast(F32), ALU.subtract).then_inc(s_y, 1)

                merge(2)

                for j in range(KD):
                    dve.wait_ge(s_mgh, KD * l + j + 1)
                    tt(Ul[:, j, :T], X[:, j, :T], Uh[:, j, :T].bitcast(F32), ALU.subtract).then_inc(s_mg, 1)

                for j in range(KD):
                    dve.wait_ge(sfree[j % 2], (jl + J_OUT + j) // 2 + 1)
                    nh_in = (KD // 2) * (l + 1) + j // 2 + 1
                    dve.wait_ge(s_hin[j % 2], 16 * nh_in)
                    stt(Z[:, j, :T], e[2 + j % 2][:, :T], ALPHA, e[j % 2][:, :T], ALU.mult,
                        ALU.add).then_inc(s_z, 1)
                    dve.wait_ge(s_z, KD * l + j + 1)
                    if j == 1:
                        st.done(tt(e[4][:, :T], Z[:, 0, :T], Z[:, 1, :T], ALU.add))
                    elif j > 1:
                        st.done(tt(e[4][:, :T], e[4][:, :T], Z[:, j, :T], ALU.add))
                dve.sem_inc(s_csum, 1)
                norm(2 * l + 1, lambda j: Z[:, j, :T], KD, 12 * l + 4)
                for j in range(KD):
                    tt(Z[:, j, :T], Z[:, j, :T], e[4][:, :T], ALU.mult).then_inc(s_norm, 1)
                    if l + 1 < DEPTH and j >= 1:
                        u_lo(l + 1, j - 1)
                if l + 1 < DEPTH:
                    u_lo(l + 1, KD - 1)


def _tiles(w):
    K, N = w.shape
    return np.ascontiguousarray(w.reshape(K // P, P, N // P, P).transpose(2, 1, 0, 3)).reshape(N // P, P, K)


def _cols(v):
    return v.reshape(-1, P).T


def _rope():
    q = HD // 4
    freqs = (10000.0 ** (-np.arange(q, dtype=np.float32) / q)).astype(np.float32)
    n = np.arange(LAT)
    ar = (n // GRID_W).astype(np.float32)[:, None] * freqs
    ac = (n % GRID_W).astype(np.float32)[:, None] * freqs
    c = np.concatenate([np.cos(ar), np.cos(ar), np.cos(ac), np.cos(ac)], 1)
    s = np.concatenate([-np.sin(ar), np.sin(ar), -np.sin(ac), np.sin(ac)], 1)
    c = np.concatenate([c, np.ones((CTX, HD))], 0)
    s = np.concatenate([s, np.zeros((CTX, HD))], 0)
    both = np.stack([np.concatenate([x, x], 1) for x in (c, s)]).astype(np.float32)
    return np.ascontiguousarray(both.reshape(2, NTOK, P, P).transpose(0, 2, 1, 3)).reshape(2, P, TALL)


def kernel(**inputs):
    import concourse.bacc as _bacc
    from concourse.bass_utils import run_bass_kernel_spmd as _run

    a = {k: np.asarray(v) for k, v in inputs.items()}
    w8, w4, vecs, gains = [], [], [], []
    for l in range(DEPTH):
        w8.append(np.concatenate([_tiles(a["w_in"][l])[W_ORDER], _tiles(a["w_out"][l])]))
        w4.append(np.concatenate([_tiles(a[n][l]) for n in ("w_proj_attn", "w_proj_short", "w_proj_conf")]))
        vecs.append(np.concatenate(
            [_cols(a["post_ln_g"][l]), _cols(a["post_ln_b"][l]), _cols(a["b_proj_conf"][l]),
             _cols(a["conf_ln_g"][l]), _cols(a["conf_ln_b"][l]), _cols(a["b_conf_dw"][l]),
             a["w_short_conv"][l].reshape(SHORT_K, KW, P).transpose(2, 1, 0).reshape(P, -1),
             a["w_conf_dw"][l].reshape(CONF_K, KW, P).transpose(2, 1, 0).reshape(P, -1)], 1))
        rows = []
        for g in (a["k_gain"][l], a["q_gain"][l]):
            sw = g.reshape(2, 2, HD // 4)[:, ::-1].reshape(HD)
            rows += [np.concatenate([g, g]), np.concatenate([sw, sw])]
        gains.append(np.broadcast_to(np.stack(rows)[None], (P, 4, P)))
    hT = np.concatenate([a["x"][0], a["ctx"][0]]).T.reshape(KD, P, TALL)
    eye = np.eye(P, dtype=np.float32)
    feed = {
        "hT_in": hT,
        "cvec": np.stack([_cols(a["c"][0]), _cols(a["c_ctx"])], 2),
        "wmod": a["w_mod"].reshape(DEPTH, KD, P, 3 * D),
        "bmod": np.broadcast_to(a["b_mod"][None], (2, DEPTH, 3 * D)),
        "w8": np.stack(w8), "w4": np.stack(w4),
        "vecs": np.stack(vecs, 1), "gains": np.stack(gains),
        "rope": _rope(), "ident_in": eye, "stack_in": np.concatenate([eye[:HD, :HD]] * 2),
    }
    nc = _bacc.Bacc("TRN2", target_bir_lowering=False, num_devices=1, dynamic_dma_scratch_size=1024)
    arrays, args = {}, []
    for name, v in feed.items():
        v = np.ascontiguousarray(v)
        arrays[name] = v
        args.append(nc.dram_tensor(name, v.shape, F32, kind="ExternalInput").ap())
    args.append(nc.dram_tensor("outT", (KD, P, LAT), F32, kind="ExternalOutput").ap())
    build(nc, *args)
    r = _run(nc, [arrays], core_ids=[0])
    return np.ascontiguousarray(r.results[0]["outT"].reshape(D, LAT).T).reshape(1, LAT, D)
```

```python
from contextlib import ExitStack, contextmanager

import numpy as np
import concourse.bass as bass
from concourse import mybir

F32 = mybir.dt.float32
F32R = mybir.dt.float32r
ACT = mybir.ActivationFunctionType
ALU = mybir.AluOpType
AX_X = mybir.AxisListType.X

P = 128
D = 1024
KD = D // P
LAT, CTX = 1024, 256
TALL = LAT + CTX
NTOK = TALL // P
DEPTH = 2
GRID_W = 64
HD = 64
NKV = 2
W3 = 512
KW = W3 // P
SHORT_K, CONF_K = 3, 31
SPAD, CPAD = SHORT_K // 2, CONF_K // 2
ALPHA = (2.0 * DEPTH) ** 0.25
LN_EPS, RMS_EPS = 1e-5, 1e-6
HCW = CPAD + LAT + CPAD + CTX + CPAD + 1
EW = 1296

_Q, _K, _V, _ZA = range(0, 4), [4], [5], range(6, 10)
_SB, _SC, _SH, _ZS = range(10, 14), range(14, 18), range(18, 22), range(22, 26)
_CA, _CG, _ZC = range(26, 30), range(30, 34), range(34, 38)
_GA, _GB, _GC = range(38, 46), range(46, 54), range(54, 62)
W_ORDER = [*_K, *_Q, *_V, *_ZA]
for _i in range(KW):
    W_ORDER += [_CG[_i], _CA[_i]]
W_ORDER += [*_GA]
for _i in range(KW):
    W_ORDER += [_SC[_i], _SH[_i], _ZS[_i], _SB[_i]]
W_ORDER += [*_GB, *_ZC, *_GC]
N_WIN = len(W_ORDER)
N_W8 = N_WIN + KD
W8_QKV, W8_ZA, W8_CONF, W8_GA, W8_SHORT, W8_GB, W8_ZC, W8_GC, W8_OUT = 0, 6, 10, 18, 26, 42, 50, 54, 62
J_QKV, J_ZA, J_CONF, J_MA, J_SHORT, J_MB, J_ZC, J_MC, J_OUT, NJ = 0, 6, 10, 18, 34, 50, 66, 70, 86, 94

V_PG, V_PB, V_BPC, V_CG, V_CB, V_BDW = 0, 8, 16, 24, 28, 32
V_WS = 36
V_WC = V_WS + KW * SHORT_K
V_BM = V_WC + KW * CONF_K
NV = V_BM + 3 * KD

O_K, O_Q0, O_Q1, O_KT0, O_KT1, O_Q2, O_Q3, O_V = range(8)
QKV_OPS = (O_K, O_Q0, O_Q1, O_Q2, O_Q3, O_V)
O_OT, O_CMEAN, O_CVAR, O_OMEAN, O_OVAR, N_OPS = 8, 12, 13, 14, 15, 16
SLOT = (0, 1536)
TB = (3072, 3584)
PT0 = (2560, 3072)
O0 = 3584


def chunks(n):
    return [(c, min(512, n - c)) for c in range(0, n, 512)]


def op_width(l, op):
    return TALL if l == 0 or op in (O_K, O_V, O_KT0, O_KT1) else LAT


def pieces(l, op):
    n = sum(len(chunks(op_width(a, b))) for a in range(DEPTH) for b in range(N_OPS) if (a, b) < (l, op))
    return [(n + i, c, m) for i, (c, m) in enumerate(chunks(op_width(l, op)))]


def segs(T):
    return [(0, LAT, 0)] + ([(LAT, CTX, 1)] if T > LAT else [])


def heads_at(nk, kt, nxt, nxt2):
    if nk == 2:
        return [(1, h) for h in range(4)] if kt == 0 and nxt else []
    if kt == nk - 1:
        return [(2, 0)] if nxt2 else []
    return [(1, (kt + 1) // 2)] if kt % 2 and kt < 7 and nxt else []


def exps_at(nk, kt, nxt):
    if nk == 2:
        return [h for _, h in heads_at(nk, kt, nxt, False)]
    return [(kt - 1) // 2] if kt % 2 and kt < 8 and nxt else []


def q_after(nk):
    return nk - 2 if nk > 2 else 1


def back_after(nk):
    return 2 if nk > 2 else 0


def fill(nk, kt, i0, i1, prev, nxt2):
    if kt % 2 == 0:
        return i0 + kt // 2
    return i1 + kt // 2 - (1 if prev and kt < back_after(nk) else 0) + (1 if nxt2 and kt > q_after(nk) else 0)


def score_parts(h, nk):
    if nk * P <= 256:
        return [], [(0, nk * P)]
    if h % 2 == 0:
        return [(0, 512), (512, 512)], [(1024, 256)]
    return [(256, 512), (768, 512)], [(0, 256)]


class Steps:

    def __init__(self, eng, sem):
        self.eng, self.sem, self.base, self.i, self.per, self.lo = eng, sem, 0, None, 0, 0

    def done(self, ins):
        ins.then_inc(self.sem, 1)
        self.base += 1
        n = self.base if self.i is None else (self.i - self.lo) * self.per + self.base
        self.eng.wait_ge(self.sem, n)

    @contextmanager
    def loop(self, lo, hi, per):
        start = self.base
        with self.eng.Fori(lo, hi) as i:
            self.i, self.per, self.lo = i, per, lo
            yield i
        assert self.base - start == per, (self.base - start, per)
        self.i = None
        self.base = start + per * (hi - lo)


def build(nc, hT_in, cvec, wmod, w8, w4, vecs, gains, rope, ident_in, stack_in, outT):
    with ExitStack() as ctx:
        def sem(name):
            return ctx.enter_context(nc.semaphore(name))

        base = [(nc.sbuf_base + 31) // 32 * 32]

        def region(nbytes):
            at = base[0]
            base[0] = at + (nbytes + 31) // 32 * 32
            return at

        def at(name, shape, dt, offset):
            return nc.alloc_sbuf_tensor_at(name, shape, dt, offset=offset)

        rU = region(2 * KD * TALL * 4)
        rY = region(2 * KW * TALL * 4)
        rX = region(41984)
        rE = region(6 * EW * 4)
        rW = region(6 * D * 4)
        rC = region(0)
        Uh = at("Uh", [P, KD, TALL], F32R, rU)
        Ul = at("Ul", [P, KD, TALL], F32R, rU + KD * TALL * 4)
        Yh = at("Yh", [P, KW, TALL], F32R, rY)
        Yl = at("Yl", [P, KW, TALL], F32R, rY + KW * TALL * 4)
        Pr = at("Pr", [P, 2, 4, TALL], F32, rY)
        Z = at("Z", [P, KD, TALL], F32, rY)
        B5 = TALL * 4
        raw = [at(f"raw{i}", [P, TALL], F32, rY + (6 + i) * B5) for i in range(2)]
        fc = [at(f"fc{i}", [P, TALL], F32, rY + i * B5) for i in range(2)]
        sq = at("sq", [P, TALL], F32, rY + 2 * B5)
        qn = at("qn", [P, TALL], F32, rY + 3 * B5)
        qa = at("qa", [P, TALL], F32, rY + 4 * B5)
        qb = at("qb", [P, TALL], F32, rY + 5 * B5)
        modrow = [at("modrow0", [2, 3 * D], F32, rY), at("modrow1", [2, 3 * D], F32, rU + 5 * 12288)]
        qo = at("qo", [P, NTOK, W3], F32, rX)
        cosT = at("cosT", [P, TALL], F32, rX)
        sinT = at("sinT", [P, TALL], F32, rX + B5)
        kT = at("kT", [P, NKV, TALL], F32R, rX + 20480)
        Vt = at("Vt", [P, NTOK, NKV, P], F32R, rX + 30720)
        hc = at("hc", [P, KW, HCW], F32, rX)
        cv = at("cv", [P, KW, TALL], F32, rX + 21248)
        X = at("X", [P, KD, TALL], F32, rX)
        wmA = [at(f"wmA{i}", [P, 2 * D], F32, rU + i * 8192) for i in range(KD)]
        wmB = [at(f"wmB{i}", [P, D], F32, rX + i * 4096) for i in range(KD)]
        wmL = [at(f"wmL{i}", [P, 3 * D], F32, (rX + i * 12288) if i < 3 else rU + (i - 3) * 12288)
               for i in range(KD)]
        e = [at(f"e{i}", [P, EW], F32, rE + i * EW * 4) for i in range(6)]
        kd = at("kd", [P, NTOK, NKV, 2, HD], F32, rE + 2 * EW * 4)
        qTh = [at(f"qTh{i}", [P, 512], F32R, rE + i * 2048) for i in range(2)]
        qTl = [at(f"qTl{i}", [P, 512], F32R, rE + 4096 + i * 2048) for i in range(2)]
        qd = [at(f"qd{i}", [P, 4, 2, HD], F32, rE + 8192 + i * 2048) for i in range(2)]
        ob = at("ob", [P, 512], F32, rE + 12288)
        PTh = [at(f"PTh{i}", [P, 512], F32R, rE + 14336 + i * 2048) for i in range(2)]
        PTl = [at(f"PTl{i}", [P, 512], F32R, rE + 18432 + i * 2048) for i in range(2)]
        wraw = [at(f"wraw{i}", [P, D], F32, rW + i * 4096) for i in range(2)]
        wh = [at(f"wh{i}", [P, D], F32R, rW + 8192 + i * 4096) for i in range(2)]
        wl = [at(f"wl{i}", [P, D], F32R, rW + 16384 + i * 4096) for i in range(2)]
        cpos = [rC]

        def small(name, shape):
            n = 4
            for s in shape[1:]:
                n *= s
            o = cpos[0]
            cpos[0] = o + (n + 31) // 32 * 32
            return at(name, shape, F32, o)

        ident = small("ident", [P, P])
        stackI = small("stackI", [P, HD])
        ones = small("ones", [P, P])
        vec = small("vec", [P, DEPTH, NV])
        gain = small("gain", [P, 4, P])
        craw = small("craw", [P, KD, 2])
        csilu = small("csilu", [P, KD, 2])
        mod = small("mod", [P, DEPTH, 3 * KD, 2])
        ss = small("ss", [P, 2 * NTOK])
        ms = small("ms", [P, 2 * NTOK])
        rstd = small("rstd", [P, 2 * NTOK])
        mhalf = small("mhalf", [P, 2 * NTOK])
        mx = small("mx", [P, 8])
        nm = small("nm", [P, 8])
        eps = small("eps", [P, 1])
        rs = small("rs", [P, 2, 2, 4])
        rsum = small("rsum", [P, 4])
        ri = small("ri", [P, NKV, 4])
        assert cpos[0] <= nc.sbuf_usable_end, (cpos[0], nc.sbuf_usable_end)

        PS = ctx.enter_context(nc.psum_tensor("PS", [P, 4096], F32))
        hT1 = nc.dram_tensor("hT1", [KD, P, TALL], F32, kind="Internal").ap()
        accd = nc.dram_tensor("accd", [2, KD, P, TALL], F32, kind="Internal").ap()

        def tbank(f, n):
            return PS[:, TB[f % 2]:TB[f % 2] + n]

        def slot(par, T):
            return PS[:, SLOT[par]:SLOT[par] + T]

        s_c = sem("s_consts")
        s_wm = [sem(f"s_wmod{i}") for i in range(KD)]
        s_wmb = sem("s_wmod_gate")
        s_wmu = sem("s_wmod_used")
        s_csilu = sem("s_csilu")
        s_modmm = sem("s_mod_product")
        s_modrow = sem("s_mod_row")
        s_modtr = sem("s_mod_transposed")
        s_mod = sem("s_mod_ready")
        s_ones = sem("s_ones")
        wland = [sem(f"w_landed{i}") for i in range(2)]
        whi = [sem(f"w_hi{i}") for i in range(2)]
        wsplit = [sem(f"w_split{i}") for i in range(2)]
        mm = [sem(f"mm_done{i}") for i in range(2)]
        sfree = [sem(f"slot_free{i}") for i in range(2)]
        t_done = sem("piece_done")
        t_free = sem("piece_read")
        s_rawfree = sem("raw_free")
        s_oraw = sem("o_transposed")
        s_mean = sem("ln_mean")
        s_tail = sem("exp_tail_done")
        s_hin = [sem(f"h_landed{i}") for i in range(2)]
        s_hused = sem("h_used")
        s_ufp = sem("u_written")
        s_u = sem("u_ready")
        s_rope = sem("s_rope")
        s_gain = sem("s_gain")
        s_tab = sem("rope_tables")
        s_fc = sem("feature_copy")
        s_sq = sem("squares")
        s_ms = sem("mean_square")
        s_rstd = sem("rstd")
        s_kd = sem("k_duplicated")
        s_vhi = sem("v_hi")
        s_khi = sem("k_hi")
        s_kv = sem("kv_ready")
        s_q = sem("q_ready")
        s_qd = sem("q_duplicated")
        pt_done = [sem(f"pt_done{i}") for i in range(2)]
        pt_hi = [sem(f"pt_hi{i}") for i in range(2)]
        pt_free = [sem(f"pt_free{i}") for i in range(2)]
        s_s = sem("scores")
        s_nm = sem("neg_max")
        s_exp = sem("exp_done")
        s_pv = sem("pv_done")
        s_o = sem("o_copied")
        s_oatt = sem("o_written")
        s_gate = sem("gate_written")
        s_yf = sem("y_float")
        s_yh = sem("y_hi")
        s_y = sem("y_ready")
        s_pad = sem("pads_zeroed")
        s_acc = sem("acc_ready")
        s_accin = sem("acc_landed")
        s_accst = sem("acc_stored")
        s_mgh = sem("merged_hi")
        s_mg = sem("merged_split")
        s_mgf = sem("merged_float")
        s_carry = sem("wait_carrier")
        s_mgd = sem("merge_done")
        s_lacc = sem("ln_square_added")
        s_csum = sem("ln_sum")
        s_dev = sem("ln_deviation")
        s_lsq = sem("ln_square")
        s_std = sem("ln_std")
        s_norm = sem("ln_normalised")
        s_hact = sem("conf_activated")
        s_scaled = sem("out_scaled")
        s_z = sem("z_ready")
        s_hn = sem("h_normalised")
        s_hst = sem("h_stored")
        s_outst = [sem(f"out_stored{i}") for i in range(2)]
        c_pe, c_act, c_dve, c_pool = sem("c_pe"), sem("c_act"), sem("c_dve"), sem("c_pool")

        TL = [TALL] + [LAT] * (DEPTH - 1)

        def jobs_qkv(l):
            return [TALL] + [TL[l]] * 4 + [TALL]

        def att_calls(l):
            out = [(0, LAT // P, 0, NTOK)]
            if TL[l] > LAT:
                out.append((LAT // P, CTX // P, LAT // P, CTX // P))
            return out

        def att_base(l, call):
            units, pt = 0, [0, 0]
            for ll in range(DEPTH):
                for n, (t0, nt, k0, nk) in enumerate(att_calls(ll)):
                    if (ll, n) == (l, call):
                        return units, pt
                    U = 2 * nt
                    pt = [pt[0] + 1 + (nk // 2) * U, pt[1] - 1 + (nk // 2 + 2) * U]
                    units += U
            return units, pt

        block = ctx.enter_context(nc.Block())

        @block.sync
        def _(sp):
            sp.dma_start(craw[:], cvec).then_inc(s_c, 16)
            sp.dma_start(ident[:], ident_in).then_inc(s_c, 16)
            sp.dma_start(stackI[:], stack_in).then_inc(s_c, 16)
            sp.dma_start(vec[:], vecs).then_inc(s_c, 16)
            for k in range(KD):
                sp.dma_start(wmA[k][:], wmod[0, k][:, :2 * D]).then_inc(s_wm[k], 16)

            def load(nh, par, src, width):
                if not isinstance(nh, int) or nh > 0:
                    sp.wait_ge(wsplit[par], nh)
                sp.dma_start(wraw[par][:, :width], src).then_inc(wland[par], 16)

            def load_merge(l, jb, w8b, w4b):
                with sp.Fori(0, 2) as i:
                    for j in range(4):
                        load(i * 4 + (jb // 2 + j), 0, w8[l, i * 4 + (w8b + j)], D)
                        load(i * 4 + (jb // 2 + j), 1, w4[l, i * 4 + (w4b + j)], W3)

            for l in range(DEPTH):
                jl = l * NJ
                if l == 0:
                    for j in range(KD):
                        if j == 2:
                            for n in range(2):
                                load(n // 2, n % 2, w8[l, W8_QKV + n], D)
                            for k in range(KD):
                                sp.dma_start(wmB[k][:], wmod[0, k][:, 2 * D:]).then_inc(s_wmb, 16)
                        if j >= 2:
                            sp.wait_ge(s_hused, j - 1)
                        sp.dma_start(e[2 + j % 2][:, :TALL], hT_in[j]).then_inc(s_hin[j % 2], 16)
                    sp.wait_ge(s_wmu, 2 * KD)
                sp.wait_ge(s_u, KD * (l + 1))
                if l > 0:
                    sp.wait_ge(s_hst, 16 * KD)
                sp.dma_start(cosT[:], rope[0]).then_inc(s_rope, 16)
                sp.dma_start(sinT[:], rope[1]).then_inc(s_rope, 16)
                sp.dma_start(gain[:], gains[l]).then_inc(s_gain, 16)
                for n in range(2, 6):
                    load((jl + n) // 2, n % 2, w8[l, W8_QKV + n], D)
                for n in range(4):
                    load((jl + J_ZA + n) // 2, n % 2, w8[l, W8_ZA + n], D)
                with sp.Fori(0, 4) as i:
                    for c in range(2):
                        load(i + (jl + J_CONF) // 2, c, w8[l, i * 2 + (W8_CONF + c)], D)
                load_merge(l, jl + J_MA, W8_GA, 0)
                with sp.Fori(0, 4) as i:
                    for c in range(4):
                        load(i * 2 + ((jl + J_SHORT) // 2 + c // 2), c % 2, w8[l, i * 4 + (W8_SHORT + c)], D)
                load_merge(l, jl + J_MB, W8_GB, KD)
                for n in range(4):
                    load((jl + J_ZC + n) // 2, n % 2, w8[l, W8_ZC + n], D)
                load_merge(l, jl + J_MC, W8_GC, 2 * KD)
                T = TL[l]
                src = hT_in if l == 0 else hT1
                for j in range(KD):
                    if j == 2:
                        sp.wait_ge(s_mgf, KD * (l + 1))
                    load((jl + J_OUT + j) // 2, j % 2, w8[l, W8_OUT + j], D)
                    if j >= 2:
                        sp.wait_ge(s_z, KD * l + j - 1)
                    if j == 4 and l + 1 < DEPTH:
                        sp.wait_ge(s_mg, KD * (l + 1))
                        for k in range(3):
                            sp.dma_start(wmL[k][:], wmod[l + 1, k]).then_inc(s_wm[k], 16)
                    sp.dma_start(e[2 + j % 2][:, :T], src[j][:, :T]).then_inc(s_hin[j % 2], 16)
                if l + 1 < DEPTH:
                    for n in range(2):
                        load((jl + NJ + n) // 2, n % 2, w8[l + 1, W8_QKV + n], D)
                    sp.wait_ge(mm[1], (jl + NJ) // 2)
                    for k in range(3, KD):
                        sp.dma_start(wmL[k][:], wmod[l + 1, k]).then_inc(s_wm[k], 16)
                    for j in range(KD):
                        sp.wait_ge(s_hn, j + 1)
                        sp.dma_start(hT1[j], X[:, j, :]).then_inc(s_hst, 16)
                else:
                    for j in range(KD):
                        sp.wait_ge(s_hn, KD * (DEPTH - 1) + j + 1)
                        sp.dma_start(outT[j], e[j % 2][:, :LAT]).then_inc(s_outst[j % 2], 16)
                    for p in range(2):
                        sp.wait_ge(s_outst[p], 16 * (KD // 2))
            sp.wait_ge(s_accst, 16 * 2 * KD * DEPTH)

        @block.gpsimd
        def _(pool):
            st = Steps(pool, c_pool)

            def split(nh, par, width):
                pool.wait_ge(wland[par], nh * 16 + 16)
                if not isinstance(nh, int) or nh > 0:
                    pool.wait_ge(mm[par], nh)
                if not isinstance(nh, int):
                    pool.sem_inc(s_carry, 1)
                nc.gpsimd.tensor_copy(wh[par][:, :width], wraw[par][:, :width]).then_inc(whi[par], 1)
                pool.wait_ge(whi[par], nh + 1)
                nc.gpsimd.tensor_tensor(wl[par][:, :width], wraw[par][:, :width],
                                        wh[par][:, :width].bitcast(F32), ALU.subtract).then_inc(wsplit[par], 1)

            def split_merge(jb):
                with pool.Fori(0, 2) as i:
                    for j in range(4):
                        split(i * 4 + (jb // 2 + j), 0, D)
                        split(i * 4 + (jb // 2 + j), 1, W3)

            nc.gpsimd.memset(ones[:], 1.0 / D).then_inc(s_ones, 1)
            nc.gpsimd.memset(mhalf[:], -0.5).then_inc(s_ones, 1)
            nc.gpsimd.memset(eps[:], LN_EPS).then_inc(s_ones, 1)
            pool.wait_ge(s_ones, 3)
            for l in range(DEPTH):
                jl = l * NJ
                T = TL[l]
                for n in range(2):
                    split((jl + n) // 2, n % 2, D)
                pool.wait_ge(s_rope, 32 * (l + 1))
                pool.wait_ge(s_gain, 16 * (l + 1))
                pool.wait_ge(s_u, KD * (l + 1))
                for g, (dst, tab) in enumerate([(e[0], cosT), (e[1], sinT), (e[4], cosT), (e[5], sinT)]):
                    nc.gpsimd.tensor_tensor(
                        dst[:, :TALL].rearrange("p (t c) -> p t c", c=P),
                        tab[:].rearrange("p (t c) -> p t c", c=P),
                        gain[:, g:g + 1, :].broadcast_to([P, NTOK, P]), ALU.mult).then_inc(s_tab, 1)

                def rms(n):
                    pool.wait_ge(s_ms, l * 5 + n + 1)
                    nc.gpsimd.tensor_tensor(rstd[:], ms[:], mhalf[:], ALU.pow).then_inc(s_rstd, 1)

                split((jl + 2) // 2, 0, D)
                split((jl + 2) // 2, 1, D)
                for n in range(4):
                    rms(n)
                    split((jl + 4 + n) // 2, n % 2, D)
                rms(4)
                pool.wait_ge(s_q, 4 * (l + 1))
                pool.wait_ge(s_kv, 3 * (l + 1))
                for n, (t0, nt, k0, nk) in enumerate(att_calls(l)):
                    ub, _ = att_base(l, n)

                    def dup(t, g):
                        pool.sem_inc(s_carry, 1)
                        nc.gpsimd.tensor_copy(
                            qd[g][:],
                            qo[:, t, g * 4 * HD:(g + 1) * 4 * HD].rearrange("p (h u d) -> p h u d", h=4, u=1)
                            .broadcast_to([P, 4, 2, HD])).then_inc(s_qd, 1)

                    if n > 0:
                        pool.wait_ge(s_s, 4 * ub)
                    for g in range(NKV):
                        dup(t0, g)
                    with pool.Fori(0, nt - 1) as i:
                        for g in range(NKV):
                            pool.wait_ge(s_s, i * 8 + (4 * (ub + g) + 4))
                            dup(i + (t0 + 1), g)
                for n in range(2, 4):
                    split((jl + J_ZA + n) // 2, n % 2, D)
                pool.wait_ge(t_done, pieces(l, O_OT + 3)[-1][0] + 1)
                for c0, n, who in segs(T):
                    nc.gpsimd.memset(hc[:, :, CPAD * who + c0:CPAD * (who + 1) + c0], 0.0).then_inc(s_pad, 1)
                nc.gpsimd.memset(hc[:, :, CPAD * (who + 1) + c0 + n:CPAD * (who + 2) + c0 + n],
                                 0.0).then_inc(s_pad, 1)
                with pool.Fori(0, 4) as i:
                    for c in range(2):
                        split(i + (jl + J_CONF) // 2, c, D)
                split_merge(jl + J_MA)
                with pool.Fori(0, 4) as i:
                    for c in range(4):
                        split(i * 2 + ((jl + J_SHORT) // 2 + c // 2), c % 2, D)
                split_merge(jl + J_MB)
                for n in range(4):
                    split((jl + J_ZC + n) // 2, n % 2, D)
                split_merge(jl + J_MC)
                for n in range(KD):
                    split((jl + J_OUT + n) // 2, n % 2, D)

        @block.tensor
        def _(pe):
            mmul = nc.tensor.matmul

            def job(nh, par, K, T, hi, lo, before_k=None):
                pe.wait_ge(wsplit[par], nh + 1)
                if not isinstance(nh, int) or nh > 0:
                    pe.wait_ge(sfree[par], nh)
                for k in range(K):
                    if before_k is not None:
                        before_k(k)
                    for a, w, x in ((0, wh, hi), (1, wh, lo), (2, wl, hi)):
                        for c, n in chunks(T):
                            last = mmul(PS[:, SLOT[par] + c:SLOT[par] + c + n], w[par][:, k * P:(k + 1) * P],
                                        x[:, k, c:c + n], start=(k == 0 and a == 0), stop=(k == K - 1 and a == 2))
                last.then_inc(mm[par], 1)

            def piece_wait(f):
                if f >= 2:
                    pe.wait_ge(t_free, f - 1)

            def transposes(l, op, srcs):
                for f, c, n in pieces(l, op):
                    piece_wait(f)
                    for t in range(n // P):
                        last = nc.tensor.transpose(tbank(f, n)[:, t * P:(t + 1) * P], srcs[c // P + t], ident[:])
                    last.then_inc(t_done, 1)

            def stat(l, op, src):
                for f, c, n in pieces(l, op):
                    piece_wait(f)
                    mmul(tbank(f, n), ones[:], src[:, c:c + n], start=True, stop=True).then_inc(t_done, 1)

            def mod_rows(k, w, col0, ncol, landed, n):
                pe.wait_ge(landed, n)
                for n in range(ncol // 512):
                    last = mmul(PS[0:2, col0 + n * 512:col0 + (n + 1) * 512], csilu[:, k, :],
                                w[k][:, n * 512:(n + 1) * 512], start=(k == 0), stop=(k == KD - 1))
                last.then_inc(s_wmu, 1)

            def mod_cols(l, first, n, at_col, turn):
                pe.wait_ge(s_modrow, turn)
                for m in range(first, first + n):
                    last = nc.tensor.transpose(PS[:, at_col + 2 * m:at_col + 2 * m + 2],
                                               modrow[l][0:2, m * P:(m + 1) * P], ident[0:2, 0:2])
                last.then_inc(s_modtr, 1)

            pe.wait_ge(s_csilu, 1)
            for k in range(KD):
                mod_rows(k, wmA, 0, 2 * D, s_wm[k], 16)
            mod_cols(0, 0, 2 * KD, 3072, 1)
            for k in range(KD):
                mod_rows(k, wmB, 2 * D, D, s_wmb, 16 * KD)

            for l in range(DEPTH):
                jl = l * NJ
                T = TL[l]
                tok = T // P

                def qkv_job(n):
                    job((jl + n) // 2, n % 2, KD, jobs_qkv(l)[n], Uh, Ul,
                        (lambda k: pe.wait_ge(s_u, KD * l + k + 1)) if n == 0 else None)

                def to_tokens(f, n):
                    pe.wait_ge(s_fc, 6 * l + n + 1)
                    transposes(l, f, [fc[n % 2][:, t * P:(t + 1) * P] for t in range(jobs_qkv(l)[n] // P)])

                def to_keys(f, g):
                    pe.wait_ge(s_kd, l + 1)
                    transposes(l, f, [kd[:, t, g].rearrange("p a d -> p (a d)") for t in range(NTOK)])

                qkv_job(0)
                if l == 0:
                    pe.wait_ge(s_mod, 1)
                    mod_cols(0, 2 * KD, KD, 3072, 2)
                    pe.wait_ge(s_mod, 2)
                qkv_job(1)
                to_tokens(O_K, 0)
                qkv_job(2)
                to_tokens(O_Q0, 1)
                qkv_job(3)
                to_tokens(O_Q1, 2)
                to_keys(O_KT0, 0)
                to_keys(O_KT1, 1)
                qkv_job(4)
                to_tokens(O_Q2, 3)
                qkv_job(5)
                to_tokens(O_Q3, 4)
                to_tokens(O_V, 5)

                for p in range(2):
                    pe.wait_ge(sfree[p], (jl + J_ZA) // 2)
                pe.wait_ge(t_free, pieces(l, O_V)[-1][0] + 1)
                pe.wait_ge(s_kv, 3 * (l + 1))
                for call, (t0, nt, k0, nk) in enumerate(att_calls(l)):
                    ub, ptb = att_base(l, call)
                    p0, p1 = nk // 2, nk // 2 + 2

                    def q_fill(un, g, par, idx):
                        pe.wait_ge(s_qd, un + (ub + 1))
                        if not isinstance(idx, int) or idx > 0:
                            pe.wait_ge(pt_free[par], idx)
                        for h in range(4):
                            last = nc.tensor.transpose(PS[:, PT0[par] + h * P:PT0[par] + (h + 1) * P],
                                                       qd[g][:, h].rearrange("p a d -> p (a d)"), ident[:])
                        last.then_inc(pt_done[par], 1)

                    def scores(un, g, h, part):
                        first = isinstance(un, int) and ub + un == 0
                        own, tail = score_parts(h, nk)
                        if part == 0 and not own:
                            return
                        if (part == 0 or not own) and not (first and h < 2):
                            pe.wait_ge(s_exp, un * 4 + (4 * ub + h - 1))
                        if part == 1 and not (first and h == 0):
                            pe.wait_ge(s_tail, un * 4 + (4 * ub + h))
                        s0 = (h % 2) * TALL
                        for c, n in (own, tail)[part]:
                            for a, x in enumerate((qTh, qTl)):
                                last = mmul(PS[:, s0 + c:s0 + c + n], x[g][:, h * P:(h + 1) * P],
                                            kT[:, g, k0 * P + c:k0 * P + c + n], start=(a == 0), stop=(a == 1))
                        if part == 1:
                            last.then_inc(s_s, 1)

                    def pv(un, g, kt, n):
                        par = kt % 2
                        pe.wait_ge(pt_free[par], n + 1)
                        if kt == 0 and (not isinstance(un, int) or un + ub > 0):
                            pe.wait_ge(s_o, un + ub)
                        for a, x in enumerate((PTh, PTl)):
                            last = mmul(PS[:, O0:O0 + 512], Vt[:, k0 + kt, g, :], x[par][:],
                                        start=(kt == 0 and a == 0), stop=(kt == nk - 1 and a == 1))
                        if kt == nk - 1:
                            last.then_inc(s_pv, 1)

                    def back(un, i):
                        pe.wait_ge(s_o, un + (ub + 1))
                        pe.wait_ge(pt_free[1], i)
                        for h in range(4):
                            last = mmul(PS[:, PT0[1] + h * HD:PT0[1] + (h + 1) * HD], ob[:, h * P:(h + 1) * P],
                                        stackI[:], start=True, stop=True)
                        last.then_inc(pt_done[1], 1)

                    def unit(un, g, i0, i1, prev, nxt, nxt2):
                        for kt in range(nk):
                            par = kt % 2
                            if kt == 0:
                                pe.wait_ge(s_exp, un * 4 + (4 * ub + 4))
                            pe.wait_ge(pt_free[par], fill(nk, kt, i0, i1, prev, nxt2))
                            for h in range(4):
                                last = nc.tensor.transpose(PS[:, PT0[par] + h * P:PT0[par] + (h + 1) * P],
                                                           Pr[:, g, h, kt * P:(kt + 1) * P], ident[:])
                            last.then_inc(pt_done[par], 1)
                            if kt == back_after(nk) and prev:
                                back(un - 1, i1 - 1 + kt // 2)
                            for a, h in heads_at(nk, kt, nxt, nxt2):
                                for part in range(2):
                                    scores(un + a, (g + a) % 2, h, part)
                            if kt >= 1:
                                pv(un, g, kt - 1, fill(nk, kt - 1, i0, i1, prev, nxt2))
                            if nxt2 and kt == q_after(nk):
                                q_fill(un + 2, g, 1, i1 + (kt + 1) // 2)
                        pv(un, g, nk - 1, fill(nk, nk - 1, i0, i1, prev, nxt2))

                    q_fill(0, 0, 0, ptb[0])
                    q_fill(1, 1, 1, ptb[1])
                    pe.wait_ge(pt_free[0], ptb[0] + 1)
                    pe.wait_ge(pt_free[1], ptb[1] + 1)
                    for un, h in [(0, 0), (0, 1), (0, 2), (0, 3)] + ([(1, 0)] if nk > 2 else []):
                        for part in range(2):
                            scores(un, un, h, part)
                    for g in range(NKV):
                        unit(g, g, ptb[0] + 1 + g * p0, ptb[1] + 1 + g * p1, g > 0, True, True)
                    if nt > 2:
                        with pe.Fori(1, nt - 1) as i:
                            for g in range(NKV):
                                unit(i * 2 + g, g, i * (2 * p0) + (ptb[0] + 1 + g * p0),
                                     i * (2 * p1) + (ptb[1] + 1 + g * p1), True, True, True)
                    un = 2 * (nt - 1)
                    unit(un, 0, ptb[0] + 1 + un * p0, ptb[1] + 1 + un * p1, True, True, False)
                    unit(un + 1, 1, ptb[0] + 1 + (un + 1) * p0, ptb[1] + (un + 1) * p1, True, False, False)
                    back(un + 1, ptb[1] - 2 + (un + 2) * p1)

                pe.wait_ge(s_oatt, sum(2 * c[1] for ll in range(l + 1) for c in att_calls(ll)))
                for i in range(KW):
                    job((jl + J_ZA + i) // 2, i % 2, KD, T, Uh, Ul)
                    transposes(l, O_OT + i, [qo[:, t, i * P:(i + 1) * P] for t in range(tok)])
                with pe.Fori(0, 4) as i:
                    for c in range(2):
                        job(i + (jl + J_CONF) // 2, c, KD, T, Uh, Ul)

                def merge_jobs(jb, y):
                    with pe.Fori(0, 2) as i:
                        for j in range(4):
                            job(i * 4 + (jb // 2 + j), 0, KD, T, Uh, Ul)
                            pe.wait_ge(s_y, y)
                            job(i * 4 + (jb // 2 + j), 1, KW, T, Yh, Yl)

                merge_jobs(jl + J_MA, 12 * l + 4)
                with pe.Fori(0, 4) as i:
                    for c in range(4):
                        job(i * 2 + ((jl + J_SHORT) // 2 + c // 2), c % 2, KD, T, Uh, Ul)
                merge_jobs(jl + J_MB, 12 * l + 8)
                def zc_job(n):
                    job((jl + J_ZC + n) // 2, n % 2, KD, T, Uh, Ul)

                zc_job(0)
                pe.wait_ge(s_csum, 4 * l + 1)
                stat(l, O_CMEAN, e[4])
                zc_job(1)
                pe.wait_ge(s_csum, 4 * l + 2)
                stat(l, O_CVAR, e[5])
                zc_job(2)
                zc_job(3)
                merge_jobs(jl + J_MC, 12 * l + 12)
                for j in range(KD):
                    job((jl + J_OUT + j) // 2, j % 2, KD, T, Uh, Ul,
                        (lambda k: pe.wait_ge(s_mg, KD * l + k + 1)) if j == 0 else None)
                nxt = l + 1 < DEPTH
                if nxt:
                    for p in range(2):
                        pe.wait_ge(sfree[p], (jl + NJ) // 2)
                    mod_rows(0, wmL, 0, 3 * D, s_wm[0], 32)
                pe.wait_ge(s_csum, 4 * l + 3)
                stat(l, O_OMEAN, e[4])
                if nxt:
                    for k in range(1, 5):
                        mod_rows(k, wmL, 0, 3 * D, s_wm[k], 32)
                pe.wait_ge(s_csum, 4 * l + 4)
                stat(l, O_OVAR, e[5])
                if nxt:
                    for k in range(5, KD):
                        mod_rows(k, wmL, 0, 3 * D, s_wm[k], 32)
                    mod_cols(l + 1, 0, 3 * KD, 0, 3)

        @block.scalar
        def _(act):
            st = Steps(act, c_act)
            fn = nc.scalar.activation

            act.wait_ge(s_c, 64)
            fn(csilu[:], craw[:], ACT.Silu).then_inc(s_csilu, 1)

            def modulate(l, j, src, first_use):
                b = KD * l + j
                if first_use is not None:
                    act.wait_ge(s_u, first_use)
                for c0, n, who in segs(TALL):
                    last = fn(e[j % 2][:, c0:c0 + n], src[:, c0:c0 + n], ACT.Identity,
                              scale=mod[:, l, KD + j, who:who + 1], bias=mod[:, l, j, who:who + 1])
                st.done(last)
                fn(Uh[:, j, :], e[j % 2][:, :TALL], ACT.Copy).then_inc(s_ufp, 1)

            act.wait_ge(s_mod, 1)
            for j in range(KD):
                act.wait_ge(s_hin[j % 2], 16 * (j // 2 + 1))
                if j >= 2:
                    act.wait_ge(s_u, j - 1)
                for c0, n, who in segs(TALL):
                    last = fn(e[j % 2][:, c0:c0 + n], e[2 + j % 2][:, c0:c0 + n], ACT.Identity,
                              scale=mod[:, 0, KD + j, who:who + 1], bias=mod[:, 0, j, who:who + 1])
                last.then_inc(s_hused, 1)
                act.wait_ge(s_hused, j + 1)
                fn(Uh[:, j, :], e[j % 2][:, :TALL], ACT.Copy).then_inc(s_ufp, 1)

            for l in range(DEPTH):
                jl = l * NJ
                T = TL[l]
                gb = 40 * l

                def evac(n):
                    act.wait_ge(mm[n % 2], (jl + n) // 2 + 1)
                    if n >= 2:
                        act.wait_ge(t_done, pieces(l, QKV_OPS[n - 2])[-1][0] + 1)
                    Tn = jobs_qkv(l)[n]
                    fn(fc[n % 2][:, :Tn], slot(n % 2, Tn), ACT.Copy).then_inc(sfree[n % 2], 1)
                    act.wait_ge(sfree[n % 2], (jl + n) // 2 + 1)
                    act.sem_inc(s_fc, 1)

                def copy_pieces(op, dst, scale=1.0):
                    for f, c, n in pieces(l, op):
                        act.wait_ge(t_done, f + 1)
                        fn(dst[:, c:c + n], tbank(f, n), ACT.Copy, scale=scale).then_inc(t_free, 1)
                    act.wait_ge(t_free, f + 1)

                def copy_raw(op):
                    if 8 * l + op >= 2:
                        act.wait_ge(s_rawfree, 8 * l + op - 1)
                    copy_pieces(op, raw[op % 2])
                    return raw[op % 2]

                def square(op):
                    Tn = op_width(l, op)
                    x = copy_raw(op)
                    if op != O_K:
                        act.wait_ge(s_ms, 5 * l + [O_K, O_Q0, O_Q1, O_Q2, O_Q3].index(op))
                    fn(sq[:, :Tn], x[:, :Tn], ACT.Square).then_inc(s_sq, 1)

                def k_hi(op, g):
                    x = copy_raw(op)
                    fn(kT[:, g, :], x[:], ACT.Copy).then_inc(s_khi, 1)

                evac(0)
                evac(1)
                square(O_K)
                evac(2)
                square(O_Q0)
                evac(3)
                square(O_Q1)
                if l > 0:
                    act.wait_ge(s_hst, 16 * KD)
                k_hi(O_KT0, 0)
                k_hi(O_KT1, 1)
                evac(4)
                square(O_Q2)
                evac(5)
                square(O_Q3)
                x = copy_raw(O_V)
                fn(Vt[:, :, :, 0:HD], x[:].rearrange("p (t g d) -> p t g d", g=NKV, d=HD),
                   ACT.Copy).then_inc(s_vhi, 1)

                act.wait_ge(s_q, 4 * (l + 1))
                act.wait_ge(s_kv, 3 * (l + 1))
                for call, (t0, nt, k0, nk) in enumerate(att_calls(l)):
                    ub, ptb = att_base(l, call)
                    p0, p1 = nk // 2, nk // 2 + 2

                    def q_hi(g, par, idx):
                        act.wait_ge(pt_done[par], idx + 1)
                        fn(qTh[g][:], PS[:, PT0[par]:PT0[par] + 512], ACT.Copy).then_inc(pt_hi[par], 1)

                    def exps(un, g, h):
                        act.wait_ge(s_nm, un * 4 + (4 * ub + h + 1))
                        s0 = (h % 2) * TALL
                        main, tail = score_parts(h, nk)
                        m = 4 * g + h
                        (c, n), = tail
                        fn(Pr[:, g, h, c:c + n], PS[:, s0 + c:s0 + c + n], ACT.Exp, bias=nm[:, m:m + 1],
                           scale=HD ** -0.5, accum_out=rs[:, g, 0, h:h + 1]).then_inc(s_tail, 1)
                        if main:
                            c = main[0][0]
                            fn(Pr[:, g, h, c:c + 1024], PS[:, s0 + c:s0 + c + 1024], ACT.Exp, bias=nm[:, m:m + 1],
                               scale=HD ** -0.5, accum_out=rs[:, g, 1, h:h + 1]).then_inc(s_exp, 1)
                        else:
                            act.wait_ge(s_tail, un * 4 + (4 * ub + h + 1))
                            act.sem_inc(s_exp, 1)

                    def o_copy(un):
                        act.wait_ge(s_pv, un + (ub + 1))
                        fn(ob[:], PS[:, O0:O0 + 512], ACT.Copy).then_inc(s_o, 1)

                    def unit(un, g, i0, i1, prev, nxt, nxt2):
                        for kt in range(nk):
                            par = kt % 2
                            if kt == 0 and prev:
                                o_copy(un - 1)
                            act.wait_ge(pt_done[par], fill(nk, kt, i0, i1, prev, nxt2) + 1)
                            fn(PTh[par][:], PS[:, PT0[par]:PT0[par] + 512], ACT.Copy).then_inc(pt_hi[par], 1)
                            for h in exps_at(nk, kt, nxt):
                                exps(un + 1, 1 - g, h)
                            if nxt2 and kt == q_after(nk):
                                q_hi(g, 1, i1 + (kt + 1) // 2)

                    q_hi(0, 0, ptb[0])
                    q_hi(1, 1, ptb[1])
                    for h in range(4):
                        exps(0, 0, h)
                    for g in range(NKV):
                        unit(g, g, ptb[0] + 1 + g * p0, ptb[1] + 1 + g * p1, g > 0, True, True)
                    if nt > 2:
                        with act.Fori(1, nt - 1) as i:
                            for g in range(NKV):
                                unit(i * 2 + g, g, i * (2 * p0) + (ptb[0] + 1 + g * p0),
                                     i * (2 * p1) + (ptb[1] + 1 + g * p1), True, True, True)
                    un = 2 * (nt - 1)
                    unit(un, 0, ptb[0] + 1 + un * p0, ptb[1] + 1 + un * p1, True, True, False)
                    unit(un + 1, 1, ptb[0] + 1 + (un + 1) * p0, ptb[1] + (un + 1) * p1, True, False, False)
                    o_copy(un + 1)

                act.wait_ge(s_oatt, sum(2 * c[1] for ll in range(l + 1) for c in att_calls(ll)))
                for i in range(KW):
                    act.wait_ge(mm[i % 2], (jl + J_ZA + i) // 2 + 1)
                    if i >= 2:
                        act.wait_ge(s_yf, 12 * l + i - 1)
                    fn(e[i % 2][:, :T], slot(i % 2, T), ACT.Silu).then_inc(sfree[i % 2], 1)
                    if i >= 2:
                        act.wait_ge(s_yf, 12 * l + i - 1)
                    copy_pieces(O_OT + i, e[4 + i % 2])
                    act.sem_inc(s_oraw, 1)
                    act.wait_ge(s_yf, 12 * l + i + 1)
                    fn(Yh[:, i, :T], e[2 + i % 2][:, :T], ACT.Copy).then_inc(s_yh, 1)

                with act.Fori(0, 4) as i:
                    act.wait_ge(mm[0], i + ((jl + J_CONF) // 2 + 1))
                    act.wait_ge(sfree[1], i + (jl + J_CONF) // 2)
                    fn(e[0][:, :T], slot(0, T), ACT.Sigmoid).then_inc(sfree[0], 1)

                def merge(branch):
                    jb = jl + (J_MA, J_MB, J_MC)[branch]
                    yb = (3 * l + branch) * KD
                    ab = 2 * l * KD
                    with act.Fori(0, 2) as i:
                        for j in range(4):
                            act.wait_ge(sfree[1], i * 4 + (jb // 2 + j))
                            if branch > 0:
                                act.wait_ge(s_mgd, i * 4 + (yb + j))
                                act.dma_start(e[1][:, :T], accd[branch - 1, i * 4 + j][:, :T]).then_inc(s_accin, 16)
                            act.wait_ge(mm[0], i * 4 + (jb // 2 + j + 1))
                            fn(e[0][:, :T], slot(0, T), ACT.Sigmoid).then_inc(sfree[0], 1)
                            if branch < 2:
                                act.wait_ge(s_mgd, i * 4 + (yb + j + 1))
                                act.dma_start(accd[branch, i * 4 + j][:, :T], e[4 + j % 2][:, :T]).then_inc(s_accst, 16)
                                act.wait_ge(s_accst, i * 64 + 16 * (ab + branch * KD + j + 1))

                merge(0)

                with act.Fori(0, 4) as i:
                    hb = (jl + J_SHORT) // 2
                    act.wait_ge(mm[0], i * 2 + (hb + 1))
                    act.wait_ge(sfree[1], i * 2 + hb)
                    fn(e[0][:, :T], slot(0, T), ACT.Copy).then_inc(sfree[0], 1)
                    act.wait_ge(mm[0], i * 2 + (hb + 2))
                    act.wait_ge(sfree[1], i * 2 + (hb + 1))
                    act.wait_ge(s_yf, i + (12 * l + 4))
                    fn(e[4][:, :T], slot(0, T), ACT.Silu).then_inc(sfree[0], 1)
                    act.wait_ge(s_yf, i + (12 * l + 5))
                    act.sem_inc(s_carry, 1)
                    fn(Yh[:, i, :T], e[3][:, :T], ACT.Copy).then_inc(s_yh, 1)

                merge(1)

                def silu_z(n):
                    act.wait_ge(mm[n % 2], (jl + J_ZC + n) // 2 + 1)
                    fn(hc[:, n, :T], slot(n % 2, T), ACT.Silu).then_inc(sfree[n % 2], 1)

                def squares(first, srcs):
                    for n, s in enumerate(srcs):
                        act.wait_ge(s_dev, first + n + 1)
                        if n >= 2:
                            act.wait_ge(s_lacc, first + n - 1)
                        fn(e[n % 2][:, :T], s, ACT.Square).then_inc(s_lsq, 1)

                def mean(op, nt):
                    copy_pieces(op, e[4], float(KD) / nt)
                    act.sem_inc(s_mean, 1)

                def root(op, nt):
                    for f, c, n in pieces(l, op):
                        act.wait_ge(t_done, f + 1)
                        fn(e[4][:, c:c + n], tbank(f, n), ACT.Sqrt, scale=float(KD) / nt,
                           bias=eps[:]).then_inc(t_free, 1)
                    act.wait_ge(t_free, f + 1)
                    act.sem_inc(s_std, 1)

                act.wait_ge(s_csum, 4 * l + 1)
                silu_z(0)
                mean(O_CMEAN, KW)
                squares(12 * l, [cv[:, n, :T] for n in range(KW)])
                silu_z(1)
                root(O_CVAR, KW)
                silu_z(2)
                silu_z(3)
                for n in range(KW):
                    act.wait_ge(s_norm, 12 * l + n + 1)
                    if n >= 2:
                        act.wait_ge(s_yf, 12 * l + 8 + n - 1)
                    fn(e[n % 2][:, :T], cv[:, n, :T], ACT.Silu, scale=vec[:, l, V_CG + n:V_CG + n + 1],
                       bias=vec[:, l, V_CB + n:V_CB + n + 1]).then_inc(s_hact, 1)
                    act.wait_ge(s_yf, 12 * l + 8 + n + 1)
                    fn(Yh[:, n, :T], e[2 + n % 2][:, :T], ACT.Copy).then_inc(s_yh, 1)

                merge(2)

                act.wait_ge(mm[0], (jl + J_OUT) // 2)
                for j in range(KD):
                    act.wait_ge(s_mgf, KD * l + j + 1)
                    fn(Uh[:, j, :T], X[:, j, :T], ACT.Copy).then_inc(s_mgh, 1)

                act.wait_ge(s_mod, 2 + l)
                for j in range(KD):
                    act.wait_ge(mm[j % 2], (jl + J_OUT + j) // 2 + 1)
                    if j >= 2:
                        act.wait_ge(s_z, KD * l + j - 1)
                    for c0, n, who in segs(T):
                        last = fn(e[j % 2][:, c0:c0 + n], PS[:, SLOT[j % 2] + c0:SLOT[j % 2] + c0 + n], ACT.Copy,
                                  scale=mod[:, l, 2 * KD + j, who:who + 1])
                    last.then_inc(sfree[j % 2], 1)
                mean(O_OMEAN, KD)
                squares(12 * l + 4, [Z[:, n, :T] for n in range(KD)])
                root(O_OVAR, KD)
                for j in range(KD):
                    act.wait_ge(s_norm, 12 * l + 4 + j + 1)
                    if l + 1 < DEPTH:
                        if j == 0:
                            act.wait_ge(s_wmu, 2 * KD + 3)
                        fn(X[:, j, :T], Z[:, j, :T], ACT.Identity, scale=vec[:, l, V_PG + j:V_PG + j + 1],
                           bias=vec[:, l, V_PB + j:V_PB + j + 1]).then_inc(s_hn, 1)
                    else:
                        if j >= 2:
                            act.wait_ge(s_outst[j % 2], 16 * (j // 2))
                        fn(e[j % 2][:, :T], Z[:, j, :T], ACT.Identity, scale=vec[:, l, V_PG + j:V_PG + j + 1],
                           bias=vec[:, l, V_PB + j:V_PB + j + 1]).then_inc(s_hn, 1)
                if l + 1 < DEPTH:
                    act.wait_ge(s_hn, KD * (l + 1))
                    act.wait_ge(s_mod, 3)
                    for j in range(KD):
                        modulate(l + 1, j, X[:, j, :], KD * (l + 1) + j - 1 if j >= 2 else None)

        @block.vector
        def _(dve):
            st = Steps(dve, c_dve)
            tt, stt, ts = nc.vector.tensor_tensor, nc.vector.scalar_tensor_tensor, nc.vector.tensor_scalar

            def mod_row(l, c0, n, turn):
                dve.wait_ge(s_wmu, KD * turn)
                nc.vector.tensor_copy(modrow[l][:, c0:c0 + n], PS[0:2, c0:c0 + n]).then_inc(s_modrow, 1)

            def mod_col(l, first, n, at_col, turn):
                dve.wait_ge(s_modtr, turn)
                cols = PS[:, at_col + 2 * first:at_col + 2 * (first + n)].rearrange("p (n w) -> p n w", w=2)
                last = tt(mod[:, l, first:first + n], cols,
                          vec[:, l, V_BM + first:V_BM + first + n].rearrange("p (n w) -> p n w", w=1)
                          .broadcast_to([P, n, 2]), ALU.add)
                if first == 0:
                    st.done(last)
                    last = ts(mod[:, l, KD:2 * KD], mod[:, l, KD:2 * KD], 1.0, None, ALU.add)
                last.then_inc(s_mod, 1)

            mod_row(0, 0, 2 * D, 1)
            mod_col(0, 0, 2 * KD, 3072, 1)

            def u_lo(l, j):
                dve.wait_ge(s_ufp, KD * l + j + 1)
                tt(Ul[:, j, :], e[j % 2][:, :TALL], Uh[:, j, :].bitcast(F32), ALU.subtract).then_inc(s_u, 1)

            for j in range(KD):
                u_lo(0, j)
            mod_row(0, 2 * D, D, 2)
            mod_col(0, 2 * KD, KD, 3072, 2)

            for l in range(DEPTH):
                jl = l * NJ
                T = TL[l]

                def normed(op, n, Tn, A, B, dst):
                    H2 = 2 * Tn // P
                    dve.wait_ge(s_sq, 5 * l + n + 1)
                    st.done(nc.vector.reduce_sum(ss[:, :H2], sq[:, :Tn].rearrange("p (h d) -> p h d", d=HD), AX_X))
                    ts(ms[:, :H2], ss[:, :H2], 1.0 / HD, RMS_EPS, ALU.mult, ALU.add).then_inc(s_ms, 1)
                    dve.wait_ge(s_rstd, 5 * l + n + 1)
                    tt(qn[:, :Tn].rearrange("p (h d) -> p h d", d=HD),
                       raw[op % 2][:, :Tn].rearrange("p (h d) -> p h d", d=HD),
                       rstd[:, :H2].rearrange("p (h o) -> p h o", o=1).broadcast_to([P, H2, HD]),
                       ALU.mult).then_inc(s_rawfree, 1)
                    dve.wait_ge(s_rawfree, 8 * l + op + 1)
                    if n < 2:
                        dve.wait_ge(s_tab, 4 * l + 2 + 2 * n)
                    tt(qa[:, :Tn], qn[:, :Tn], A[:, :Tn], ALU.mult)

                    def pair(x, a):
                        return x[:, :Tn].rearrange("p (b a c) -> p b a c", a=2, c=HD // 4)[:, :, a, :]

                    tt(pair(qb, 0), pair(qn, 1), pair(B, 0), ALU.mult)
                    st.done(tt(pair(qb, 1), pair(qn, 0), pair(B, 1), ALU.mult))
                    return dst(Tn)

                def k_out(Tn):
                    for a in range(2):
                        last = tt(kd[:, :, :, a, :].rearrange("p t g d -> p (t g) d"),
                                  qa[:].rearrange("p (h d) -> p h d", d=HD),
                                  qb[:].rearrange("p (h d) -> p h d", d=HD), ALU.add)
                    last.then_inc(s_kd, 1)

                def q_out(i):
                    def f(Tn):
                        tt(qo[:, :Tn // P, i * P:(i + 1) * P], qa[:, :Tn].rearrange("p (t c) -> p t c", c=P),
                           qb[:, :Tn].rearrange("p (t c) -> p t c", c=P), ALU.add).then_inc(s_q, 1)
                    return f

                def k_lo(op, g):
                    dve.wait_ge(s_khi, 2 * l + g + 1)
                    st.done(tt(kT[HD:P, g, :], raw[op % 2][HD:P, :], kT[HD:P, g, :].bitcast(F32), ALU.subtract))
                    dve.sem_inc(s_rawfree, 1)
                    dve.sem_inc(s_kv, 1)

                normed(O_K, 0, TALL, e[0], e[1], k_out)
                normed(O_Q0, 1, T, e[4], e[5], q_out(0))
                normed(O_Q1, 2, T, e[4], e[5], q_out(1))
                k_lo(O_KT0, 0)
                k_lo(O_KT1, 1)
                normed(O_Q2, 3, T, e[4], e[5], q_out(2))
                normed(O_Q3, 4, T, e[4], e[5], q_out(3))
                dve.wait_ge(s_vhi, l + 1)
                st.done(tt(Vt[:, :, :, HD:P].rearrange("p t g d -> p (t g) d"),
                           raw[O_V % 2][:].rearrange("p (h d) -> p h d", d=HD),
                           Vt[:, :, :, 0:HD].rearrange("p t g d -> p (t g) d").bitcast(F32), ALU.subtract))
                dve.sem_inc(s_rawfree, 1)
                dve.sem_inc(s_kv, 1)

                for call, (t0, nt, k0, nk) in enumerate(att_calls(l)):
                    ub, ptb = att_base(l, call)
                    p0, p1, hi1 = nk // 2, nk // 2 + 2, nk // 2 + 1
                    hb = [ptb[0], ptb[1] - ub]

                    def q_lo(g, par, idx_hi):
                        dve.wait_ge(pt_hi[par], idx_hi + 1)
                        tt(qTl[g][:], PS[:, PT0[par]:PT0[par] + 512], qTh[g][:].bitcast(F32),
                           ALU.subtract).then_inc(pt_free[par], 1)

                    def maxes(un, g, h):
                        dve.wait_ge(s_s, un * 4 + (4 * ub + h + 1))
                        s0 = (h % 2) * TALL
                        m = 4 * g + h
                        st.done(nc.vector.reduce_max(mx[:, m:m + 1], PS[:, s0:s0 + nk * P], AX_X))
                        ts(nm[:, m:m + 1], mx[:, m:m + 1], -(HD ** -0.5), None, ALU.mult).then_inc(s_nm, 1)

                    def sums(un, g):
                        dve.wait_ge(s_exp, un * 4 + (4 * ub + 4))
                        if nk * P > 256:
                            st.done(tt(rsum[:], rs[:, g, 0, :], rs[:, g, 1, :], ALU.add))
                            st.done(nc.vector.reciprocal(ri[:, g], rsum[:]))
                        else:
                            st.done(nc.vector.reciprocal(ri[:, g], rs[:, g, 0, :]))

                    def back(t, g, i):
                        dve.wait_ge(pt_done[1], i)
                        st.done(tt(qo[:, t, g * 4 * HD:(g + 1) * 4 * HD].rearrange("p (h d) -> p h d", d=HD),
                                   PS[:, PT0[1]:PT0[1] + 4 * HD].rearrange("p (h d) -> p h d", d=HD),
                                   ri[:, g].rearrange("p (h o) -> p h o", o=1).broadcast_to([P, 4, HD]), ALU.mult))
                        dve.sem_inc(pt_free[1], 1)
                        dve.sem_inc(s_oatt, 1)

                    def unit(un, t, g, h0, h1, prev, nxt, nxt2):
                        for kt in range(nk):
                            par = kt % 2
                            dve.wait_ge(pt_hi[par], fill(nk, kt, h0, h1, False, nxt2) + 1)
                            tt(PTl[par][:], PS[:, PT0[par]:PT0[par] + 512], PTh[par][:].bitcast(F32),
                               ALU.subtract).then_inc(pt_free[par], 1)
                            if kt == back_after(nk) and prev:
                                back(t if g == 1 else t - 1, 1 - g, h1 + un + ub + kt // 2)
                            for a, h in heads_at(nk, kt, nxt, nxt2):
                                maxes(un + a, (g + a) % 2, h)
                            if nxt2 and kt == q_after(nk):
                                q_lo(g, 1, h1 + (kt + 1) // 2)
                            if nxt and kt == nk - 1:
                                sums(un + 1, 1 - g)

                    q_lo(0, 0, hb[0])
                    q_lo(1, 1, hb[1])
                    for un, h in [(0, 0), (0, 1), (0, 2), (0, 3)] + ([(1, 0)] if nk > 2 else []):
                        maxes(un, un, h)
                    sums(0, 0)
                    for g in range(NKV):
                        unit(g, t0, g, hb[0] + 1 + g * p0, hb[1] + 1 + g * hi1, g > 0, True, True)
                    if nt > 2:
                        with st.loop(1, nt - 1, 14) as i:
                            for g in range(NKV):
                                unit(i * 2 + g, i + t0, g, i * (2 * p0) + (hb[0] + 1 + g * p0),
                                     i * (2 * hi1) + (hb[1] + 1 + g * hi1), True, True, True)
                    un = 2 * (nt - 1)
                    unit(un, t0 + nt - 1, 0, hb[0] + 1 + un * p0, hb[1] + 1 + un * hi1, True, True, False)
                    unit(un + 1, t0 + nt - 1, 1, hb[0] + 1 + (un + 1) * p0, hb[1] + (un + 1) * hi1,
                         True, False, False)
                    back(t0 + nt - 1, 1, ptb[1] - 1 + (un + 2) * p1)

                for i in range(KW):
                    dve.wait_ge(sfree[i % 2], (jl + J_ZA + i) // 2 + 1)
                    dve.wait_ge(s_oraw, KW * l + i + 1)
                    tt(e[2 + i % 2][:, :T], e[4 + i % 2][:, :T], e[i % 2][:, :T], ALU.mult).then_inc(s_yf, 1)
                    dve.wait_ge(s_yh, 12 * l + i + 1)
                    tt(Yl[:, i, :T], e[2 + i % 2][:, :T], Yh[:, i, :T].bitcast(F32), ALU.subtract).then_inc(s_y, 1)

                dve.wait_ge(s_pad, sum(len(segs(t)) + 1 for t in TL[:l + 1]))
                hb = (jl + J_CONF) // 2
                wmid = V_WC + CPAD
                with st.loop(0, 4, 2) as i:
                    dve.wait_ge(mm[1], i + (hb + 1))
                    dve.wait_ge(sfree[0], i + (hb + 1))
                    for c0, n, who in segs(T):
                        last = tt(hc[:, i, CPAD * (1 + who) + c0:CPAD * (1 + who) + c0 + n],
                                  PS[:, SLOT[1] + c0:SLOT[1] + c0 + n], e[0][:, c0:c0 + n], ALU.mult)
                    st.done(last)
                    dve.sem_inc(sfree[1], 1)
                    for c0, n, who in segs(T):
                        last = ts(cv[:, i, c0:c0 + n], hc[:, i, CPAD * (1 + who) + c0:CPAD * (1 + who) + c0 + n],
                           vec[:, l, bass.ds(i * CONF_K + wmid, 1)], vec[:, l, bass.ds(i + V_BDW, 1)],
                           ALU.mult, ALU.add)
                    st.done(last)

                def conv_taps(i, c_base, taps):
                    for tap in taps:
                        for c0, n, who in segs(T):
                            last = stt(cv[:, i + c_base, c0:c0 + n],
                                       hc[:, i + c_base, CPAD * who + c0 + tap:CPAD * who + c0 + tap + n],
                                       vec[:, l, bass.ds(i * CONF_K + (V_WC + c_base * CONF_K + tap), 1)],
                                       cv[:, i + c_base, c0:c0 + n], ALU.mult, ALU.add)
                        st.done(last)

                TAPS = [t for t in range(CONF_K) if t != CPAD]
                PART = [TAPS[0:8], TAPS[8:15], TAPS[15:23], TAPS[23:30]]

                def merge(branch):
                    jb = (jl + (J_MA, J_MB, J_MC)[branch]) // 2
                    conv = branch < 2
                    with st.loop(0, 2, (30 if conv else 0) + (4 if branch > 0 else 0)) as i:
                        for j in range(4):
                            if conv:
                                conv_taps(i, 2 * branch, PART[j])
                            dve.wait_ge(mm[1], i * 4 + (jb + j + 1))
                            dve.wait_ge(sfree[0], i * 4 + (jb + j + 1))
                            a = e[4 + j % 2][:, :T]
                            if branch == 0:
                                tt(a, slot(1, T), e[0][:, :T], ALU.mult).then_inc(sfree[1], 1)
                                dve.wait_ge(sfree[1], i * 4 + (jb + j + 1))
                                dve.sem_inc(s_mgd, 1)
                                continue
                            if branch == 1:
                                tt(a, slot(1, T), e[0][:, :T], ALU.mult).then_inc(sfree[1], 1)
                            else:
                                stt(a, slot(1, T), vec[:, l, bass.ds(i * 4 + (V_BPC + j), 1)], e[0][:, :T],
                                    ALU.add, ALU.mult).then_inc(sfree[1], 1)
                            dve.wait_ge(sfree[1], i * 4 + (jb + j + 1))
                            nin = (2 * l + branch - 1) * KD + j
                            dve.wait_ge(s_accin, i * 64 + 16 * (nin + 1))
                            dst = a if branch == 1 else X[:, i * 4 + j, :T]
                            st.done(tt(dst, a, e[1][:, :T], ALU.add))
                            dve.sem_inc(s_mgd, 1)
                            if branch == 2:
                                dve.sem_inc(s_mgf, 1)

                merge(0)
                dve.wait_ge(s_accst, 16 * (2 * l + 1) * KD)

                dve.wait_ge(mm[1], (jl + J_SHORT) // 2)
                st.done(nc.vector.memset(e[1][:], 0.0))
                hb = (jl + J_SHORT) // 2
                with st.loop(0, 4, 5) as i:
                    dve.wait_ge(mm[1], i * 2 + (hb + 1))
                    dve.wait_ge(sfree[0], i * 2 + (hb + 1))
                    for c0, n, who in segs(T):
                        last = tt(e[1][:, SPAD * (1 + who) + c0:SPAD * (1 + who) + c0 + n],
                                  PS[:, SLOT[1] + c0:SLOT[1] + c0 + n], e[0][:, c0:c0 + n], ALU.mult)
                    st.done(last)
                    dve.sem_inc(sfree[1], 1)
                    for tap in range(SHORT_K):
                        wt = vec[:, l, bass.ds(i * SHORT_K + (V_WS + tap), 1)]
                        for c0, n, who in segs(T):
                            x = e[1][:, SPAD * who + c0 + tap:SPAD * who + c0 + tap + n]
                            if tap == 0:
                                last = ts(e[2][:, c0:c0 + n], x, wt, None, ALU.mult)
                            else:
                                last = stt(e[2][:, c0:c0 + n], x, wt, e[2][:, c0:c0 + n], ALU.mult, ALU.add)
                        st.done(last)
                    dve.wait_ge(mm[1], i * 2 + (hb + 2))
                    st.done(tt(e[2][:, :T], slot(1, T), e[2][:, :T], ALU.mult))
                    dve.wait_ge(sfree[0], i * 2 + (hb + 2))
                    tt(e[3][:, :T], e[2][:, :T], e[4][:, :T], ALU.mult).then_inc(s_yf, 1)
                    dve.sem_inc(sfree[1], 1)
                    dve.wait_ge(s_yh, i + (12 * l + 5))
                    tt(Yl[:, i, :T], e[3][:, :T], Yh[:, i, :T].bitcast(F32), ALU.subtract).then_inc(s_y, 1)

                merge(1)
                dve.wait_ge(s_accst, 16 * (2 * l + 2) * KD)

                def norm(k, z, nt, first):
                    dve.wait_ge(s_mean, k + 1)
                    for j in range(nt):
                        tt(z(j), z(j), e[4][:, :T], ALU.subtract).then_inc(s_dev, 1)
                        if j >= 1:
                            add_square(j - 1, first)
                    add_square(nt - 1, first)
                    dve.wait_ge(s_lacc, first + nt)
                    dve.sem_inc(s_csum, 1)
                    dve.wait_ge(s_std, k + 1)
                    st.done(nc.vector.reciprocal(e[4][:, :T], e[4][:, :T]))

                def add_square(j, first):
                    dve.wait_ge(s_lsq, first + j + 1)
                    if j == 0:
                        nc.vector.tensor_copy(e[5][:, :T], e[0][:, :T]).then_inc(s_lacc, 1)
                    else:
                        dve.wait_ge(s_lacc, first + j)
                        tt(e[5][:, :T], e[5][:, :T], e[j % 2][:, :T], ALU.add).then_inc(s_lacc, 1)

                st.done(tt(e[4][:, :T], cv[:, 0, :T], cv[:, 1, :T], ALU.add))
                st.done(tt(e[4][:, :T], e[4][:, :T], cv[:, 2, :T], ALU.add))
                st.done(tt(e[4][:, :T], e[4][:, :T], cv[:, 3, :T], ALU.add))
                dve.sem_inc(s_csum, 1)
                norm(2 * l, lambda j: cv[:, j, :T], KW, 12 * l)
                for n in range(KW):
                    tt(cv[:, n, :T], cv[:, n, :T], e[4][:, :T], ALU.mult).then_inc(s_norm, 1)
                dve.wait_ge(mm[1], (jl + J_ZC) // 2)
                for n in range(KW):
                    dve.wait_ge(s_hact, 4 * l + n + 1)
                    dve.wait_ge(sfree[n % 2], (jl + J_ZC + n) // 2 + 1)
                    tt(e[2 + n % 2][:, :T], e[n % 2][:, :T], hc[:, n, :T], ALU.mult).then_inc(s_yf, 1)
                    dve.wait_ge(s_yh, 12 * l + 8 + n + 1)
                    tt(Yl[:, n, :T], e[2 + n % 2][:, :T], Yh[:, n, :T].bitcast(F32), ALU.subtract).then_inc(s_y, 1)

                merge(2)

                for j in range(KD):
                    dve.wait_ge(s_mgh, KD * l + j + 1)
                    tt(Ul[:, j, :T], X[:, j, :T], Uh[:, j, :T].bitcast(F32), ALU.subtract).then_inc(s_mg, 1)

                for j in range(KD):
                    dve.wait_ge(sfree[j % 2], (jl + J_OUT + j) // 2 + 1)
                    nh_in = (KD // 2) * (l + 1) + j // 2 + 1
                    dve.wait_ge(s_hin[j % 2], 16 * nh_in)
                    stt(Z[:, j, :T], e[2 + j % 2][:, :T], ALPHA, e[j % 2][:, :T], ALU.mult,
                        ALU.add).then_inc(s_z, 1)
                    dve.wait_ge(s_z, KD * l + j + 1)
                    if j == 1:
                        st.done(tt(e[4][:, :T], Z[:, 0, :T], Z[:, 1, :T], ALU.add))
                    elif j > 1:
                        st.done(tt(e[4][:, :T], e[4][:, :T], Z[:, j, :T], ALU.add))
                dve.sem_inc(s_csum, 1)
                norm(2 * l + 1, lambda j: Z[:, j, :T], KD, 12 * l + 4)
                for j in range(KD):
                    tt(Z[:, j, :T], Z[:, j, :T], e[4][:, :T], ALU.mult).then_inc(s_norm, 1)
                if l + 1 < DEPTH:
                    mod_row(l + 1, 0, 3 * D, 3)
                    mod_col(l + 1, 0, 3 * KD, 0, 3)
                    for j in range(KD):
                        u_lo(l + 1, j)


def _tiles(w):
    K, N = w.shape
    return np.ascontiguousarray(w.reshape(K // P, P, N // P, P).transpose(2, 1, 0, 3)).reshape(N // P, P, K)


def _cols(v):
    return v.reshape(-1, P).T


def _rope():
    q = HD // 4
    freqs = (10000.0 ** (-np.arange(q, dtype=np.float32) / q)).astype(np.float32)
    n = np.arange(LAT)
    ar = (n // GRID_W).astype(np.float32)[:, None] * freqs
    ac = (n % GRID_W).astype(np.float32)[:, None] * freqs
    c = np.concatenate([np.cos(ar), np.cos(ar), np.cos(ac), np.cos(ac)], 1)
    s = np.concatenate([-np.sin(ar), np.sin(ar), -np.sin(ac), np.sin(ac)], 1)
    c = np.concatenate([c, np.ones((CTX, HD))], 0)
    s = np.concatenate([s, np.zeros((CTX, HD))], 0)
    both = np.stack([np.concatenate([x, x], 1) for x in (c, s)]).astype(np.float32)
    return np.ascontiguousarray(both.reshape(2, NTOK, P, P).transpose(0, 2, 1, 3)).reshape(2, P, TALL)


def kernel(**inputs):
    import concourse.bacc as _bacc
    from concourse.bass_utils import run_bass_kernel_spmd as _run

    a = {k: np.asarray(v) for k, v in inputs.items()}
    w8, w4, vecs, gains = [], [], [], []
    for l in range(DEPTH):
        w8.append(np.concatenate([_tiles(a["w_in"][l])[W_ORDER], _tiles(a["w_out"][l])]))
        w4.append(np.concatenate([_tiles(a[n][l]) for n in ("w_proj_attn", "w_proj_short", "w_proj_conf")]))
        vecs.append(np.concatenate(
            [_cols(a["post_ln_g"][l]), _cols(a["post_ln_b"][l]), _cols(a["b_proj_conf"][l]),
             _cols(a["conf_ln_g"][l]), _cols(a["conf_ln_b"][l]), _cols(a["b_conf_dw"][l]),
             a["w_short_conv"][l].reshape(SHORT_K, KW, P).transpose(2, 1, 0).reshape(P, -1),
             a["w_conf_dw"][l].reshape(CONF_K, KW, P).transpose(2, 1, 0).reshape(P, -1),
             _cols(a["b_mod"][l])], 1))
        rows = []
        for g in (a["k_gain"][l], a["q_gain"][l]):
            sw = g.reshape(2, 2, HD // 4)[:, ::-1].reshape(HD)
            rows += [np.concatenate([g, g]), np.concatenate([sw, sw])]
        gains.append(np.broadcast_to(np.stack(rows)[None], (P, 4, P)))
    hT = np.concatenate([a["x"][0], a["ctx"][0]]).T.reshape(KD, P, TALL)
    eye = np.eye(P, dtype=np.float32)
    feed = {
        "hT_in": hT,
        "cvec": np.stack([_cols(a["c"][0]), _cols(a["c_ctx"])], 2),
        "wmod": a["w_mod"].reshape(DEPTH, KD, P, 3 * D),
        "w8": np.stack(w8), "w4": np.stack(w4),
        "vecs": np.stack(vecs, 1), "gains": np.stack(gains),
        "rope": _rope(), "ident_in": eye, "stack_in": np.concatenate([eye[:HD, :HD]] * 2),
    }
    nc = _bacc.Bacc("TRN2", target_bir_lowering=False, num_devices=1, dynamic_dma_scratch_size=1024)
    arrays, args = {}, []
    for name, v in feed.items():
        v = np.ascontiguousarray(v)
        arrays[name] = v
        args.append(nc.dram_tensor(name, v.shape, F32, kind="ExternalInput").ap())
    args.append(nc.dram_tensor("outT", (KD, P, LAT), F32, kind="ExternalOutput").ap())
    build(nc, *args)
    r = _run(nc, [arrays], core_ids=[0])
    return np.ascontiguousarray(r.results[0]["outT"].reshape(D, LAT).T).reshape(1, LAT, D)
```

```python
from contextlib import ExitStack, contextmanager

import numpy as np
import concourse.bass as bass
from concourse import mybir

F32 = mybir.dt.float32
F32R = mybir.dt.float32r
ACT = mybir.ActivationFunctionType
ALU = mybir.AluOpType
AX_X = mybir.AxisListType.X

P = 128
D = 1024
KD = D // P
LAT, CTX = 1024, 256
TALL = LAT + CTX
NTOK = TALL // P
DEPTH = 2
GRID_W = 64
HD = 64
NKV = 2
W3 = 512
KW = W3 // P
SHORT_K, CONF_K = 3, 31
SPAD, CPAD = SHORT_K // 2, CONF_K // 2
ALPHA = (2.0 * DEPTH) ** 0.25
LN_EPS, RMS_EPS = 1e-5, 1e-6
HCW = CPAD + LAT + CPAD + CTX + CPAD + 1
EW = 1296

_Q, _K, _V, _ZA = range(0, 4), [4], [5], range(6, 10)
_SB, _SC, _SH, _ZS = range(10, 14), range(14, 18), range(18, 22), range(22, 26)
_CA, _CG, _ZC = range(26, 30), range(30, 34), range(34, 38)
_GA, _GB, _GC = range(38, 46), range(46, 54), range(54, 62)
W_ORDER = [*_K, *_Q, *_V, *_ZA]
for _i in range(KW):
    W_ORDER += [_CG[_i], _CA[_i]]
W_ORDER += [*_GA]
for _i in range(KW):
    W_ORDER += [_SC[_i], _SH[_i], _ZS[_i], _SB[_i]]
W_ORDER += [*_GB, *_ZC, *_GC]
N_WIN = len(W_ORDER)
N_W8 = N_WIN + KD
W8_QKV, W8_ZA, W8_CONF, W8_GA, W8_SHORT, W8_GB, W8_ZC, W8_GC, W8_OUT = 0, 6, 10, 18, 26, 42, 50, 54, 62
J_QKV, J_ZA, J_CONF, J_MA, J_SHORT, J_MB, J_ZC, J_MC, J_OUT, NJ = 0, 6, 10, 18, 34, 50, 66, 70, 86, 94

V_PG, V_PB, V_BPC, V_CG, V_CB, V_BDW = 0, 8, 16, 24, 28, 32
V_WS = 36
V_WC = V_WS + KW * SHORT_K
V_BM = V_WC + KW * CONF_K
NV = V_BM + 3 * KD

O_K, O_Q0, O_Q1, O_KT0, O_KT1, O_Q2, O_Q3, O_V = range(8)
QKV_OPS = (O_K, O_Q0, O_Q1, O_Q2, O_Q3, O_V)
O_OT, O_CMEAN, O_CVAR, O_OMEAN, O_OVAR, N_OPS = 8, 12, 13, 14, 15, 16
SLOT = (0, 1536)
TB = (3072, 3584)
PT0 = (2560, 3072)
O0 = 3584


def chunks(n):
    return [(c, min(512, n - c)) for c in range(0, n, 512)]


def op_width(l, op):
    return TALL if l == 0 or op in (O_K, O_V, O_KT0, O_KT1) else LAT


def pieces(l, op):
    n = sum(len(chunks(op_width(a, b))) for a in range(DEPTH) for b in range(N_OPS) if (a, b) < (l, op))
    return [(n + i, c, m) for i, (c, m) in enumerate(chunks(op_width(l, op)))]


def segs(T):
    return [(0, LAT, 0)] + ([(LAT, CTX, 1)] if T > LAT else [])


def heads_at(nk, kt, nxt, nxt2):
    if nk == 2:
        return [(1, h) for h in range(4)] if kt == 0 and nxt else []
    if kt == nk - 1:
        return [(2, 0)] if nxt2 else []
    return [(1, (kt + 1) // 2)] if kt % 2 and kt < 7 and nxt else []


def exps_at(nk, kt, nxt):
    if nk == 2:
        return [h for _, h in heads_at(nk, kt, nxt, False)]
    return {1: [0], 3: [1], 5: [2], nk - 1: [3]}.get(kt, []) if nxt else []


def back_at(nk):
    return 3 if nk > 2 else 1


def q_at(nk):
    return 5 if nk > 2 else 1


def pv_tiles(kt, prev):
    return [k for k in ((kt - 3, kt - 2) if kt % 2 else ()) if k >= 0 or prev]


def pt_buf(g, kt):
    return (kt + 2 * g) % 4


def fill(nk, kt, i0, i1, prev, nxt2):
    if kt % 2:
        return i1 + kt // 2
    return i0 + kt // 2 - (1 if prev and kt < back_at(nk) else 0) + (1 if nxt2 and kt > q_at(nk) else 0)


def score_parts(h, nk):
    if nk * P <= 256:
        return [], [(0, nk * P)]
    if h % 2 == 0:
        return [(0, 512), (512, 512)], [(1024, 256)]
    return [(256, 512), (768, 512)], [(0, 256)]


def score_at(h, nk):
    return 512 * h if nk * P <= 256 else (h % 2) * TALL


class Steps:

    def __init__(self, eng, sem):
        self.eng, self.sem, self.base, self.i, self.per, self.lo = eng, sem, 0, None, 0, 0

    def done(self, ins):
        ins.then_inc(self.sem, 1)
        self.base += 1
        n = self.base if self.i is None else (self.i - self.lo) * self.per + self.base
        self.eng.wait_ge(self.sem, n)

    @contextmanager
    def loop(self, lo, hi, per):
        start = self.base
        with self.eng.Fori(lo, hi) as i:
            self.i, self.per, self.lo = i, per, lo
            yield i
        assert self.base - start == per, (self.base - start, per)
        self.i = None
        self.base = start + per * (hi - lo)


def build(nc, hT_in, cvec, wmod, w8, w4, vecs, gains, rope, ident_in, stack_in, outT):
    with ExitStack() as ctx:
        def sem(name):
            return ctx.enter_context(nc.semaphore(name))

        base = [(nc.sbuf_base + 31) // 32 * 32]

        def region(nbytes):
            at = base[0]
            base[0] = at + (nbytes + 31) // 32 * 32
            return at

        def at(name, shape, dt, offset):
            return nc.alloc_sbuf_tensor_at(name, shape, dt, offset=offset)

        rU = region(2 * KD * TALL * 4)
        rY = region(2 * KW * TALL * 4)
        rX = region(41984)
        rE = region(6 * EW * 4)
        rW = region(6 * D * 4)
        rC = region(0)
        Uh = at("Uh", [P, KD, TALL], F32R, rU)
        Ul = at("Ul", [P, KD, TALL], F32R, rU + KD * TALL * 4)
        Yh = at("Yh", [P, KW, TALL], F32R, rY)
        Yl = at("Yl", [P, KW, TALL], F32R, rY + KW * TALL * 4)
        Pr = at("Pr", [P, 2, 4, TALL], F32, rY)
        Z = at("Z", [P, KD, TALL], F32, rY)
        B5 = TALL * 4
        raw = [at(f"raw{i}", [P, TALL], F32, rY + (6 + i) * B5) for i in range(2)]
        fc = [at(f"fc{i}", [P, TALL], F32, rY + i * B5) for i in range(2)]
        sq = at("sq", [P, TALL], F32, rY + 2 * B5)
        qn = at("qn", [P, TALL], F32, rY + 3 * B5)
        qa = at("qa", [P, TALL], F32, rY + 4 * B5)
        qb = at("qb", [P, TALL], F32, rY + 5 * B5)
        modrow = [at("modrow0", [2, 3 * D], F32, rY), at("modrow1", [2, 3 * D], F32, rU + 5 * 12288)]
        qo = at("qo", [P, NTOK, W3], F32, rX)
        cosT = at("cosT", [P, TALL], F32, rX)
        sinT = at("sinT", [P, TALL], F32, rX + B5)
        kT = at("kT", [P, NKV, TALL], F32R, rX + 20480)
        Vt = at("Vt", [P, NTOK, NKV, P], F32R, rX + 30720)
        hc = at("hc", [P, KW, HCW], F32, rX)
        cv = at("cv", [P, KW, TALL], F32, rX + 21248)
        X = at("X", [P, KD, TALL], F32, rX)
        wmA = [at(f"wmA{i}", [P, 2 * D], F32, rU + i * 8192) for i in range(KD)]
        wmB = [at(f"wmB{i}", [P, D], F32, rX + i * 4096) for i in range(KD)]
        wmL = [at(f"wmL{i}", [P, 3 * D], F32, (rX + i * 12288) if i < 3 else rU + (i - 3) * 12288)
               for i in range(KD)]
        e = [at(f"e{i}", [P, EW], F32, rE + i * EW * 4) for i in range(6)]
        kd = at("kd", [P, NTOK, NKV, 2, HD], F32, rE + 2 * EW * 4)
        qTh = [at(f"qTh{i}", [P, 512], F32R, rE + i * 2048) for i in range(2)]
        qTl = [at(f"qTl{i}", [P, 512], F32R, rE + 4096 + i * 2048) for i in range(2)]
        qd = [at(f"qd{i}", [P, 4, 2, HD], F32, rE + 8192 + i * 2048) for i in range(2)]
        ob = at("ob", [P, 512], F32, rE + 12288)
        PTh = [at(f"PTh{i}", [P, 512], F32R, rE + 14336 + i * 2048) for i in range(4)]
        PTl = [at(f"PTl{i}", [P, 512], F32R, rE + 22528 + i * 2048) for i in range(4)]
        wraw = [at(f"wraw{i}", [P, D], F32, rW + i * 4096) for i in range(2)]
        wh = [at(f"wh{i}", [P, D], F32R, rW + 8192 + i * 4096) for i in range(2)]
        wl = [at(f"wl{i}", [P, D], F32R, rW + 16384 + i * 4096) for i in range(2)]
        cpos = [rC]

        def small(name, shape):
            n = 4
            for s in shape[1:]:
                n *= s
            o = cpos[0]
            cpos[0] = o + (n + 31) // 32 * 32
            return at(name, shape, F32, o)

        ident = small("ident", [P, P])
        stackI = small("stackI", [P, HD])
        ones = small("ones", [P, P])
        vec = small("vec", [P, DEPTH, NV])
        gain = small("gain", [P, 4, P])
        craw = small("craw", [P, KD, 2])
        csilu = small("csilu", [P, KD, 2])
        mod = small("mod", [P, DEPTH, 3 * KD, 2])
        ss = small("ss", [P, 2 * NTOK])
        ms = small("ms", [P, 2, 2 * NTOK])
        rstd = small("rstd", [P, 2, 2 * NTOK])
        mhalf = small("mhalf", [P, 2 * NTOK])
        nm = small("nm", [P, 8])
        eps = small("eps", [P, 1])
        rs = small("rs", [P, 2, 2, 4])
        rsum = small("rsum", [P, 4])
        ri = small("ri", [P, NKV, 4])
        assert cpos[0] <= nc.sbuf_usable_end, (cpos[0], nc.sbuf_usable_end)

        PS = ctx.enter_context(nc.psum_tensor("PS", [P, 4096], F32))
        hT1 = nc.dram_tensor("hT1", [KD, P, TALL], F32, kind="Internal").ap()
        accd = nc.dram_tensor("accd", [2, KD, P, TALL], F32, kind="Internal").ap()

        def tbank(f, n):
            return PS[:, TB[f % 2]:TB[f % 2] + n]

        def slot(par, T):
            return PS[:, SLOT[par]:SLOT[par] + T]

        s_c = sem("s_consts")
        s_wm = [sem(f"s_wmod{i}") for i in range(KD)]
        s_wmb = sem("s_wmod_gate")
        s_wmu = sem("s_wmod_used")
        s_csilu = sem("s_csilu")
        s_modrow = sem("s_mod_row")
        s_modtr = sem("s_mod_transposed")
        s_mod = sem("s_mod_ready")
        s_ones = sem("s_ones")
        wland = [sem(f"w_landed{i}") for i in range(2)]
        whi = [sem(f"w_hi{i}") for i in range(2)]
        wsplit = [sem(f"w_split{i}") for i in range(2)]
        mm = [sem(f"mm_done{i}") for i in range(2)]
        sfree = [sem(f"slot_free{i}") for i in range(2)]
        t_done = sem("piece_done")
        t_free = sem("piece_read")
        s_rawfree = sem("raw_free")
        s_oraw = sem("o_transposed")
        s_mean = sem("ln_mean")
        s_tail = sem("exp_tail_done")
        s_hin = [sem(f"h_landed{i}") for i in range(2)]
        s_um = [sem(f"u_float{i}") for i in range(2)]
        s_ufp = sem("u_hi")
        s_u = sem("u_ready")
        s_rope = sem("s_rope")
        s_gain = sem("s_gain")
        s_tab = sem("rope_tables")
        s_fc = sem("feature_copy")
        s_sq = sem("squares")
        s_ms = sem("mean_square")
        s_rstd = sem("rstd")
        s_kd = sem("k_duplicated")
        s_vhi = sem("v_hi")
        s_khi = sem("k_hi")
        s_kv = sem("kv_ready")
        s_q = sem("q_ready")
        s_qd = sem("q_duplicated")
        pt_done = [sem(f"pt_done{i}") for i in range(2)]
        pt_hi = [sem(f"pt_hi{i}") for i in range(2)]
        pt_free = [sem(f"pt_free{i}") for i in range(2)]
        s_s = sem("scores")
        s_nm = sem("neg_max")
        s_exp = sem("exp_done")
        s_pv = sem("pv_done")
        s_o = sem("o_copied")
        s_oatt = sem("o_written")
        s_yf = sem("y_float")
        s_yh = sem("y_hi")
        s_y = sem("y_ready")
        s_pad = sem("pads_zeroed")
        s_accin = sem("acc_landed")
        s_accst = sem("acc_stored")
        s_mgh = sem("merged_hi")
        s_mg = sem("merged_split")
        s_mgf = sem("merged_float")
        s_carry = sem("wait_carrier")
        s_mgd = sem("merge_done")
        s_lacc = sem("ln_square_added")
        s_csum = sem("ln_sum")
        s_dev = sem("ln_deviation")
        s_lsq = sem("ln_square")
        s_std = sem("ln_std")
        s_norm = sem("ln_normalised")
        s_hact = sem("conf_activated")
        s_z = sem("z_ready")
        s_hn = sem("h_normalised")
        s_hst = sem("h_stored")
        s_outst = sem("out_stored")
        c_dve = sem("c_dve")

        TL = [TALL] + [LAT] * (DEPTH - 1)

        def jobs_qkv(l):
            return [TALL] + [TL[l]] * 4 + [TALL]

        def att_calls(l):
            out = [(0, LAT // P, 0, NTOK)]
            if TL[l] > LAT:
                out.append((LAT // P, CTX // P, LAT // P, CTX // P))
            return out

        def att_base(l, call):
            units, pt = 0, [0, 0]
            for ll in range(DEPTH):
                for n, (t0, nt, k0, nk) in enumerate(att_calls(ll)):
                    if (ll, n) == (l, call):
                        return units, pt
                    U = 2 * nt
                    pt = [pt[0] - 1 + (nk // 2 + 2) * U, pt[1] + 1 + (nk // 2) * U]
                    units += U
            return units, pt

        block = ctx.enter_context(nc.Block())

        @block.sync
        def _(sp):
            sp.dma_start(craw[:], cvec).then_inc(s_c, 16)
            sp.dma_start(ident[:], ident_in).then_inc(s_c, 16)
            sp.dma_start(stackI[:], stack_in).then_inc(s_c, 16)
            sp.dma_start(vec[:], vecs).then_inc(s_c, 16)
            for k in range(KD):
                sp.dma_start(wmA[k][:], wmod[0, k][:, :2 * D]).then_inc(s_wm[k], 16)

            def load(nh, par, src, width):
                if not isinstance(nh, int) or nh > 0:
                    sp.wait_ge(wsplit[par], nh * 2)
                sp.dma_start(wraw[par][:, :width], src).then_inc(wland[par], 16)

            def load_merge(l, jb, w8b, w4b):
                with sp.Fori(0, 2) as i:
                    for j in range(4):
                        load(i * 4 + (jb // 2 + j), 0, w8[l, i * 4 + (w8b + j)], D)
                        load(i * 4 + (jb // 2 + j), 1, w4[l, i * 4 + (w4b + j)], W3)

            for l in range(DEPTH):
                jl = l * NJ
                if l == 0:
                    for j in range(KD):
                        if j == 2:
                            for n in range(2):
                                load(n // 2, n % 2, w8[l, W8_QKV + n], D)
                            for k in range(KD):
                                sp.dma_start(wmB[k][:], wmod[0, k][:, 2 * D:]).then_inc(s_wmb, 16)
                        if j >= 2:
                            sp.wait_ge(s_um[j % 2], j // 2)
                        sp.dma_start(e[2 + j % 2][:, :TALL], hT_in[j]).then_inc(s_hin[j % 2], 16)
                    sp.wait_ge(s_wmu, 2 * KD)
                sp.wait_ge(s_u, KD * (l + 1))
                if l > 0:
                    sp.wait_ge(s_hst, 16 * KD)
                sp.dma_start(cosT[:], rope[0]).then_inc(s_rope, 16)
                sp.dma_start(sinT[:], rope[1]).then_inc(s_rope, 16)
                sp.dma_start(gain[:], gains[l]).then_inc(s_gain, 16)
                for n in range(2, 6):
                    load((jl + n) // 2, n % 2, w8[l, W8_QKV + n], D)
                for n in range(4):
                    load((jl + J_ZA + n) // 2, n % 2, w8[l, W8_ZA + n], D)
                with sp.Fori(0, 4) as i:
                    for c in range(2):
                        load(i + (jl + J_CONF) // 2, c, w8[l, i * 2 + (W8_CONF + c)], D)
                load_merge(l, jl + J_MA, W8_GA, 0)
                with sp.Fori(0, 4) as i:
                    for c in range(4):
                        load(i * 2 + ((jl + J_SHORT) // 2 + c // 2), c % 2, w8[l, i * 4 + (W8_SHORT + c)], D)
                load_merge(l, jl + J_MB, W8_GB, KD)
                for n in range(4):
                    load((jl + J_ZC + n) // 2, n % 2, w8[l, W8_ZC + n], D)
                load_merge(l, jl + J_MC, W8_GC, 2 * KD)
                T = TL[l]
                src = hT_in if l == 0 else hT1
                for j in range(KD):
                    if j == 2:
                        sp.wait_ge(s_mgf, KD * (l + 1))
                    load((jl + J_OUT + j) // 2, j % 2, w8[l, W8_OUT + j], D)
                    if j >= 2:
                        sp.wait_ge(s_z, KD * l + j - 1)
                    if j == 4 and l + 1 < DEPTH:
                        sp.wait_ge(s_mg, KD * (l + 1))
                        for k in range(3):
                            sp.dma_start(wmL[k][:], wmod[l + 1, k]).then_inc(s_wm[k], 16)
                    sp.dma_start(e[2 + j % 2][:, :T], src[j][:, :T]).then_inc(s_hin[j % 2], 16)
                if l + 1 < DEPTH:
                    for n in range(2):
                        load((jl + NJ + n) // 2, n % 2, w8[l + 1, W8_QKV + n], D)
                    sp.wait_ge(mm[1], (jl + NJ) // 2)
                    for k in range(3, KD):
                        sp.dma_start(wmL[k][:], wmod[l + 1, k]).then_inc(s_wm[k], 16)
                    for j in range(KD):
                        sp.wait_ge(s_hn, j + 1)
                        sp.dma_start(hT1[j], X[:, j, :]).then_inc(s_hst, 16)
                else:
                    for j in range(KD):
                        sp.wait_ge(s_hn, KD * (DEPTH - 1) + j + 1)
                        sp.dma_start(outT[j], X[:, j, :LAT]).then_inc(s_outst, 16)
                    sp.wait_ge(s_outst, 16 * KD)
            sp.wait_ge(s_accst, 16 * 2 * KD * DEPTH)

        @block.gpsimd
        def _(pool):

            def split(nh, par, width):
                pool.wait_ge(wland[par], nh * 16 + 16)
                if not isinstance(nh, int) or nh > 0:
                    pool.wait_ge(mm[par], nh)
                if not isinstance(nh, int):
                    pool.sem_inc(s_carry, 1)
                for a in range(2):
                    s = slice(a * width // 2, (a + 1) * width // 2)
                    nc.gpsimd.tensor_copy(wh[par][:, s], wraw[par][:, s]).then_inc(whi[par], 1)
                    pool.wait_ge(whi[par], nh * 2 + (a + 1))
                    nc.gpsimd.tensor_tensor(wl[par][:, s], wraw[par][:, s],
                                            wh[par][:, s].bitcast(F32), ALU.subtract).then_inc(wsplit[par], 1)

            def split_merge(jb):
                with pool.Fori(0, 2) as i:
                    for j in range(4):
                        split(i * 4 + (jb // 2 + j), 0, D)
                        split(i * 4 + (jb // 2 + j), 1, W3)

            nc.gpsimd.memset(ones[:], 1.0 / D).then_inc(s_ones, 1)
            nc.gpsimd.memset(mhalf[:], -0.5).then_inc(s_ones, 1)
            nc.gpsimd.memset(eps[:], LN_EPS).then_inc(s_ones, 1)
            pool.wait_ge(s_ones, 3)
            for l in range(DEPTH):
                jl = l * NJ
                T = TL[l]
                for n in range(2):
                    split((jl + n) // 2, n % 2, D)
                def table(g, dst, tab):
                    nc.gpsimd.tensor_tensor(
                        dst[:, :TALL].rearrange("p (t c) -> p t c", c=P),
                        tab[:].rearrange("p (t c) -> p t c", c=P),
                        gain[:, g:g + 1, :].broadcast_to([P, NTOK, P]), ALU.mult).then_inc(s_tab, 1)

                def rms(n):
                    pool.wait_ge(s_ms, l * 5 + n + 1)
                    nc.gpsimd.tensor_tensor(rstd[:, n % 2], ms[:, n % 2], mhalf[:], ALU.pow).then_inc(s_rstd, 1)

                if l > 0:
                    split((jl + 2) // 2, 0, D)
                pool.wait_ge(s_rope, 32 * (l + 1))
                pool.wait_ge(s_gain, 16 * (l + 1))
                pool.wait_ge(s_u, KD * (l + 1))
                table(0, e[0], cosT)
                table(1, e[1], sinT)
                if l == 0:
                    split((jl + 2) // 2, 0, D)
                split((jl + 2) // 2, 1, D)
                rms(0)
                table(2, e[4], cosT)
                table(3, e[5], sinT)
                split((jl + 4) // 2, 0, D)
                for n in range(1, 3):
                    rms(n)
                    split((jl + 4 + n) // 2, n % 2, D)
                rms(3)
                rms(4)
                split((jl + 7) // 2, 1, D)
                pool.wait_ge(s_q, 4 * (l + 1))
                pool.wait_ge(s_kv, 3 * (l + 1))
                for n, (t0, nt, k0, nk) in enumerate(att_calls(l)):
                    ub, _ = att_base(l, n)

                    def dup(t, g):
                        pool.sem_inc(s_carry, 1)
                        nc.gpsimd.tensor_copy(
                            qd[g][:],
                            qo[:, t, g * 4 * HD:(g + 1) * 4 * HD].rearrange("p (h u d) -> p h u d", h=4, u=1)
                            .broadcast_to([P, 4, 2, HD])).then_inc(s_qd, 1)

                    if n > 0:
                        pool.wait_ge(s_s, 4 * ub)
                    for g in range(NKV):
                        dup(t0, g)
                    with pool.Fori(0, nt - 1) as i:
                        for g in range(NKV):
                            pool.wait_ge(s_s, i * 8 + (4 * (ub + g) + 4))
                            dup(i + (t0 + 1), g)
                for n in range(2, 4):
                    split((jl + J_ZA + n) // 2, n % 2, D)
                for c in range(2):
                    split((jl + J_CONF) // 2, c, D)
                pool.wait_ge(t_done, pieces(l, O_OT + 3)[-1][0] + 1)
                for c0, n, who in segs(T):
                    nc.gpsimd.memset(hc[:, :, CPAD * who + c0:CPAD * (who + 1) + c0], 0.0).then_inc(s_pad, 1)
                nc.gpsimd.memset(hc[:, :, CPAD * (who + 1) + c0 + n:CPAD * (who + 2) + c0 + n],
                                 0.0).then_inc(s_pad, 1)
                with pool.Fori(1, 4) as i:
                    for c in range(2):
                        split(i + (jl + J_CONF) // 2, c, D)
                split_merge(jl + J_MA)
                with pool.Fori(0, 4) as i:
                    for c in range(4):
                        split(i * 2 + ((jl + J_SHORT) // 2 + c // 2), c % 2, D)
                split_merge(jl + J_MB)
                for n in range(4):
                    split((jl + J_ZC + n) // 2, n % 2, D)
                split_merge(jl + J_MC)
                for n in range(KD):
                    split((jl + J_OUT + n) // 2, n % 2, D)

        @block.tensor
        def _(pe):
            mmul = nc.tensor.matmul

            def job(nh, par, K, T, hi, lo, before_k=None, before_lo=None):
                if not isinstance(nh, int) or nh > 0:
                    pe.wait_ge(sfree[par], nh)
                for k in range(K):
                    if k % (K // 2) == 0:
                        pe.wait_ge(wsplit[par], nh * 2 + (k // (K // 2) + 1))
                    if before_k is not None:
                        before_k(k)
                    for a, w, x in ((0, wh, hi), (1, wl, hi)) + (((2, wh, lo),) if before_lo is None else ()):
                        for c, n in chunks(T):
                            last = mmul(PS[:, SLOT[par] + c:SLOT[par] + c + n], w[par][:, k * P:(k + 1) * P],
                                        x[:, k, c:c + n], start=(k == 0 and a == 0), stop=(k == K - 1 and a == 2))
                for k in range(K if before_lo is not None else 0):
                    before_lo(k)
                    for c, n in chunks(T):
                        last = mmul(PS[:, SLOT[par] + c:SLOT[par] + c + n], wh[par][:, k * P:(k + 1) * P],
                                    lo[:, k, c:c + n], start=False, stop=(k == K - 1))
                last.then_inc(mm[par], 1)

            def piece_wait(f):
                if f >= 2:
                    pe.wait_ge(t_free, f - 1)

            def transposes(l, op, srcs):
                for f, c, n in pieces(l, op):
                    piece_wait(f)
                    for t in range(n // P):
                        last = nc.tensor.transpose(tbank(f, n)[:, t * P:(t + 1) * P], srcs[c // P + t], ident[:])
                    last.then_inc(t_done, 1)

            def stat(l, op, src):
                for f, c, n in pieces(l, op):
                    piece_wait(f)
                    mmul(tbank(f, n), ones[:], src[:, c:c + n], start=True, stop=True).then_inc(t_done, 1)

            def mod_rows(k, w, col0, ncol, landed, n):
                pe.wait_ge(landed, n)
                for n in range(ncol // 512):
                    last = mmul(PS[0:2, col0 + n * 512:col0 + (n + 1) * 512], csilu[:, k, :],
                                w[k][:, n * 512:(n + 1) * 512], start=(k == 0), stop=(k == KD - 1))
                last.then_inc(s_wmu, 1)

            def mod_cols(l, first, n, at_col, turn):
                pe.wait_ge(s_modrow, turn)
                for m in range(first, first + n):
                    last = nc.tensor.transpose(PS[:, at_col + 2 * m:at_col + 2 * m + 2],
                                               modrow[l][0:2, m * P:(m + 1) * P], ident[0:2, 0:2])
                last.then_inc(s_modtr, 1)

            pe.wait_ge(s_csilu, 1)
            for k in range(KD):
                mod_rows(k, wmA, 0, 2 * D, s_wm[k], 16)
            mod_cols(0, 0, 2 * KD, 3072, 1)
            for k in range(KD):
                mod_rows(k, wmB, 2 * D, D, s_wmb, 16 * KD)

            for l in range(DEPTH):
                jl = l * NJ
                T = TL[l]
                tok = T // P

                def qkv_job(n):
                    job((jl + n) // 2, n % 2, KD, jobs_qkv(l)[n], Uh, Ul,
                        (lambda k: pe.wait_ge(s_ufp, KD * l + k + 1)) if n == 0 else None,
                        (lambda k: pe.wait_ge(s_u, KD * l + k + 1)) if n == 0 else None)

                def to_tokens(f, n):
                    pe.wait_ge(s_fc, 6 * l + n + 1)
                    transposes(l, f, [fc[n % 2][:, t * P:(t + 1) * P] for t in range(jobs_qkv(l)[n] // P)])

                def to_keys(f, g):
                    pe.wait_ge(s_kd, l + 1)
                    transposes(l, f, [kd[:, t, g].rearrange("p a d -> p (a d)") for t in range(NTOK)])

                qkv_job(0)
                if l == 0:
                    pe.wait_ge(s_mod, 1)
                    mod_cols(0, 2 * KD, KD, 3072, 2)
                    pe.wait_ge(s_mod, 2)
                qkv_job(1)
                to_tokens(O_K, 0)
                qkv_job(2)
                to_tokens(O_Q0, 1)
                qkv_job(3)
                to_tokens(O_Q1, 2)
                to_keys(O_KT0, 0)
                qkv_job(4)
                to_keys(O_KT1, 1)
                to_tokens(O_Q2, 3)
                to_tokens(O_Q3, 4)
                qkv_job(5)
                to_tokens(O_V, 5)

                for p in range(2):
                    pe.wait_ge(sfree[p], (jl + J_ZA) // 2)
                pe.wait_ge(t_free, pieces(l, O_V)[-1][0] + 1)
                pe.wait_ge(s_kv, 3 * (l + 1))
                for call, (t0, nt, k0, nk) in enumerate(att_calls(l)):
                    ub, ptb = att_base(l, call)
                    p0, p1 = nk // 2 + 2, nk // 2

                    def q_fill(un, g, par, idx):
                        pe.wait_ge(s_qd, un + (ub + 1))
                        if not isinstance(idx, int) or idx > 0:
                            pe.wait_ge(pt_free[par], idx)
                        for h in range(4):
                            last = nc.tensor.transpose(PS[:, PT0[par] + h * P:PT0[par] + (h + 1) * P],
                                                       qd[g][:, h].rearrange("p a d -> p (a d)"), ident[:])
                        last.then_inc(pt_done[par], 1)

                    def scores(un, g, h, part):
                        first = isinstance(un, int) and ub + un == 0
                        own, tail = score_parts(h, nk)
                        if part == 0 and not own:
                            return
                        if not own:
                            pe.wait_ge(s_exp, 4 * ub if isinstance(un, int) and un == 0 else un * 4 + (4 * ub + h - 3))
                        elif part == 0 and not (first and h < 2):
                            pe.wait_ge(s_exp, un * 4 + (4 * ub + h - 1))
                        if part == 1 and own and not (first and h == 0):
                            pe.wait_ge(s_tail, un * 4 + (4 * ub + h))
                        s0 = score_at(h, nk)
                        for c, n in (own, tail)[part]:
                            for a, x in enumerate((qTh, qTl)):
                                last = mmul(PS[:, s0 + c:s0 + c + n], x[g][:, h * P:(h + 1) * P],
                                            kT[:, g, k0 * P + c:k0 * P + c + n], start=(a == 0), stop=(a == 1))
                        if part == 1:
                            last.then_inc(s_s, 1)

                    def pv(un, g, kt, n):
                        b = pt_buf(g, kt)
                        pe.wait_ge(pt_free[kt % 2], n + 1)
                        if kt == 0 and (not isinstance(un, int) or un + ub > 0):
                            pe.wait_ge(s_o, un + ub)
                        for a, x in enumerate((PTh, PTl)):
                            last = mmul(PS[:, O0:O0 + 512], Vt[:, k0 + kt, g, :], x[b][:],
                                        start=(kt == 0 and a == 0), stop=(kt == nk - 1 and a == 1))
                        if kt == nk - 1:
                            last.then_inc(s_pv, 1)

                    def back(un, i):
                        pe.wait_ge(s_o, un + (ub + 1))
                        pe.wait_ge(pt_free[0], i)
                        for h in range(4):
                            last = mmul(PS[:, PT0[0] + h * HD:PT0[0] + (h + 1) * HD], ob[:, h * P:(h + 1) * P],
                                        stackI[:], start=True, stop=True)
                        last.then_inc(pt_done[0], 1)

                    def unit(un, g, i0, i1, prev, nxt, nxt2):
                        for kt in range(nk):
                            par = kt % 2
                            if kt == 0:
                                pe.wait_ge(s_exp, un * 4 + (4 * ub + 4))
                            pe.wait_ge(pt_free[par], fill(nk, kt, i0, i1, prev, nxt2))
                            for h in range(4):
                                last = nc.tensor.transpose(PS[:, PT0[par] + h * P:PT0[par] + (h + 1) * P],
                                                           Pr[:, g, h, kt * P:(kt + 1) * P], ident[:])
                            last.then_inc(pt_done[par], 1)
                            heads = heads_at(nk, kt, nxt, nxt2)
                            for a, h in heads:
                                scores(un + a, (g + a) % 2, h, 0)
                                if nk == 2:
                                    scores(un + a, (g + a) % 2, h, 1)
                            if nxt2 and nk > 2 and kt == q_at(nk):
                                q_fill(un + 2, g, 0, i0 + (kt + 1) // 2)
                            for k in pv_tiles(kt, prev):
                                if k < 0:
                                    pv(un - 1, 1 - g, nk + k, (i0 - 1 if k % 2 == 0 else i1) - 1)
                                else:
                                    pv(un, g, k, fill(nk, k, i0, i1, prev, nxt2))
                            if prev and kt == back_at(nk):
                                back(un - 1, i0 - 1 + (kt + 1) // 2)
                            if nxt2 and nk == 2 and kt == q_at(nk):
                                q_fill(un + 2, g, 0, i0 + (kt + 1) // 2)
                            if nk > 2:
                                for a, h in heads:
                                    scores(un + a, (g + a) % 2, h, 1)

                    q_fill(0, 0, 0, ptb[0])
                    q_fill(1, 1, 1, ptb[1])
                    pe.wait_ge(pt_free[0], ptb[0] + 1)
                    pe.wait_ge(pt_free[1], ptb[1] + 1)
                    for un, h in [(0, 0), (0, 1), (0, 2), (0, 3)] + ([(1, 0)] if nk > 2 else []):
                        for part in range(2):
                            scores(un, un, h, part)
                    for g in range(NKV):
                        unit(g, g, ptb[0] + 1 + g * p0, ptb[1] + 1 + g * p1, g > 0, True, True)
                    if nt > 2:
                        with pe.Fori(1, nt - 1) as i:
                            for g in range(NKV):
                                unit(i * 2 + g, g, i * (2 * p0) + (ptb[0] + 1 + g * p0),
                                     i * (2 * p1) + (ptb[1] + 1 + g * p1), True, True, True)
                    un = 2 * (nt - 1)
                    unit(un, 0, ptb[0] + 1 + un * p0, ptb[1] + 1 + un * p1, True, True, False)
                    unit(un + 1, 1, ptb[0] + (un + 1) * p0, ptb[1] + 1 + (un + 1) * p1, True, False, False)
                    for kt in range(nk - 2, nk):
                        pv(un + 1, 1, kt, fill(nk, kt, ptb[0] + (un + 1) * p0, ptb[1] + 1 + (un + 1) * p1, True, False))
                    back(un + 1, ptb[0] - 2 + (un + 2) * p0)

                pe.wait_ge(s_oatt, sum(2 * c[1] for ll in range(l + 1) for c in att_calls(ll)))
                for i in range(KW):
                    job((jl + J_ZA + i) // 2, i % 2, KD, T, Uh, Ul)
                    transposes(l, O_OT + i, [qo[:, t, i * P:(i + 1) * P] for t in range(tok)])
                with pe.Fori(0, 4) as i:
                    for c in range(2):
                        job(i + (jl + J_CONF) // 2, c, KD, T, Uh, Ul)

                def merge_jobs(jb, y):
                    with pe.Fori(0, 2) as i:
                        for j in range(4):
                            job(i * 4 + (jb // 2 + j), 0, KD, T, Uh, Ul)
                            pe.wait_ge(s_y, y)
                            job(i * 4 + (jb // 2 + j), 1, KW, T, Yh, Yl)

                merge_jobs(jl + J_MA, 12 * l + 4)
                with pe.Fori(0, 4) as i:
                    for c in range(4):
                        job(i * 2 + ((jl + J_SHORT) // 2 + c // 2), c % 2, KD, T, Uh, Ul)
                merge_jobs(jl + J_MB, 12 * l + 8)
                def zc_job(n):
                    job((jl + J_ZC + n) // 2, n % 2, KD, T, Uh, Ul)

                zc_job(0)
                pe.wait_ge(s_csum, 4 * l + 1)
                stat(l, O_CMEAN, e[4])
                zc_job(1)
                pe.wait_ge(s_csum, 4 * l + 2)
                stat(l, O_CVAR, e[5])
                zc_job(2)
                zc_job(3)
                merge_jobs(jl + J_MC, 12 * l + 12)
                for j in range(KD):
                    job((jl + J_OUT + j) // 2, j % 2, KD, T, Uh, Ul,
                        (lambda k: pe.wait_ge(s_mgh, KD * l + k + 1)) if j == 0 else None,
                        (lambda k: pe.wait_ge(s_mg, KD * l + k + 1)) if j == 0 else None)
                nxt = l + 1 < DEPTH
                if nxt:
                    for p in range(2):
                        pe.wait_ge(sfree[p], (jl + NJ) // 2)
                    mod_rows(0, wmL, 0, 3 * D, s_wm[0], 32)
                pe.wait_ge(s_csum, 4 * l + 3)
                stat(l, O_OMEAN, e[4])
                if nxt:
                    for k in range(1, 5):
                        mod_rows(k, wmL, 0, 3 * D, s_wm[k], 32)
                pe.wait_ge(s_csum, 4 * l + 4)
                stat(l, O_OVAR, e[5])
                if nxt:
                    for k in range(5, KD):
                        mod_rows(k, wmL, 0, 3 * D, s_wm[k], 32)
                    mod_cols(l + 1, 0, 3 * KD, 0, 3)

        @block.scalar
        def _(act):
            fn = nc.scalar.activation

            act.wait_ge(s_c, 64)
            fn(csilu[:], craw[:], ACT.Silu).then_inc(s_csilu, 1)

            def make_u(l, src):
                for j in range(KD):
                    n = (KD * l + j) // 2
                    if j % 2 == 0:
                        if l == 0:
                            act.wait_ge(s_hin[0], 16 * (n + 1))
                        if j >= 2:
                            act.wait_ge(s_u, KD * l + j - 1)
                        for c0, m, who in segs(TALL):
                            last = fn(e[0][:, c0:c0 + m], src(j)[:, c0:c0 + m], ACT.Identity,
                                      scale=mod[:, l, KD + j, who:who + 1], bias=mod[:, l, j, who:who + 1])
                        last.then_inc(s_um[0], 1)
                    act.wait_ge(s_um[j % 2], n + 1)
                    fn(Uh[:, j, :], e[j % 2][:, :TALL], ACT.Copy).then_inc(s_ufp, 1)

            act.wait_ge(s_mod, 1)
            make_u(0, lambda j: e[2 + j % 2])

            for l in range(DEPTH):
                jl = l * NJ
                T = TL[l]

                def evac(n):
                    act.wait_ge(mm[n % 2], (jl + n) // 2 + 1)
                    if n >= 2:
                        act.wait_ge(t_done, pieces(l, QKV_OPS[n - 2])[-1][0] + 1)
                    Tn = jobs_qkv(l)[n]
                    fn(fc[n % 2][:, :Tn], slot(n % 2, Tn), ACT.Copy).then_inc(sfree[n % 2], 1)
                    act.wait_ge(sfree[n % 2], (jl + n) // 2 + 1)
                    act.sem_inc(s_fc, 1)

                def copy_pieces(op, dst, scale=1.0):
                    for f, c, n in pieces(l, op):
                        act.wait_ge(t_done, f + 1)
                        fn(dst[:, c:c + n], tbank(f, n), ACT.Copy, scale=scale).then_inc(t_free, 1)
                    act.wait_ge(t_free, f + 1)

                def copy_raw(op):
                    if 8 * l + op >= 2:
                        act.wait_ge(s_rawfree, 8 * l + op - 1)
                    copy_pieces(op, raw[op % 2])
                    return raw[op % 2]

                def square(op):
                    Tn = op_width(l, op)
                    x = copy_raw(op)
                    if op != O_K:
                        act.wait_ge(s_ms, 5 * l + [O_K, O_Q0, O_Q1, O_Q2, O_Q3].index(op))
                    fn(sq[:, :Tn], x[:, :Tn], ACT.Square).then_inc(s_sq, 1)

                def k_hi(op, g):
                    x = copy_raw(op)
                    fn(kT[:, g, :], x[:], ACT.Copy).then_inc(s_khi, 1)

                evac(0)
                evac(1)
                square(O_K)
                evac(2)
                square(O_Q0)
                evac(3)
                square(O_Q1)
                if l > 0:
                    act.wait_ge(s_hst, 16 * KD)
                k_hi(O_KT0, 0)
                evac(4)
                k_hi(O_KT1, 1)
                square(O_Q2)
                square(O_Q3)
                evac(5)
                x = copy_raw(O_V)
                fn(Vt[:, :, :, 0:HD], x[:].rearrange("p (t g d) -> p t g d", g=NKV, d=HD),
                   ACT.Copy).then_inc(s_vhi, 1)

                act.wait_ge(s_q, 4 * (l + 1))
                act.wait_ge(s_kv, 3 * (l + 1))
                for call, (t0, nt, k0, nk) in enumerate(att_calls(l)):
                    ub, ptb = att_base(l, call)
                    p0, p1 = nk // 2 + 2, nk // 2

                    def q_hi(g, par, idx):
                        act.wait_ge(pt_done[par], idx + 1)
                        fn(qTh[g][:], PS[:, PT0[par]:PT0[par] + 512], ACT.Copy,
                           scale=HD ** -0.5).then_inc(pt_hi[par], 1)

                    def exps(un, g, h):
                        act.wait_ge(s_nm, un * 4 + (4 * ub + h + 1))
                        s0 = score_at(h, nk)
                        main, tail = score_parts(h, nk)
                        m = 4 * g + h
                        (c, n), = tail
                        fn(Pr[:, g, h, c:c + n], PS[:, s0 + c:s0 + c + n], ACT.Exp, bias=nm[:, m:m + 1],
                           accum_out=rs[:, g, 0, h:h + 1]).then_inc(s_tail, 1)
                        if main:
                            c = main[0][0]
                            fn(Pr[:, g, h, c:c + 1024], PS[:, s0 + c:s0 + c + 1024], ACT.Exp, bias=nm[:, m:m + 1],
                               accum_out=rs[:, g, 1, h:h + 1]).then_inc(s_exp, 1)
                        else:
                            act.wait_ge(s_tail, un * 4 + (4 * ub + h + 1))
                            act.sem_inc(s_exp, 1)

                    def o_copy(un):
                        act.wait_ge(s_pv, un + (ub + 1))
                        fn(ob[:], PS[:, O0:O0 + 512], ACT.Copy).then_inc(s_o, 1)

                    def unit(un, g, i0, i1, prev, nxt, nxt2):
                        for kt in range(nk):
                            par = kt % 2
                            act.wait_ge(pt_done[par], fill(nk, kt, i0, i1, prev, nxt2) + 1)
                            fn(PTh[pt_buf(g, kt)][:], PS[:, PT0[par]:PT0[par] + 512], ACT.Copy).then_inc(pt_hi[par], 1)
                            if prev and nk == 2 and kt == 1:
                                o_copy(un - 1)
                            if nxt2 and kt == q_at(nk):
                                q_hi(g, 0, i0 + (kt + 1) // 2)
                            for h in exps_at(nk, kt, nxt):
                                exps(un + 1, 1 - g, h)
                            if prev and nk > 2 and kt == 1:
                                o_copy(un - 1)

                    q_hi(0, 0, ptb[0])
                    q_hi(1, 1, ptb[1])
                    for h in range(4):
                        exps(0, 0, h)
                    for g in range(NKV):
                        unit(g, g, ptb[0] + 1 + g * p0, ptb[1] + 1 + g * p1, g > 0, True, True)
                    if nt > 2:
                        with act.Fori(1, nt - 1) as i:
                            for g in range(NKV):
                                unit(i * 2 + g, g, i * (2 * p0) + (ptb[0] + 1 + g * p0),
                                     i * (2 * p1) + (ptb[1] + 1 + g * p1), True, True, True)
                    un = 2 * (nt - 1)
                    unit(un, 0, ptb[0] + 1 + un * p0, ptb[1] + 1 + un * p1, True, True, False)
                    unit(un + 1, 1, ptb[0] + (un + 1) * p0, ptb[1] + 1 + (un + 1) * p1, True, False, False)
                    o_copy(un + 1)

                act.wait_ge(s_oatt, sum(2 * c[1] for ll in range(l + 1) for c in att_calls(ll)))
                for i in range(KW):
                    act.wait_ge(mm[i % 2], (jl + J_ZA + i) // 2 + 1)
                    if i >= 2:
                        act.wait_ge(s_yf, 12 * l + i - 1)
                    fn(e[i % 2][:, :T], slot(i % 2, T), ACT.Silu).then_inc(sfree[i % 2], 1)
                    if i >= 2:
                        act.wait_ge(s_yf, 12 * l + i - 1)
                    copy_pieces(O_OT + i, e[4 + i % 2])
                    act.sem_inc(s_oraw, 1)
                    act.wait_ge(s_yf, 12 * l + i + 1)
                    fn(Yh[:, i, :T], e[2 + i % 2][:, :T], ACT.Copy).then_inc(s_yh, 1)

                with act.Fori(0, 4) as i:
                    act.wait_ge(mm[0], i + ((jl + J_CONF) // 2 + 1))
                    act.wait_ge(sfree[1], i + (jl + J_CONF) // 2)
                    fn(e[0][:, :T], slot(0, T), ACT.Sigmoid).then_inc(sfree[0], 1)

                def merge(branch):
                    jb = jl + (J_MA, J_MB, J_MC)[branch]
                    yb = (3 * l + branch) * KD
                    ab = 2 * l * KD
                    with act.Fori(0, 2) as i:
                        for j in range(4):
                            act.wait_ge(sfree[1], i * 4 + (jb // 2 + j))
                            if branch > 0:
                                act.wait_ge(s_mgd, i * 4 + (yb + j))
                                act.dma_start(e[1][:, :T], accd[branch - 1, i * 4 + j][:, :T]).then_inc(s_accin, 16)
                            act.wait_ge(mm[0], i * 4 + (jb // 2 + j + 1))
                            fn(e[0][:, :T], slot(0, T), ACT.Sigmoid).then_inc(sfree[0], 1)
                            if branch < 2:
                                act.wait_ge(s_mgd, i * 4 + (yb + j + 1))
                                act.dma_start(accd[branch, i * 4 + j][:, :T], e[4 + j % 2][:, :T]).then_inc(s_accst, 16)
                                act.wait_ge(s_accst, i * 64 + 16 * (ab + branch * KD + j + 1))

                merge(0)

                with act.Fori(0, 4) as i:
                    hb = (jl + J_SHORT) // 2
                    act.wait_ge(mm[0], i * 2 + (hb + 1))
                    act.wait_ge(sfree[1], i * 2 + hb)
                    fn(e[0][:, :T], slot(0, T), ACT.Copy).then_inc(sfree[0], 1)
                    act.wait_ge(mm[0], i * 2 + (hb + 2))
                    act.wait_ge(sfree[1], i * 2 + (hb + 1))
                    act.wait_ge(s_yf, i + (12 * l + 4))
                    fn(e[4][:, :T], slot(0, T), ACT.Silu).then_inc(sfree[0], 1)
                    act.wait_ge(s_yf, i + (12 * l + 5))
                    act.sem_inc(s_carry, 1)
                    fn(Yh[:, i, :T], e[3][:, :T], ACT.Copy).then_inc(s_yh, 1)

                merge(1)

                def silu_z(n):
                    act.wait_ge(mm[n % 2], (jl + J_ZC + n) // 2 + 1)
                    fn(hc[:, n, :T], slot(n % 2, T), ACT.Silu).then_inc(sfree[n % 2], 1)

                def squares(first, srcs):
                    for n, s in enumerate(srcs):
                        act.wait_ge(s_dev, first + n + 1)
                        if n >= 2:
                            act.wait_ge(s_lacc, first + n - 1)
                        fn(e[n % 2][:, :T], s, ACT.Square).then_inc(s_lsq, 1)

                def mean(op, nt):
                    copy_pieces(op, e[4], float(KD) / nt)
                    act.sem_inc(s_mean, 1)

                def root(op, nt):
                    for f, c, n in pieces(l, op):
                        act.wait_ge(t_done, f + 1)
                        fn(e[4][:, c:c + n], tbank(f, n), ACT.Sqrt, scale=float(KD) / nt,
                           bias=eps[:]).then_inc(t_free, 1)
                    act.wait_ge(t_free, f + 1)
                    act.sem_inc(s_std, 1)

                act.wait_ge(s_csum, 4 * l + 1)
                silu_z(0)
                mean(O_CMEAN, KW)
                squares(12 * l, [cv[:, n, :T] for n in range(KW)])
                silu_z(1)
                root(O_CVAR, KW)
                silu_z(2)
                silu_z(3)
                for n in range(KW):
                    act.wait_ge(s_norm, 12 * l + n + 1)
                    if n >= 2:
                        act.wait_ge(s_yf, 12 * l + 8 + n - 1)
                    fn(e[n % 2][:, :T], cv[:, n, :T], ACT.Silu, scale=vec[:, l, V_CG + n:V_CG + n + 1],
                       bias=vec[:, l, V_CB + n:V_CB + n + 1]).then_inc(s_hact, 1)
                    act.wait_ge(s_yf, 12 * l + 8 + n + 1)
                    fn(Yh[:, n, :T], e[2 + n % 2][:, :T], ACT.Copy).then_inc(s_yh, 1)

                merge(2)

                act.wait_ge(mm[0], (jl + J_OUT) // 2)
                for j in range(KD):
                    act.wait_ge(s_mgf, KD * l + j + 1)
                    fn(Uh[:, j, :T], X[:, j, :T], ACT.Copy).then_inc(s_mgh, 1)

                act.wait_ge(s_mod, 2 + l)
                for j in range(KD):
                    act.wait_ge(mm[j % 2], (jl + J_OUT + j) // 2 + 1)
                    if j >= 2:
                        act.wait_ge(s_z, KD * l + j - 1)
                    for c0, n, who in segs(T):
                        last = fn(e[j % 2][:, c0:c0 + n], PS[:, SLOT[j % 2] + c0:SLOT[j % 2] + c0 + n], ACT.Copy,
                                  scale=mod[:, l, 2 * KD + j, who:who + 1])
                    last.then_inc(sfree[j % 2], 1)
                mean(O_OMEAN, KD)
                squares(12 * l + 4, [Z[:, n, :T] for n in range(KD)])
                root(O_OVAR, KD)
                for j in range(KD):
                    act.wait_ge(s_norm, 12 * l + 4 + j + 1)
                    if l + 1 < DEPTH and j == 0:
                        act.wait_ge(s_wmu, 2 * KD + 3)
                    fn(X[:, j, :T], Z[:, j, :T], ACT.Identity, scale=vec[:, l, V_PG + j:V_PG + j + 1],
                       bias=vec[:, l, V_PB + j:V_PB + j + 1]).then_inc(s_hn, 1)
                if l + 1 < DEPTH:
                    act.wait_ge(s_hn, KD * (l + 1))
                    act.wait_ge(s_mod, 3)
                    make_u(l + 1, lambda j: X[:, j, :])

        @block.vector
        def _(dve):
            st = Steps(dve, c_dve)
            tt, stt, ts = nc.vector.tensor_tensor, nc.vector.scalar_tensor_tensor, nc.vector.tensor_scalar

            def mod_row(l, c0, n, turn):
                dve.wait_ge(s_wmu, KD * turn)
                nc.vector.tensor_copy(modrow[l][:, c0:c0 + n], PS[0:2, c0:c0 + n]).then_inc(s_modrow, 1)

            def mod_col(l, first, n, at_col, turn):
                dve.wait_ge(s_modtr, turn)
                cols = PS[:, at_col + 2 * first:at_col + 2 * (first + n)].rearrange("p (n w) -> p n w", w=2)
                last = tt(mod[:, l, first:first + n], cols,
                          vec[:, l, V_BM + first:V_BM + first + n].rearrange("p (n w) -> p n w", w=1)
                          .broadcast_to([P, n, 2]), ALU.add)
                if first == 0:
                    st.done(last)
                    last = ts(mod[:, l, KD:2 * KD], mod[:, l, KD:2 * KD], 1.0, None, ALU.add)
                last.then_inc(s_mod, 1)

            mod_row(0, 0, 2 * D, 1)
            mod_col(0, 0, 2 * KD, 3072, 1)

            def make_u(l, src, landed):
                dve.wait_ge(s_mod, 1 + 2 * l)
                for j in range(KD):
                    if j % 2 == 0:
                        landed(j + 1)
                        if j >= 2:
                            dve.wait_ge(s_u, KD * l + j)
                        for c0, m, who in segs(TALL):
                            last = ts(e[1][:, c0:c0 + m], src(j + 1)[:, c0:c0 + m],
                                      mod[:, l, KD + j + 1, who:who + 1], mod[:, l, j + 1, who:who + 1],
                                      ALU.mult, ALU.add)
                        last.then_inc(s_um[1], 1)
                    dve.wait_ge(s_ufp, KD * l + j + 1)
                    tt(Ul[:, j, :], e[j % 2][:, :TALL], Uh[:, j, :].bitcast(F32), ALU.subtract).then_inc(s_u, 1)

            make_u(0, lambda j: e[2 + j % 2], lambda j: dve.wait_ge(s_hin[1], 16 * (j // 2 + 1)))
            mod_row(0, 2 * D, D, 2)
            mod_col(0, 2 * KD, KD, 3072, 2)

            for l in range(DEPTH):
                jl = l * NJ
                T = TL[l]

                def mean_square(n, Tn):
                    H2 = 2 * Tn // P
                    dve.wait_ge(s_sq, 5 * l + n + 1)
                    st.done(nc.vector.reduce_sum(ss[:, :H2], sq[:, :Tn].rearrange("p (h d) -> p h d", d=HD), AX_X))
                    ts(ms[:, n % 2, :H2], ss[:, :H2], 1.0 / HD, RMS_EPS, ALU.mult, ALU.add).then_inc(s_ms, 1)

                def normed(op, n, Tn, A, B, dst):
                    H2 = 2 * Tn // P
                    dve.wait_ge(s_rstd, 5 * l + n + 1)
                    tt(qn[:, :Tn].rearrange("p (h d) -> p h d", d=HD),
                       raw[op % 2][:, :Tn].rearrange("p (h d) -> p h d", d=HD),
                       rstd[:, n % 2, :H2].rearrange("p (h o) -> p h o", o=1).broadcast_to([P, H2, HD]),
                       ALU.mult).then_inc(s_rawfree, 1)
                    dve.wait_ge(s_rawfree, 8 * l + op + 1)
                    if n < 2:
                        dve.wait_ge(s_tab, 4 * l + 2 + 2 * n)
                    tt(qa[:, :Tn], qn[:, :Tn], A[:, :Tn], ALU.mult)

                    def pair(x, a):
                        return x[:, :Tn].rearrange("p (b a c) -> p b a c", a=2, c=HD // 4)[:, :, a, :]

                    tt(pair(qb, 0), pair(qn, 1), pair(B, 0), ALU.mult)
                    st.done(tt(pair(qb, 1), pair(qn, 0), pair(B, 1), ALU.mult))
                    return dst(Tn)

                def k_out(Tn):
                    for a in range(2):
                        last = tt(kd[:, :, :, a, :].rearrange("p t g d -> p (t g) d"),
                                  qa[:].rearrange("p (h d) -> p h d", d=HD),
                                  qb[:].rearrange("p (h d) -> p h d", d=HD), ALU.add)
                    last.then_inc(s_kd, 1)

                def q_out(i):
                    def f(Tn):
                        tt(qo[:, :Tn // P, i * P:(i + 1) * P], qa[:, :Tn].rearrange("p (t c) -> p t c", c=P),
                           qb[:, :Tn].rearrange("p (t c) -> p t c", c=P), ALU.add).then_inc(s_q, 1)
                    return f

                def k_lo(op, g):
                    dve.wait_ge(s_khi, 2 * l + g + 1)
                    st.done(tt(kT[HD:P, g, :], raw[op % 2][HD:P, :], kT[HD:P, g, :].bitcast(F32), ALU.subtract))
                    dve.sem_inc(s_rawfree, 1)
                    dve.sem_inc(s_kv, 1)

                mean_square(0, TALL)
                normed(O_K, 0, TALL, e[0], e[1], k_out)
                mean_square(1, T)
                normed(O_Q0, 1, T, e[4], e[5], q_out(0))
                mean_square(2, T)
                normed(O_Q1, 2, T, e[4], e[5], q_out(1))
                k_lo(O_KT0, 0)
                k_lo(O_KT1, 1)
                mean_square(3, T)
                mean_square(4, T)
                normed(O_Q2, 3, T, e[4], e[5], q_out(2))
                normed(O_Q3, 4, T, e[4], e[5], q_out(3))
                dve.wait_ge(s_vhi, l + 1)
                st.done(tt(Vt[:, :, :, HD:P].rearrange("p t g d -> p (t g) d"),
                           raw[O_V % 2][:].rearrange("p (h d) -> p h d", d=HD),
                           Vt[:, :, :, 0:HD].rearrange("p t g d -> p (t g) d").bitcast(F32), ALU.subtract))
                dve.sem_inc(s_rawfree, 1)
                dve.sem_inc(s_kv, 1)

                for call, (t0, nt, k0, nk) in enumerate(att_calls(l)):
                    ub, ptb = att_base(l, call)
                    p0, p1, hi0 = nk // 2 + 2, nk // 2, nk // 2 + 1
                    hb = [ptb[0] - ub, ptb[1]]

                    def q_lo(g, par, idx_hi):
                        dve.wait_ge(pt_hi[par], idx_hi + 1)
                        stt(qTl[g][:], PS[:, PT0[par]:PT0[par] + 512], HD ** -0.5, qTh[g][:].bitcast(F32),
                            ALU.mult, ALU.subtract).then_inc(pt_free[par], 1)

                    def maxes(un, g, h):
                        dve.wait_ge(s_s, un * 4 + (4 * ub + h + 1))
                        s0 = score_at(h, nk)
                        m = 4 * g + h
                        nc.vector.reduce_max(nm[:, m:m + 1], PS[:, s0:s0 + nk * P], AX_X,
                                             negate=True).then_inc(s_nm, 1)

                    def sums(un, g):
                        dve.wait_ge(s_exp, un * 4 + (4 * ub + 4))
                        if nk * P > 256:
                            st.done(tt(rsum[:], rs[:, g, 0, :], rs[:, g, 1, :], ALU.add))
                            st.done(nc.vector.reciprocal(ri[:, g], rsum[:]))
                        else:
                            st.done(nc.vector.reciprocal(ri[:, g], rs[:, g, 0, :]))

                    def back(t, g, i):
                        dve.wait_ge(pt_done[0], i)
                        st.done(tt(qo[:, t, g * 4 * HD:(g + 1) * 4 * HD].rearrange("p (h d) -> p h d", d=HD),
                                   PS[:, PT0[0]:PT0[0] + 4 * HD].rearrange("p (h d) -> p h d", d=HD),
                                   ri[:, g].rearrange("p (h o) -> p h o", o=1).broadcast_to([P, 4, HD]), ALU.mult))
                        dve.sem_inc(pt_free[0], 1)
                        dve.sem_inc(s_oatt, 1)

                    def unit(un, t, g, h0, h1, prev, nxt, nxt2):
                        for kt in range(nk):
                            par = kt % 2
                            dve.wait_ge(pt_hi[par], fill(nk, kt, h0, h1, False, nxt2) + 1)
                            b = pt_buf(g, kt)
                            tt(PTl[b][:], PS[:, PT0[par]:PT0[par] + 512], PTh[b][:].bitcast(F32),
                               ALU.subtract).then_inc(pt_free[par], 1)
                            if prev and kt == back_at(nk):
                                back(t if g == 1 else t - 1, 1 - g, h0 + un + ub + (kt + 1) // 2)
                            if nxt2 and kt == q_at(nk):
                                q_lo(g, 0, h0 + (kt + 1) // 2)
                            for a, h in heads_at(nk, kt, nxt, nxt2):
                                maxes(un + a, (g + a) % 2, h)
                            if nxt and kt == nk - 1:
                                sums(un + 1, 1 - g)

                    q_lo(0, 0, hb[0])
                    q_lo(1, 1, hb[1])
                    for un, h in [(0, 0), (0, 1), (0, 2), (0, 3)] + ([(1, 0)] if nk > 2 else []):
                        maxes(un, un, h)
                    sums(0, 0)
                    for g in range(NKV):
                        unit(g, t0, g, hb[0] + 1 + g * hi0, hb[1] + 1 + g * p1, g > 0, True, True)
                    if nt > 2:
                        with st.loop(1, nt - 1, 6) as i:
                            for g in range(NKV):
                                unit(i * 2 + g, i + t0, g, i * (2 * hi0) + (hb[0] + 1 + g * hi0),
                                     i * (2 * p1) + (hb[1] + 1 + g * p1), True, True, True)
                    un = 2 * (nt - 1)
                    unit(un, t0 + nt - 1, 0, hb[0] + 1 + un * hi0, hb[1] + 1 + un * p1, True, True, False)
                    unit(un + 1, t0 + nt - 1, 1, hb[0] + (un + 1) * hi0, hb[1] + 1 + (un + 1) * p1,
                         True, False, False)
                    back(t0 + nt - 1, 1, ptb[0] - 1 + (un + 2) * p0)

                for i in range(KW):
                    dve.wait_ge(sfree[i % 2], (jl + J_ZA + i) // 2 + 1)
                    dve.wait_ge(s_oraw, KW * l + i + 1)
                    tt(e[2 + i % 2][:, :T], e[4 + i % 2][:, :T], e[i % 2][:, :T], ALU.mult).then_inc(s_yf, 1)
                    dve.wait_ge(s_yh, 12 * l + i + 1)
                    tt(Yl[:, i, :T], e[2 + i % 2][:, :T], Yh[:, i, :T].bitcast(F32), ALU.subtract).then_inc(s_y, 1)

                dve.wait_ge(s_pad, sum(len(segs(t)) + 1 for t in TL[:l + 1]))
                hb = (jl + J_CONF) // 2
                wmid = V_WC + CPAD
                with st.loop(0, 4, 2) as i:
                    dve.wait_ge(mm[1], i + (hb + 1))
                    dve.wait_ge(sfree[0], i + (hb + 1))
                    for c0, n, who in segs(T):
                        last = tt(hc[:, i, CPAD * (1 + who) + c0:CPAD * (1 + who) + c0 + n],
                                  PS[:, SLOT[1] + c0:SLOT[1] + c0 + n], e[0][:, c0:c0 + n], ALU.mult)
                    st.done(last)
                    dve.sem_inc(sfree[1], 1)
                    for c0, n, who in segs(T):
                        last = ts(cv[:, i, c0:c0 + n], hc[:, i, CPAD * (1 + who) + c0:CPAD * (1 + who) + c0 + n],
                           vec[:, l, bass.ds(i * CONF_K + wmid, 1)], vec[:, l, bass.ds(i + V_BDW, 1)],
                           ALU.mult, ALU.add)
                    st.done(last)

                def conv_taps(i, c_base, taps):
                    for tap in taps:
                        for c0, n, who in segs(T):
                            last = stt(cv[:, i + c_base, c0:c0 + n],
                                       hc[:, i + c_base, CPAD * who + c0 + tap:CPAD * who + c0 + tap + n],
                                       vec[:, l, bass.ds(i * CONF_K + (V_WC + c_base * CONF_K + tap), 1)],
                                       cv[:, i + c_base, c0:c0 + n], ALU.mult, ALU.add)
                        st.done(last)

                TAPS = [t for t in range(CONF_K) if t != CPAD]
                PART = [TAPS[0:8], TAPS[8:15], TAPS[15:23], TAPS[23:30]]

                def merge(branch):
                    jb = (jl + (J_MA, J_MB, J_MC)[branch]) // 2
                    conv = branch < 2
                    with st.loop(0, 2, (30 if conv else 0) + (4 if branch > 0 else 0)) as i:
                        for j in range(4):
                            if conv:
                                conv_taps(i, 2 * branch, PART[j])
                            dve.wait_ge(mm[1], i * 4 + (jb + j + 1))
                            dve.wait_ge(sfree[0], i * 4 + (jb + j + 1))
                            a = e[4 + j % 2][:, :T]
                            if branch == 0:
                                tt(a, slot(1, T), e[0][:, :T], ALU.mult).then_inc(sfree[1], 1)
                                dve.wait_ge(sfree[1], i * 4 + (jb + j + 1))
                                dve.sem_inc(s_mgd, 1)
                                continue
                            if branch == 1:
                                tt(a, slot(1, T), e[0][:, :T], ALU.mult).then_inc(sfree[1], 1)
                            else:
                                stt(a, slot(1, T), vec[:, l, bass.ds(i * 4 + (V_BPC + j), 1)], e[0][:, :T],
                                    ALU.add, ALU.mult).then_inc(sfree[1], 1)
                            dve.wait_ge(sfree[1], i * 4 + (jb + j + 1))
                            nin = (2 * l + branch - 1) * KD + j
                            dve.wait_ge(s_accin, i * 64 + 16 * (nin + 1))
                            dst = a if branch == 1 else X[:, i * 4 + j, :T]
                            st.done(tt(dst, a, e[1][:, :T], ALU.add))
                            dve.sem_inc(s_mgd, 1)
                            if branch == 2:
                                dve.sem_inc(s_mgf, 1)

                merge(0)
                dve.wait_ge(s_accst, 16 * (2 * l + 1) * KD)

                dve.wait_ge(mm[1], (jl + J_SHORT) // 2)
                st.done(nc.vector.memset(e[1][:], 0.0))
                hb = (jl + J_SHORT) // 2
                with st.loop(0, 4, 5) as i:
                    dve.wait_ge(mm[1], i * 2 + (hb + 1))
                    dve.wait_ge(sfree[0], i * 2 + (hb + 1))
                    for c0, n, who in segs(T):
                        last = tt(e[1][:, SPAD * (1 + who) + c0:SPAD * (1 + who) + c0 + n],
                                  PS[:, SLOT[1] + c0:SLOT[1] + c0 + n], e[0][:, c0:c0 + n], ALU.mult)
                    st.done(last)
                    dve.sem_inc(sfree[1], 1)
                    for tap in range(SHORT_K):
                        wt = vec[:, l, bass.ds(i * SHORT_K + (V_WS + tap), 1)]
                        for c0, n, who in segs(T):
                            x = e[1][:, SPAD * who + c0 + tap:SPAD * who + c0 + tap + n]
                            if tap == 0:
                                last = ts(e[2][:, c0:c0 + n], x, wt, None, ALU.mult)
                            else:
                                last = stt(e[2][:, c0:c0 + n], x, wt, e[2][:, c0:c0 + n], ALU.mult, ALU.add)
                        st.done(last)
                    dve.wait_ge(mm[1], i * 2 + (hb + 2))
                    st.done(tt(e[2][:, :T], slot(1, T), e[2][:, :T], ALU.mult))
                    dve.wait_ge(sfree[0], i * 2 + (hb + 2))
                    tt(e[3][:, :T], e[2][:, :T], e[4][:, :T], ALU.mult).then_inc(s_yf, 1)
                    dve.sem_inc(sfree[1], 1)
                    dve.wait_ge(s_yh, i + (12 * l + 5))
                    tt(Yl[:, i, :T], e[3][:, :T], Yh[:, i, :T].bitcast(F32), ALU.subtract).then_inc(s_y, 1)

                merge(1)
                dve.wait_ge(s_accst, 16 * (2 * l + 2) * KD)

                def norm(k, z, nt, first):
                    dve.wait_ge(s_mean, k + 1)
                    for j in range(nt):
                        tt(z(j), z(j), e[4][:, :T], ALU.subtract).then_inc(s_dev, 1)
                        if j >= 1:
                            add_square(j - 1, first)
                    add_square(nt - 1, first)
                    dve.wait_ge(s_lacc, first + nt)
                    dve.sem_inc(s_csum, 1)
                    dve.wait_ge(s_std, k + 1)
                    st.done(nc.vector.reciprocal(e[4][:, :T], e[4][:, :T]))

                def add_square(j, first):
                    dve.wait_ge(s_lsq, first + j + 1)
                    if j == 0:
                        nc.vector.tensor_copy(e[5][:, :T], e[0][:, :T]).then_inc(s_lacc, 1)
                    else:
                        dve.wait_ge(s_lacc, first + j)
                        tt(e[5][:, :T], e[5][:, :T], e[j % 2][:, :T], ALU.add).then_inc(s_lacc, 1)

                st.done(tt(e[4][:, :T], cv[:, 0, :T], cv[:, 1, :T], ALU.add))
                st.done(tt(e[4][:, :T], e[4][:, :T], cv[:, 2, :T], ALU.add))
                st.done(tt(e[4][:, :T], e[4][:, :T], cv[:, 3, :T], ALU.add))
                dve.sem_inc(s_csum, 1)
                norm(2 * l, lambda j: cv[:, j, :T], KW, 12 * l)
                for n in range(KW):
                    tt(cv[:, n, :T], cv[:, n, :T], e[4][:, :T], ALU.mult).then_inc(s_norm, 1)
                dve.wait_ge(mm[1], (jl + J_ZC) // 2)
                for n in range(KW):
                    dve.wait_ge(s_hact, 4 * l + n + 1)
                    dve.wait_ge(sfree[n % 2], (jl + J_ZC + n) // 2 + 1)
                    tt(e[2 + n % 2][:, :T], e[n % 2][:, :T], hc[:, n, :T], ALU.mult).then_inc(s_yf, 1)
                    dve.wait_ge(s_yh, 12 * l + 8 + n + 1)
                    tt(Yl[:, n, :T], e[2 + n % 2][:, :T], Yh[:, n, :T].bitcast(F32), ALU.subtract).then_inc(s_y, 1)

                merge(2)

                for j in range(KD):
                    dve.wait_ge(s_mgh, KD * l + j + 1)
                    tt(Ul[:, j, :T], X[:, j, :T], Uh[:, j, :T].bitcast(F32), ALU.subtract).then_inc(s_mg, 1)

                for j in range(KD):
                    dve.wait_ge(sfree[j % 2], (jl + J_OUT + j) // 2 + 1)
                    nh_in = (KD // 2) * (l + 1) + j // 2 + 1
                    dve.wait_ge(s_hin[j % 2], 16 * nh_in)
                    stt(Z[:, j, :T], e[2 + j % 2][:, :T], ALPHA, e[j % 2][:, :T], ALU.mult,
                        ALU.add).then_inc(s_z, 1)
                    dve.wait_ge(s_z, KD * l + j + 1)
                    if j == 1:
                        st.done(tt(e[4][:, :T], Z[:, 0, :T], Z[:, 1, :T], ALU.add))
                    elif j > 1:
                        st.done(tt(e[4][:, :T], e[4][:, :T], Z[:, j, :T], ALU.add))
                dve.sem_inc(s_csum, 1)
                norm(2 * l + 1, lambda j: Z[:, j, :T], KD, 12 * l + 4)
                for j in range(KD):
                    if l + 1 < DEPTH and j == KD // 2:
                        mod_row(l + 1, 0, 3 * D, 3)
                    tt(Z[:, j, :T], Z[:, j, :T], e[4][:, :T], ALU.mult).then_inc(s_norm, 1)
                if l + 1 < DEPTH:
                    mod_col(l + 1, 0, 3 * KD, 0, 3)
                    make_u(l + 1, lambda j: X[:, j, :], lambda j: dve.wait_ge(s_hn, KD * l + j + 1))


def _tiles(w):
    K, N = w.shape
    return np.ascontiguousarray(w.reshape(K // P, P, N // P, P).transpose(2, 1, 0, 3)).reshape(N // P, P, K)


def _cols(v):
    return v.reshape(-1, P).T


def _rope():
    q = HD // 4
    freqs = (10000.0 ** (-np.arange(q, dtype=np.float32) / q)).astype(np.float32)
    n = np.arange(LAT)
    ar = (n // GRID_W).astype(np.float32)[:, None] * freqs
    ac = (n % GRID_W).astype(np.float32)[:, None] * freqs
    c = np.concatenate([np.cos(ar), np.cos(ar), np.cos(ac), np.cos(ac)], 1)
    s = np.concatenate([-np.sin(ar), np.sin(ar), -np.sin(ac), np.sin(ac)], 1)
    c = np.concatenate([c, np.ones((CTX, HD))], 0)
    s = np.concatenate([s, np.zeros((CTX, HD))], 0)
    both = np.stack([np.concatenate([x, x], 1) for x in (c, s)]).astype(np.float32)
    return np.ascontiguousarray(both.reshape(2, NTOK, P, P).transpose(0, 2, 1, 3)).reshape(2, P, TALL)


def kernel(**inputs):
    import concourse.bacc as _bacc
    from concourse.bass_utils import run_bass_kernel_spmd as _run

    a = {k: np.asarray(v) for k, v in inputs.items()}
    w8, w4, vecs, gains = [], [], [], []
    for l in range(DEPTH):
        w8.append(np.concatenate([_tiles(a["w_in"][l])[W_ORDER], _tiles(a["w_out"][l])]))
        w4.append(np.concatenate([_tiles(a[n][l]) for n in ("w_proj_attn", "w_proj_short", "w_proj_conf")]))
        vecs.append(np.concatenate(
            [_cols(a["post_ln_g"][l]), _cols(a["post_ln_b"][l]), _cols(a["b_proj_conf"][l]),
             _cols(a["conf_ln_g"][l]), _cols(a["conf_ln_b"][l]), _cols(a["b_conf_dw"][l]),
             a["w_short_conv"][l].reshape(SHORT_K, KW, P).transpose(2, 1, 0).reshape(P, -1),
             a["w_conf_dw"][l].reshape(CONF_K, KW, P).transpose(2, 1, 0).reshape(P, -1),
             _cols(a["b_mod"][l])], 1))
        rows = []
        for g in (a["k_gain"][l], a["q_gain"][l]):
            sw = g.reshape(2, 2, HD // 4)[:, ::-1].reshape(HD)
            rows += [np.concatenate([g, g]), np.concatenate([sw, sw])]
        gains.append(np.broadcast_to(np.stack(rows)[None], (P, 4, P)))
    hT = np.concatenate([a["x"][0], a["ctx"][0]]).T.reshape(KD, P, TALL)
    eye = np.eye(P, dtype=np.float32)
    feed = {
        "hT_in": hT,
        "cvec": np.stack([_cols(a["c"][0]), _cols(a["c_ctx"])], 2),
        "wmod": a["w_mod"].reshape(DEPTH, KD, P, 3 * D),
        "w8": np.stack(w8), "w4": np.stack(w4),
        "vecs": np.stack(vecs, 1), "gains": np.stack(gains),
        "rope": _rope(), "ident_in": eye, "stack_in": np.concatenate([eye[:HD, :HD]] * 2),
    }
    nc = _bacc.Bacc("TRN2", target_bir_lowering=False, num_devices=1, dynamic_dma_scratch_size=1024)
    arrays, args = {}, []
    for name, v in feed.items():
        v = np.ascontiguousarray(v)
        arrays[name] = v
        args.append(nc.dram_tensor(name, v.shape, F32, kind="ExternalInput").ap())
    args.append(nc.dram_tensor("outT", (KD, P, LAT), F32, kind="ExternalOutput").ap())
    build(nc, *args)
    r = _run(nc, [arrays], core_ids=[0])
    return np.ascontiguousarray(r.results[0]["outT"].reshape(D, LAT).T).reshape(1, LAT, D)
```
